# Optimizing a Trainium2 kernel written in Bass

```python
import jax, jax.numpy as jnp
from jax import lax
import numpy as np

D_MODEL = 1024
BATCH = 1
SEQ = 256
DEPTH = 2

CHUNK = 64
QBLK = 128
EPS = 1e-6

A_HEADS = 8
A_HEAD_DIM = 64
A_WIDTH = A_HEADS * A_HEAD_DIM
A_DECAY_LORA = 64
A_AAA_LORA = 64
A_GATE_LORA = 128
A_GN_EPS = 64e-5
A_DECAY_SCALE = 0.6065306597126334
A_SHIFT_COLS = 3 * A_WIDTH + A_DECAY_LORA + A_AAA_LORA + A_GATE_LORA
A_SPLIT_POINTS = (A_WIDTH, 2 * A_WIDTH, 3 * A_WIDTH, 3 * A_WIDTH + A_DECAY_LORA,
                  3 * A_WIDTH + A_DECAY_LORA + A_AAA_LORA)

B_HEADS = 8
B_HEAD_DIM = 64
B_WIDTH = B_HEADS * B_HEAD_DIM

C_HEADS = 4
C_QK_DIM = 64
C_V_DIM = 2 * C_QK_DIM
C_QK_COLS = C_HEADS * 2 * C_QK_DIM
C_WIDTH = C_HEADS * C_V_DIM
ROPE_THETA = 500000.0
C_ROT_DIMS = C_QK_DIM // 4

N_BRANCHES = 3
D_FF = 2816
CONV_WIDTH = 3

GROUP_POINTS = (A_SHIFT_COLS,
                A_SHIFT_COLS + 3 * B_WIDTH,
                A_SHIFT_COLS + 3 * B_WIDTH + 2 * C_QK_COLS + C_WIDTH)
IN_COLS = GROUP_POINTS[2] + N_BRANCHES * D_MODEL

kernel_name = "hybrid_rwkv7_stickbreak_diffattn_convffn"

def rms_norm(x, g):
    xf = x.astype(jnp.float32)
    y = xf * lax.rsqrt(jnp.mean(xf * xf, axis=-1, keepdims=True) + EPS)
    return (y * g.astype(jnp.float32)).astype(x.dtype)

def causal_shift(z, n):
    return jnp.pad(z, ((0, 0), (n, 0), (0, 0)))[:, :z.shape[1]]

def sweep_query_blocks(block_fn, q_list, kv_list):
    t_len = q_list[0].shape[2]
    outs = []
    for lo in range(0, t_len, QBLK):
        hi = lo + QBLK
        outs.append(block_fn(lo, *[q[:, :, lo:hi] for q in q_list],
                             *[z[:, :, :hi] for z in kv_list]))
    return jnp.concatenate(outs, axis=2)

def partial_rope(x, cos, sin):
    half = C_ROT_DIMS // 2
    x1, x2, xp = x[..., :half], x[..., half:C_ROT_DIMS], x[..., C_ROT_DIMS:]
    return jnp.concatenate([x1 * cos - x2 * sin, x1 * sin + x2 * cos, xp], axis=-1)

def rwkv7_time_mix(pa, mu, w0, w_up, a0, a_up, g_up, k_k, k_a, r_k, ln_w, ln_b):
    f32 = jnp.float32
    bsz, t_len, _ = pa.shape
    pa = pa + (causal_shift(pa, 1) - pa) * mu
    r, k, v, dw, da, dg = jnp.split(pa, A_SPLIT_POINTS, axis=-1)
    decay = jnp.exp(-A_DECAY_SCALE * jax.nn.sigmoid((w0 + jnp.tanh(dw) @ w_up).astype(f32)))
    a = jax.nn.sigmoid(a0 + da @ a_up)
    g = jax.nn.sigmoid(dg) @ g_up
    kk = k * k_k
    k = k * (1 + (a - 1) * k_a)
    heads = lambda z: z.reshape(bsz, t_len, A_HEADS, A_HEAD_DIM).astype(f32)
    r, k, v, a, kk, decay = heads(r), heads(k), heads(v), heads(a), heads(kk), heads(decay)
    kk = kk * lax.rsqrt(jnp.maximum(jnp.sum(kk * kk, axis=-1, keepdims=True), 1e-24))

    def step(S, inp):
        r_t, w_t, k_t, v_t, kk_t, a_t = inp
        sa = jnp.einsum('bhvk,bhk->bhv', S, -kk_t)
        S = (S * w_t[:, :, None, :] + sa[..., None] * (kk_t * a_t)[:, :, None, :]
             + v_t[..., None] * k_t[:, :, None, :])
        return S, jnp.einsum('bhvk,bhk->bhv', S, r_t)

    xs = tuple(jnp.swapaxes(z, 0, 1) for z in (r, decay, k, v, kk, a))
    S0 = jnp.zeros((bsz, A_HEADS, A_HEAD_DIM, A_HEAD_DIM), f32)
    _, o = lax.scan(step, S0, xs)
    o = jnp.swapaxes(o, 0, 1)
    mean = jnp.mean(o, axis=-1, keepdims=True)
    var = jnp.mean(jnp.square(o - mean), axis=-1, keepdims=True)
    o = ((o - mean) * lax.rsqrt(var + A_GN_EPS)).reshape(bsz, t_len, A_WIDTH)
    o = o * ln_w.astype(f32) + ln_b.astype(f32)
    bonus = jnp.sum(r * k * r_k.astype(f32), axis=-1, keepdims=True) * v
    o = o + bonus.reshape(bsz, t_len, A_WIDTH)
    return o.astype(pa.dtype) * g

def stick_breaking_attention(pb):
    f32 = jnp.float32
    bsz, t_len, _ = pb.shape
    q, k, v = (z.reshape(bsz, t_len, B_HEADS, B_HEAD_DIM).transpose(0, 2, 1, 3)
               for z in jnp.split(pb, 3, axis=-1))
    scale = B_HEAD_DIM ** -0.5

    def block(lo, qb, kb, vb):
        z = jnp.einsum('bhqd,bhkd->bhqk', qb, kb).astype(f32) * scale
        t = lo + jnp.arange(qb.shape[2])[:, None]
        s = jnp.arange(kb.shape[2])[None, :]
        mask = s < t
        log_skip = jnp.where(mask, jax.nn.log_sigmoid(-z), 0.0)
        later = lax.cumsum(log_skip, axis=3, reverse=True) - log_skip
        A = jnp.where(mask, jnp.exp(jax.nn.log_sigmoid(z) + later), 0.0)
        return jnp.einsum('bhqk,bhkd->bhqd', A.astype(vb.dtype), vb)

    o = sweep_query_blocks(block, (q,), (k, v))
    return o.transpose(0, 2, 1, 3).reshape(bsz, t_len, B_WIDTH)

def differential_attention(pc, lam_vecs, subln_g, lambda_init, cos, sin):
    f32 = jnp.float32
    bsz, t_len, _ = pc.shape
    q, k, v = jnp.split(pc, (C_QK_COLS, 2 * C_QK_COLS), axis=-1)
    qk_heads = lambda z: z.reshape(bsz, t_len, C_HEADS, 2, C_QK_DIM).transpose(3, 0, 2, 1, 4)
    q = partial_rope(qk_heads(q), cos, sin)
    k = partial_rope(qk_heads(k), cos, sin)
    v = v.reshape(bsz, t_len, C_HEADS, C_V_DIM).transpose(0, 2, 1, 3)
    lv = lam_vecs.astype(f32)
    lam = jnp.exp(jnp.sum(lv[0] * lv[1])) - jnp.exp(jnp.sum(lv[2] * lv[3])) + lambda_init
    scale = C_QK_DIM ** -0.5

    def block(lo, q1b, q2b, k1b, k2b, vb):
        q_chunk = (lo + jnp.arange(q1b.shape[2])) // CHUNK
        k_chunk = jnp.arange(k1b.shape[2]) // CHUNK
        mask = k_chunk[None, :] <= q_chunk[:, None]

        def attn_map(qb, kb):
            z = jnp.einsum('bhqd,bhkd->bhqk', qb, kb).astype(f32) * scale
            return jax.nn.softmax(jnp.where(mask, z, -jnp.inf), axis=-1)

        A = attn_map(q1b, k1b) - lam * attn_map(q2b, k2b)
        return jnp.einsum('bhqk,bhkd->bhqd', A.astype(vb.dtype), vb)

    o = sweep_query_blocks(block, (q[0], q[1]), (k[0], k[1], v))
    o = rms_norm(o, subln_g) * (1.0 - lambda_init)
    return o.transpose(0, 2, 1, 3).reshape(bsz, t_len, C_WIDTH)

def conv_ffn(h, w_up, conv_w, conv_b, w_down):
    u = h @ w_up
    u = conv_b + sum(conv_w[j] * causal_shift(u, CONV_WIDTH - 1 - j) for j in range(CONV_WIDTH))
    gate, val = jnp.split(u, 2, axis=-1)
    return (jax.nn.silu(gate) * val) @ w_down

def setup_inputs(seed: int = 0) -> dict:
    key = jax.random.key(seed)
    ks = iter(jax.random.split(key, 40))
    nrm = lambda shape, scale: scale * jax.random.normal(next(ks), shape, jnp.float32)
    L, D = DEPTH, D_MODEL
    return {
        'x': nrm((BATCH, SEQ, D), 1.0),
        'norm_mix_g': 1.0 + nrm((L, D), 0.02),
        'norm_ffn_g': 1.0 + nrm((L, D), 0.02),
        'w_in': nrm((L, D, IN_COLS), D ** -0.5),
        'rwkv_mu': jax.random.uniform(next(ks), (L, A_SHIFT_COLS), jnp.float32),
        'rwkv_w0': nrm((L, A_WIDTH), 0.5),
        'rwkv_w_up': nrm((L, A_DECAY_LORA, A_WIDTH), 0.5 * A_DECAY_LORA ** -0.5),
        'rwkv_a0': nrm((L, A_WIDTH), 0.5),
        'rwkv_a_up': nrm((L, A_AAA_LORA, A_WIDTH), 0.5 * A_AAA_LORA ** -0.5),
        'rwkv_g_up': nrm((L, A_GATE_LORA, A_WIDTH), A_GATE_LORA ** -0.5),
        'rwkv_k_k': 0.85 + nrm((L, A_WIDTH), 0.05),
        'rwkv_k_a': 1.0 + nrm((L, A_WIDTH), 0.05),
        'rwkv_r_k': nrm((L, A_HEADS, A_HEAD_DIM), 0.1),
        'rwkv_ln_w': 1.0 + nrm((L, A_WIDTH), 0.02),
        'rwkv_ln_b': nrm((L, A_WIDTH), 0.02),
        'diff_lambda': nrm((L, 4, C_QK_DIM), 0.1),
        'diff_subln_g': 1.0 + nrm((L, C_V_DIM), 0.02),
        'w_branch_a': nrm((L, A_WIDTH, D), A_WIDTH ** -0.5),
        'w_branch_b': nrm((L, B_WIDTH, D), B_WIDTH ** -0.5),
        'w_branch_c': nrm((L, C_WIDTH, D), C_WIDTH ** -0.5),
        'w_out': nrm((L, D, D), D ** -0.5),
        'ffn_w_up': nrm((L, D, 2 * D_FF), D ** -0.5),
        'ffn_conv_w': nrm((L, CONV_WIDTH, 2 * D_FF), CONV_WIDTH ** -0.5),
        'ffn_conv_b': nrm((L, 2 * D_FF), 0.02),
        'ffn_w_down': nrm((L, D_FF, D), D_FF ** -0.5),
        'norm_final_g': 1.0 + nrm((D,), 0.02),
    }

def reference(x, norm_mix_g, norm_ffn_g, w_in, rwkv_mu, rwkv_w0, rwkv_w_up, rwkv_a0,
              rwkv_a_up, rwkv_g_up, rwkv_k_k, rwkv_k_a, rwkv_r_k, rwkv_ln_w, rwkv_ln_b,
              diff_lambda, diff_subln_g, w_branch_a, w_branch_b, w_branch_c, w_out,
              ffn_w_up, ffn_conv_w, ffn_conv_b, ffn_w_down, norm_final_g):
    t_len = x.shape[1]
    inv_freq = ROPE_THETA ** (-jnp.arange(0, C_ROT_DIMS, 2, dtype=jnp.float32) / C_ROT_DIMS)
    ang = jnp.arange(t_len, dtype=jnp.float32)[:, None] * inv_freq[None, :]
    cos, sin = jnp.cos(ang).astype(x.dtype), jnp.sin(ang).astype(x.dtype)

    for l in range(DEPTH):
        h = rms_norm(x, norm_mix_g[l])
        proj = h @ w_in[l]
        pa, pb, pc, pg = jnp.split(proj, GROUP_POINTS, axis=-1)
        oa = rwkv7_time_mix(pa, rwkv_mu[l], rwkv_w0[l], rwkv_w_up[l], rwkv_a0[l], rwkv_a_up[l],
                            rwkv_g_up[l], rwkv_k_k[l], rwkv_k_a[l], rwkv_r_k[l],
                            rwkv_ln_w[l], rwkv_ln_b[l])
        ob = stick_breaking_attention(pb)
        lambda_init = 0.8 - 0.6 * float(np.exp(-0.3 * l))
        oc = differential_attention(pc, diff_lambda[l], diff_subln_g[l], lambda_init, cos, sin)
        ga, gb, gc = jnp.split(jax.nn.sigmoid(pg), N_BRANCHES, axis=-1)
        merged = ga * (oa @ w_branch_a[l]) + gb * (ob @ w_branch_b[l]) + gc * (oc @ w_branch_c[l])
        x = x + merged @ w_out[l]
        x = x + conv_ffn(rms_norm(x, norm_ffn_g[l]), ffn_w_up[l], ffn_conv_w[l],
                         ffn_conv_b[l], ffn_w_down[l])
    return rms_norm(x, norm_final_g)


_drawn_inputs = setup_inputs


def setup_inputs(seed=0):
    import zlib

    import numpy as np

    out = dict(_drawn_inputs(seed))
    spreads = {}
    factors = {'norm_ffn_g': 2.879,
     'rwkv_k_k': 8.0,
     'rwkv_ln_w': 7.148,
     'rwkv_ln_b': 6.401,
     'diff_lambda': 5.249,
     'diff_subln_g': 4.801,
     'ffn_conv_b': 2.954,
     'norm_final_g': 2.794}
    for name, (base, spread) in spreads.items():
        noise = np.random.default_rng([zlib.crc32(name.encode()), seed]).standard_normal(out[name].shape)
        drawn = base * np.exp(spread * noise) if base else spread * noise
        out[name] = __import__('jax').numpy.asarray(drawn.astype(out[name].dtype))
    for name, factor in factors.items():
        out[name] = (out[name] * factor).astype(out[name].dtype)
    return out
```

```python
from contextlib import ExitStack

import concourse.bass as bass
from concourse import mybir

F32 = mybir.dt.float32
F32R = mybir.dt.float32r
F16 = mybir.dt.float16
ALU = mybir.AluOpType
ACT = mybir.ActivationFunctionType
AX = mybir.AxisListType

P = 128
T = 256
D = 1024
KT = D // P
C = 128
HD = 64
AH = 8
CH = 4
BW = 512
BT = BW // P
FT = 2816 // P
SLAB = 1024
RING = 4
AHEAD = 3
DECAY_SCALE = 0.6065306597126334

A_SLABS = 14
DENSE = ([("A", j) for j in range(A_SLABS)]
         + [("Bq", c) for c in range(BT)] + [("Bk", c) for c in range(BT)] + [("Bv", i) for i in range(4)]
         + [("Cq", c) for c in range(BT)] + [("Ck", c) for c in range(BT)] + [("Cv", i) for i in range(4)]
         + [("G", g) for g in range(3 * KT)]
         + [("BR", cp, b) for cp in range(KT // 2) for b in range(3)]
         + [("O", c) for c in range(KT)])
FFN0 = len(DENSE)
SLABS = FFN0 + 3 * FT
FU = 4
FTURNS = (FT - 2) // FU

OUTS, OUT_OF = [], {}
for _n, _s in enumerate(DENSE):
    if _s[0] in ("Bv", "Cv"):
        if _s[1] == 0:
            OUT_OF[_n] = [len(OUTS), len(OUTS) + 1]
            OUTS += ["act", "act"]
        else:
            OUT_OF[_n] = OUT_OF[_n - 1]
    elif _s[0] == "BR":
        OUT_OF[_n] = [len(OUTS), len(OUTS) + 1]
        OUTS += ["dve", "dve"]
    else:
        OUT_OF[_n] = [len(OUTS)]
        OUTS.append("act" if _s[0] in ("Bq", "Bk", "G") else "dve")
EMPTIED = {m: OUTS[:m + 1].count(OUTS[m]) for m in range(len(OUTS))}


def mixing_steps():
    def woven(steps, slabs):
        out, done = [], 0
        for i, s in enumerate(steps):
            out.append(s)
            while done < len(slabs) and done * len(steps) < (i + 1) * len(slabs):
                out.append(("D", slabs[done]))
                done += 1
        return out + [("D", n) for n in slabs[done:]]

    rwkv = [("bon",), ("nat",)]
    for pair in ((0, 1), (2, 3)):
        rwkv += [("mat", c) for c in pair] + [("m1", c, 1) for c in pair]
        for z in (2, 4, 8, 16, 32, 64):
            rwkv += [("m1", c, z) for c in pair] + [("dxy", c, z) for c in pair]
        for s in ("rhs0", "u0", "s1", "rhs1", "u1", "o"):
            rwkv += [(s, c) for c in pair]
    rwkv += [("gn1",), ("gn2",)]
    att = []
    for h in range(AH + 2):
        att += [("bz", h)] if h < AH else []
        att += [("btri", h - 1)] if 1 <= h <= AH else []
        att += [("bav", h - 2)] if h >= 2 else []
    cs = [(h, tt) for h in range(CH) for tt in range(2)]
    for i in range(len(cs) + 1):
        att += [("cs",) + cs[i]] if i < len(cs) else []
        if i:
            att += [("ct",) + cs[i - 1]]
            att += [("cav", cs[i - 1][0])] if cs[i - 1][1] else []
    att += [("crms",)]
    b0 = A_SLABS
    g0 = b0 + 24
    steps = [("norm", 0), ("lam",)] + [("D", n) for n in range(4)] + [("up",)]
    steps += [("D", 4), ("D", 5), ("upg",), ("D", 6), ("kk",)] + [("D", n) for n in range(7, b0)] + [("prep",)]
    steps += woven(rwkv, list(range(b0, g0)))
    steps += woven(att, list(range(g0, g0 + 24)))
    steps += [("gsig",)] + [("D", n) for n in range(g0 + 24, FFN0)] + [("norm", 1)]
    return steps


STEPS = mixing_steps()
TIMES = {}
ORD = {}
for _s in STEPS:
    ORD[_s] = TIMES.get(_s[0], 0)
    TIMES[_s[0]] = ORD[_s] + 1

CF = {"ident": (0, 128), "ones": (128, 128), "bones": (256, 128), "rope": (384, 128), "triN": (512, 128),
      "onesN": (640, 128), "cos": (768, 256), "sin": (1024, 256), "rowL": (1280, 128), "rowR": (1408, 64),
      "eps": (1472, 1), "gneps": (1473, 1), "kkb": (1474, 1), "one": (1475, 1), "zero": (1476, 1), "pad": (1477, 1)}
NCF = 1478
LEVELS = (1, 2, 4, 8, 16, 32, 64)
CB = {"maskS": (0, 128), "maskI": (128, 128), "levelT": (256, 128)}
CB.update({f"level{z}": (384 + 128 * i, 128) for i, z in enumerate(LEVELS)})
NCB = 384 + 128 * len(LEVELS)
PM, _o = {}, 0
for _name, _w in (("g", 8), ("mu", 14), ("w0", 4), ("a0", 4), ("k_k", 4), ("k_a", 4), ("r_k", 4), ("ln_w", 4),
                  ("ln_b", 4), ("subln", 1), ("lam", 4), ("li", 1), ("omli", 1), ("wa_up", 512), ("g_up", 512)):
    PM[_name] = (_o, _w)
    _o += _w
NPM = _o + _o % 2
PF = {"g": (0, 8), "conv": (8, 4 * 2 * FT)}
NPF = 8 + 8 * FT
ACT_OWN = {"turn": 0, "layer": 28}
DVE_OWN = {"turn": 8, "layer": 124}


class Own:

    def __init__(self, eng, sem, counts):
        self.eng, self.sem, self.counts = eng, sem, counts
        self.base, self.n = 0, 0

    def mark(self, ins):
        ins.then_inc(self.sem, 1)
        self.n += 1
        return self.n

    def wait(self, n=None):
        self.eng.wait_ge(self.sem, self.base + (self.n if n is None else n))


def hybrid_blocks(nc, x_in, w_in, mix_in, ffn_in, fin_in, cf_in, cb_in, y_out):
    DEPTH = w_in.shape[0] // SLABS
    with ExitStack() as ctx:
        def sb(name, shape, dt=F32):
            return ctx.enter_context(nc.sbuf_tensor("sb_" + name, shape, dt))

        def sem(name):
            return ctx.enter_context(nc.semaphore(name))

        raw = sb("raw", [P, RING, SLAB])
        hi = sb("hi", [P, RING, SLAB], F32R)
        lo = sb("lo", [P, RING, SLAB], F32R)
        x = sb("x", [P, KT, T])
        hh = sb("hh", [P, KT, T], F32R)
        hl = sb("hl", [P, KT, T], F32R)
        oh = sb("oh", [P, 3 * BT, T], F32R)
        ol = sb("ol", [P, 3 * BT, T], F32R)
        rw = sb("rw", [P, 11 * 1024 + 8])
        inv = sb("inv", [P, 7168])
        qb = sb("qb", [P, BT, T])
        kb = sb("kb", [P, BT, T])
        vb = sb("vb", [P, 2, BW])
        qc = sb("qc", [P, BT, T])
        kc = sb("kc", [P, BT, T])
        vc = sb("vc", [P, 2, BW])
        cf = sb("cf", [P, NCF])
        cb = sb("cb", [P, NCB], F16)
        pm = sb("pm", [P, NPM])
        pf = sb("pf", [P, NPF])
        fin = sb("fin", [P, KT])
        omu = sb("omu", [P, 32])
        small = sb("small", [P, 64])
        s0 = sb("s0", [P, BT, HD])
        rs = sb("rs", [P, T])

        def unit(i, n=1):
            return rw[:, i * 1024:(i + n) * 1024]

        def tiles(i, n=1):
            return unit(i, n).rearrange("p (c t) -> p c t", t=T)

        R, K, V, G, KKt, A_, SG, B1 = [tiles(i) for i in range(8)]
        AR = unit(8, 2).rearrange("p (c h a t) -> p c h a t", c=BT, h=2, a=2)
        SQ, SB = tiles(8), tiles(9)
        PP = rw[:, 10240:10240 + 8 * (C + 1)].rearrange("p (n t) -> p n t", t=C + 1)
        DD, DG = rw[:, 10240:10496], rw[:, 10496:10752]
        Vn = unit(10).rearrange("p (h c) -> p h c", h=2)
        BKn = unit(7).rearrange("p (a c) -> p a c", a=2)
        RHS = rw[:, 6144:6144 + 256].rearrange("p (c n) -> p c n", c=2)
        NU = rw[:, 6400:6400 + 512].rearrange("p (c h n) -> p c h n", c=2, h=2)
        OT = KKt
        GATE = unit(0, 6).rearrange("p (b c t) -> p b c t", b=3, t=T)
        HF = unit(0, 2).rearrange("p (c t) -> p c t", t=T)
        XSQ = unit(2, 2).rearrange("p (c t) -> p c t", t=T)
        MG = unit(6, 2).rearrange("p (c t) -> p c t", t=T)
        BTMP = unit(8).rearrange("p (c t) -> p c t", t=T)
        CV = unit(9).rearrange("p (s t) -> p s t", s=4)
        ABT = inv[:, 0:2048].rearrange("p (c i n) -> p c i n", c=2, i=4)
        KBT = inv[:, 2048:4096].rearrange("p (c i n) -> p c i n", c=2, i=4)
        X = inv[:, 4096:5120].rearrange("p (c i n) -> p c i n", c=2, i=4)
        Y = inv[:, 5120:6144].rearrange("p (c i n) -> p c i n", c=2, i=4)
        M1 = inv[:, 6144:7168].rearrange("p (c i n) -> p c i n", c=2, i=4)
        W1 = inv[:, 0:768].rearrange("p (s n) -> p s n", s=2)
        SP = inv[:, 768:1536].rearrange("p (s n) -> p s n", s=2)
        AB = inv[:, 1536:2304].rearrange("p (s n) -> p s n", s=2)
        PC = inv[:, 2304:3328].rearrange("p (s m n) -> p s m n", s=2, m=2)
        ATC = inv[:, 3328:4352].rearrange("p (s k t) -> p s k t", s=2, k=2)
        OC = inv[:, 4352:5376].rearrange("p (c t) -> p c t", c=CH)
        OSQ = inv[:, 5376:6400].rearrange("p (c t) -> p c t", c=CH)

        psum = ctx.enter_context(nc.psum_tensor("psum", [P, 8, 512], F32))
        bank = [psum[:, i, :] for i in range(8)]

        def banks(b, n=2):
            return psum[:, b:b + n, :]

        def cst(name):
            a, n = CF[name]
            return cf[:, a:a + n]

        def mask(name):
            a, n = CB[name]
            return cb[:, a:a + n]

        def par(name, i=0, n=1):
            a = PM[name][0]
            return pm[:, a + i:a + i + n]

        raw_in = [sem(f"raw_in{i}") for i in range(RING)]
        hi_done = sem("hi_done")
        lo_done = sem("lo_done")
        slab_done = sem("slab_done")
        emptied = {"act": sem("emptied_act"), "dve": sem("emptied_dve")}
        const_in, x_loaded = sem("const_in"), sem("x_loaded")
        mix_in_s, ffn_in_s = sem("mix_params_in"), sem("ffn_params_in")
        squared = sem("squared")
        rms_inv = sem("rms_inv")
        normed = sem("normed")
        split_h, split_l = sem("split_h"), sem("split_l")
        x_added = sem("x_added")
        mixed_now = sem("mixed_now")
        lora_ready = sem("lora_ready")
        rope_raw, rope_mm = sem("rope_raw"), sem("rope_mm")
        gates_ready, merged, branches_h = sem("gates_ready"), sem("merged"), sem("branches_h")
        y_ready, y_stored = sem("y_ready"), sem("y_stored")
        tap2, conv_done = sem("tap2"), sem("conv_done")
        silu_done, prod_done, prod_h, prod_l = sem("silu_done"), sem("prod_done"), sem("prod_h"), sem("prod_l")
        pe_ = {k: sem("pe_" + k) for k in TIMES if k not in ("D", "gsig", "prep")}
        act_ = {k: sem("act_" + k) for k in TIMES if k not in ("D", "norm")}
        dve_ = {k: sem("dve_" + k) for k in TIMES if k not in ("D", "norm")}
        dve_mid = {k: sem("dve_mid_" + k) for k in ("lam", "kk", "prep", "gn1", "gn2", "cs", "crms")}
        act_mid = {k: sem("act_mid_" + k) for k in ("kk", "prep", "gn2", "crms")}
        act_own_s, dve_own_s = sem("act_own"), sem("dve_own")
        block = ctx.enter_context(nc.Block())

        def n_of(kind, l, k):
            return l * TIMES[kind] + k

        def n_out(l, m):
            return emptied[OUTS[m]], l * OUTS.count(OUTS[m]) + EMPTIED[m]

        OUT_BV, OUT_CV = OUT_OF[DENSE.index(("Bv", 3))][1], OUT_OF[DENSE.index(("Cv", 3))][1]
        OUT_CK, OUT_O = OUT_OF[DENSE.index(("Ck", 3))][0], OUT_OF[DENSE.index(("O", 0))][0]

        def ahead_in(split, l, i, n):
            split(None, (n + AHEAD) % RING, l * SLABS + 3 * FU * i + n,
                  l * (16 * SLABS // RING) + (16 * 3 * FU // RING) * i + 16 * ((n + AHEAD) // RING + 1))

        def tap(col, k):
            return pf[:, bass.ds(col + k, 1)]

        def a_tile(j):
            if j < 2:
                return (DD, DG)[j][:, :]
            return (K, R, V)[(j - 2) // BT][:, (j - 2) % BT, :]

        @block.sync
        def _(sp):
            for s in range(RING):
                sp.dma_start(raw[:, s], w_in[s]).then_inc(raw_in[s], 16)
                if s == 0:
                    sp.dma_start(cf[:, :], cf_in).then_inc(const_in, 16)
                    sp.dma_start(cb[:, :], cb_in).then_inc(const_in, 16)
            with sp.Fori(1, DEPTH * SLABS // RING + 1) as i:
                for s in range(RING):
                    sp.wait_ge(hi_done, RING * i + (s - RING + 1))
                    sp.wait_ge(lo_done, RING * i + (s - RING + 1))
                    sp.dma_start(raw[:, s], w_in[RING * i + s]).then_inc(raw_in[s], 16)
            sp.wait_ge(y_ready, KT)
            sp.dma_start(y_out, HF).then_inc(y_stored, 16)
            sp.wait_ge(y_stored, 16)
            for s in range(RING):
                sp.wait_ge(raw_in[s], 16 * (DEPTH * SLABS // RING + 1))

        @block.gpsimd
        def _(pool):
            pool.dma_start(x[:, :, :], x_in).then_inc(x_loaded, 16)
            pool.dma_start(fin[:, :], fin_in).then_inc(x_loaded, 16)
            pool.dma_start(pm[:, :], mix_in[0]).then_inc(mix_in_s, 16)
            pool.dma_start(pf[:, :], ffn_in[0]).then_inc(ffn_in_s, 16)
            with pool.Fori(1, DEPTH) as l:
                pool.wait_ge(dve_["gn2"], n_of("gn2", l, 0))
                pool.dma_start(pm[:, :], mix_in[l]).then_inc(mix_in_s, 16)
                pool.wait_ge(conv_done, l * 2 * FT)
                pool.dma_start(pf[:, :], ffn_in[l]).then_inc(ffn_in_s, 16)

        @block.tensor
        def _(pe):
            def mm(out, lhsT, rhs, start, stop):
                return pe.matmul(out, lhsT, rhs, start=start, stop=stop, skip_group_check=True)

            def after(sig, kind, l, k):
                if k:
                    pe.wait_ge(sig[kind], n_of(kind, l, k))

            def split_mm(out, w, a, start, stop):
                mm(out, w[0], a[0], start, False)
                mm(out, w[0], a[1], False, False)
                return mm(out, w[1], a[0], False, stop)

            def rope(l, n):
                kind, c = DENSE[n]
                pe.wait_ge(rope_raw, l * 2 * BT + (n - DENSE.index(("Cq", 0)) + 1))
                mm(bank[OUT_OF[n][0] % 3][:, T:2 * T], cst("rope"), (qc if kind == "Cq" else kc)[:, c, :],
                   True, True).then_inc(rope_mm, 1)

            def dense(l, n):
                s, kind = n % RING, DENSE[n][0]
                pe.wait_ge(lo_done, l * SLABS + n + 1)
                for m in OUT_OF[n]:
                    if m >= 3 and (n == 0 or m not in OUT_OF[n - 1]):
                        pe.wait_ge(*n_out(l, m - 3))
                if DENSE[n] == ("BR", 0, 0):
                    pe.wait_ge(dve_["gn2"], n_of("gn2", l, 1))
                    pe.wait_ge(dve_["bav"], l * BT + BT)
                    pe.wait_ge(dve_["crms"], n_of("crms", l, 1))
                if kind == "O":
                    pe.wait_ge(split_l, l * 3 * KT + 2 * KT)
                if kind in ("Bv", "Cv"):
                    i = DENSE[n][1]
                    for tt, m in enumerate(OUT_OF[n]):
                        tok = slice(tt * P, (tt + 1) * P)
                        for k2 in range(2):
                            k, cols = 2 * i + k2, slice(k2 * BW, (k2 + 1) * BW)
                            last = split_mm(bank[m % 3][:, :], (hh[:, k, tok], hl[:, k, tok]),
                                            (hi[:, s, cols], lo[:, s, cols]), k == 0, k == KT - 1)
                elif kind == "BR":
                    b = DENSE[n][2]
                    for u, m in enumerate(OUT_OF[n]):
                        for k in range(BT):
                            cols = slice(k * 2 * P + u * P, k * 2 * P + (u + 1) * P)
                            last = split_mm(bank[m % 3][:, 0:T], (hi[:, s, cols], lo[:, s, cols]),
                                            (oh[:, b * BT + k, :], ol[:, b * BT + k, :]), k == 0, k == BT - 1)
                else:
                    m = OUT_OF[n][0]
                    for k in range(KT):
                        if n == 0:
                            pe.wait_ge(split_l, l * 3 * KT + k + 1)
                        cols = slice(k * P, (k + 1) * P)
                        last = split_mm(bank[m % 3][:, 0:T], (hi[:, s, cols], lo[:, s, cols]),
                                        (hh[:, k, :], hl[:, k, :]), k == 0, k == KT - 1)
                last.then_inc(slab_done, 1)
                if n and DENSE[n - 1][0] in ("Cq", "Ck"):
                    rope(l, n - 1)

            def norm(half):
                for c in range(KT):
                    if c % (KT // 2) == 0:
                        pe.wait_ge(squared, half + 1 + c // (KT // 2))
                    last = mm(bank[3][:, 0:T], cst("ones"), XSQ[:, c, :], c == 0, c == KT - 1)
                last.then_inc(pe_["norm"], 1)

            def step(l, s):
                kind = s[0]
                c = s[1] if len(s) > 1 else 0
                j = c % 2
                if kind == "D":
                    dense(l, s[1])
                elif kind == "norm":
                    norm(4 * l + 2 * s[1])
                elif kind == "lam":
                    pe.wait_ge(dve_mid["lam"], n_of("lam", l, 1))
                    mm(bank[7][:, 0:2], cst("ones"), small[:, 0:2], True, True).then_inc(pe_["lam"], 1)
                elif kind == "up":
                    pe.wait_ge(lora_ready, 2 * l + 1)
                    for half, b0 in ((0, 3), (1, 5)):
                        rows = slice(HD * half, HD * (half + 1))
                        for c in range(BT):
                            last = mm(bank[b0 + c // 2][:, (c % 2) * T:(c % 2 + 1) * T],
                                      par("wa_up", c * P, P)[rows], DD[rows, :], c % 2 == 0, True)
                    last.then_inc(pe_["up"], 1)
                elif kind == "upg":
                    pe.wait_ge(lora_ready, 2 * l + 2)
                    pe.wait_ge(act_["up"], n_of("up", l, 1))
                    for c in range(BT):
                        last = mm(bank[3 + c // 2][:, (c % 2) * T:(c % 2 + 1) * T], par("g_up", c * P, P),
                                  DG[:, :], c % 2 == 0, True)
                    last.then_inc(pe_["upg"], 1)
                elif kind == "kk":
                    pe.wait_ge(act_mid["kk"], n_of("kk", l, 1))
                    for b in range(2):
                        last = mm(bank[5 + b][:, :], cst("bones"), unit(8)[:, b * 512:(b + 1) * 512], True, True)
                    last.then_inc(pe_["kk"], 1)
                elif kind == "bon":
                    pe.wait_ge(act_["prep"], n_of("prep", l, 1))
                    for b in range(2):
                        last = mm(bank[3 + b][:, :], cst("bones"), unit(9)[:, b * 512:(b + 1) * 512], True, True)
                    last.then_inc(pe_["bon"], 1)
                elif kind == "nat":
                    pe.wait_ge(dve_["bon"], n_of("bon", l, 1))
                    for ch in range(2):
                        for c in range(BT):
                            pe.transpose(bank[3 + ch][:, c * P:(c + 1) * P], V[:, c, ch * C:(ch + 1) * C], cst("ident"))
                    for i, src in enumerate((K, A_)):
                        for c in range(BT):
                            last = pe.transpose(bank[5 + i][:, c * P:(c + 1) * P], src[:, c, 0:C], cst("ident"))
                    last.then_inc(pe_["nat"], 1)
                elif kind == "mat":
                    pe.wait_ge(act_["nat"], n_of("nat", l, 1))
                    after(dve_, "mat", l, ORD[s])
                    if ORD[s] == 2:
                        pe.wait_ge(act_["o"], n_of("o", l, 2))
                    for src, b0 in ((A_, 3), (K, 5)):
                        for i in range(4):
                            rows, ch = slice(HD * (i // 2), HD * (i // 2 + 1)), i % 2
                            last = mm(bank[b0 + i // 2][:, ch * 256:(ch + 1) * 256], src[rows, c, ch * C:(ch + 1) * C],
                                      AR[rows, c, ch].rearrange("p a t -> p (a t)"), ch == 0, True)
                    last.then_inc(pe_["mat"], 1)
                elif kind == "m1":
                    if s[2] == 1:
                        pe.wait_ge(dve_["mat"], n_of("mat", l, ORD[("mat", c | 1)] + 1))
                    elif s[2] > 2:
                        pe.wait_ge(dve_["dxy"], n_of("dxy", l, ORD[("dxy", c, s[2] // 2)] + 1))
                    after(dve_, "m1", l, ORD[s])
                    for i in range(4):
                        last = mm(bank[3][:, i * P:(i + 1) * P], ABT[:, j, i, 0:C],
                                  cst("ident") if s[2] == 1 else X[:, j, i, :], i == 0, True)
                    last.then_inc(pe_["m1"], 1)
                elif kind == "dxy":
                    pe.wait_ge(dve_["m1"], n_of("m1", l, ORD[("m1", c, s[2])] + 1))
                    if ORD[s] >= 2:
                        pe.wait_ge(dve_["dxy"], n_of("dxy", l, ORD[s] - 1))
                    if s[2] < LEVELS[-1]:
                        for i in range(4):
                            mm(bank[4 + 2 * j][:, i * P:(i + 1) * P], Y[:, j, i, :], M1[:, j, i, :], i == 0, True)
                    for i in range(4):
                        last = mm(bank[5 + 2 * j][:, i * P:(i + 1) * P], M1[:, j, i, :], Y[:, j, i, :], i == 0, True)
                    last.then_inc(pe_["dxy"], 1)
                elif kind == "rhs0":
                    pe.wait_ge(dve_["dxy"], n_of("dxy", l, ORD[("dxy", c | 1, LEVELS[-1])] + 1))
                    after(dve_, "rhs0", l, c)
                    for hp in range(2):
                        last = mm(bank[3 + hp][:, 0:HD], KBT[:, j, 2 * hp, 0:C],
                                  Vn[:, 0, c * P + hp * HD:c * P + (hp + 1) * HD], True, True)
                    last.then_inc(pe_["rhs0"], 1)
                elif kind in ("u0", "u1"):
                    ch = int(kind[1])
                    pe.wait_ge(dve_[f"rhs{ch}"], n_of(f"rhs{ch}", l, c + 1))
                    for hp in range(2):
                        last = mm(bank[5 + j][:, hp * HD:(hp + 1) * HD], Y[:, j, 2 * hp + ch, :],
                                  RHS[:, j, hp * HD:(hp + 1) * HD], hp == 0, True)
                    last.then_inc(pe_[kind], 1)
                elif kind == "s1":
                    pe.wait_ge(act_["u0"], n_of("u0", l, c + 1))
                    after(dve_, "s1", l, c)
                    mm(bank[7][:, 0:P], BKn[:, 0, c * P:(c + 1) * P], Vn[:, 0, c * P:(c + 1) * P], True, False)
                    mm(bank[7][:, 0:P], BKn[:, 1, c * P:(c + 1) * P], NU[:, j, 0, :], False, True)\
                        .then_inc(pe_["s1"], 1)
                elif kind == "rhs1":
                    pe.wait_ge(dve_["s1"], n_of("s1", l, c + 1))
                    after(dve_, "rhs1", l, c)
                    for hp in range(2):
                        rows, out = slice(hp * HD, (hp + 1) * HD), bank[3 + hp][:, 0:HD]
                        mm(out, KBT[:, j, 2 * hp + 1, 0:C], Vn[:, 1, c * P + hp * HD:c * P + (hp + 1) * HD],
                           True, False)
                        last = mm(out, AR[rows, c, 1, 0, :], s0[rows, c, :], False, True)
                    last.then_inc(pe_["rhs1"], 1)
                elif kind == "o":
                    pe.wait_ge(act_["u1"], n_of("u1", l, c + 1))
                    after(act_, "o", l, c)
                    pe.wait_ge(dve_["rhs1"], n_of("rhs1", l, (c | 1) + 1))
                    for hp in range(2):
                        rows, head = slice(hp * HD, (hp + 1) * HD), slice(c * P + hp * HD, c * P + (hp + 1) * HD)
                        for ch in range(2):
                            out, i = bank[3 + hp][rows, ch * C:(ch + 1) * C], 2 * hp + ch
                            mm(out, Vn[:, ch, head], KBT[:, j, i, C:2 * C], ch == 0, False)
                            if ch == 1:
                                mm(out, s0[rows, c, :], AR[rows, c, 1, 1, :], False, False)
                            last = mm(out, NU[:, j, ch, hp * HD:(hp + 1) * HD], ABT[:, j, i, C:2 * C], False, True)
                    last.then_inc(pe_["o"], 1)
                elif kind in ("gn1", "gn2"):
                    if kind == "gn1":
                        pe.wait_ge(act_["o"], n_of("o", l, BT))
                    else:
                        pe.wait_ge(act_["gn1"], n_of("gn1", l, 1))
                    for b in range(2):
                        last = mm(bank[(3 if kind == "gn1" else 5) + b][:, :], cst("bones"),
                                  unit(4 if kind == "gn1" else 7)[:, b * 512:(b + 1) * 512], True, True)
                    last.then_inc(pe_[kind], 1)
                elif kind == "bz":
                    h, rows = c, slice(HD * (c % 2), HD * (c % 2 + 1))
                    if h == 0:
                        pe.wait_ge(*n_out(l, OUT_BV))
                        pe.wait_ge(dve_["gn1"], n_of("gn1", l, 1))
                    if h >= 2:
                        pe.wait_ge(act_["btri"], n_of("btri", l, h - 1))
                    out = bank[3 + h % 2]
                    mm(out[:, 0:T], kb[rows, h // 2, 0:P], qb[rows, h // 2, :], True, False)
                    mm(out[:, T:T + P], kb[rows, h // 2, P:T], qb[rows, h // 2, P:T], False, False)\
                        .then_inc(pe_["bz"], 1)
                elif kind == "btri":
                    h, out = c, bank[3 + c % 2]
                    pe.wait_ge(dve_["bz"], n_of("bz", l, h + 1))
                    mm(out[:, 0:T], cst("triN"), SP[:, j, 0:T], False, False)
                    mm(out[:, P:T], cst("onesN"), SP[:, j, T:T + P], False, False)
                    mm(out[:, T:T + P], cst("triN"), SP[:, j, T:T + P], False, True).then_inc(pe_["btri"], 1)
                elif kind == "bav":
                    h, c, rows = c, c // 2, slice(HD * (c % 2), HD * (c % 2 + 1))
                    out = bank[5 + c % 2]
                    pe.wait_ge(dve_["btri"], n_of("btri", l, h + 1))
                    if h == 0:
                        pe.wait_ge(act_mid["gn2"], 2 * l + 1)
                    if h % 2 == 0 and c >= 2:
                        pe.wait_ge(dve_["bav"], l * BT + c - 1)
                    mm(out[rows, 0:T], vb[:, 0, h * HD:(h + 1) * HD], AB[:, j, 0:T], True, False)
                    mm(out[rows, P:T], vb[:, 1, h * HD:(h + 1) * HD], AB[:, j, T:T + P], False, True)\
                        .then_inc(pe_["bav"], 1)
                elif kind == "cs":
                    h, tt, n, keys = s[1], s[2], ORD[s], P * (s[2] + 1)
                    if n == 0:
                        pe.wait_ge(*n_out(l, OUT_CV))
                        pe.wait_ge(*n_out(l, OUT_CK))
                        pe.wait_ge(act_["btri"], n_of("btri", l, AH))
                    if n == 1:
                        pe.wait_ge(dve_["bav"], l * BT + BT)
                    if n >= 2:
                        pe.wait_ge(act_["cs"], n_of("cs", l, n - 1))
                    for m in range(2):
                        rows, out = slice(HD * m, HD * (m + 1)), bank[3 + 2 * (n % 2) + m]
                        mm(out[:, 0:keys], qc[rows, h, tt * P:(tt + 1) * P], kc[rows, h, 0:keys], True, False)
                        one = slice(HD * m, HD * m + 1)
                        last = mm(out[:, keys - 64:keys], cst("rowL")[one, :], cst("rowR")[one, :], False, True)
                    last.then_inc(pe_["cs"], 1)
                elif kind == "ct":
                    n = ORD[s]
                    pe.wait_ge(dve_["cs"], n_of("cs", l, n + 1))
                    after(act_, "ct", l, n)
                    after(act_, "cav", l, n // 2)
                    for b in range(s[2] + 1):
                        last = pe.transpose(bank[7][:, b * P:(b + 1) * P],
                                            PC[:, n % 2, 0, b * P:(b + 1) * P], cst("ident"))
                    last.then_inc(pe_["ct"], 1)
                elif kind == "cav":
                    h = c
                    pe.wait_ge(act_["ct"], n_of("ct", l, 2 * h + 2))
                    mm(bank[7][:, 0:T], vc[:, 0, h * P:(h + 1) * P], ATC[:, h % 2, 0, :], True, False)
                    mm(bank[7][:, P:T], vc[:, 1, h * P:(h + 1) * P], ATC[:, h % 2, 1, P:T], False, True)\
                        .then_inc(pe_["cav"], 1)
                elif kind == "crms":
                    pe.wait_ge(act_["cav"], n_of("cav", l, CH))
                    pe.wait_ge(act_["cs"], n_of("cs", l, 2 * CH))
                    for b in range(2):
                        last = mm(bank[3 + b][:, :], cst("ones"),
                                  OSQ[:, 2 * b:2 * b + 2, :].rearrange("p c t -> p (c t)"), True, True)
                    last.then_inc(pe_["crms"], 1)

            def ffn_up(l, t, u, slab, s0_, first):
                for which in range(2):
                    s = (s0_ + which) % RING
                    pe.wait_ge(lo_done, slab + (which + 1))
                    if not first:
                        pe.wait_ge(conv_done, l * 2 * FT + 2 * t + (which - 3))
                    for k in range(KT):
                        if first and u == 0 and which == 0:
                            pe.wait_ge(split_l, l * 3 * KT + 2 * KT + k + 1)
                        cols = slice(k * P, (k + 1) * P)
                        last = split_mm(bank[2 * (u % 2) + which][:, 0:T], (hi[:, s, cols], lo[:, s, cols]),
                                        (hh[:, k, :], hl[:, k, :]), k == 0, k == KT - 1)
                    last.then_inc(slab_done, 1)

            def ffn_down(l, t, u, slab, s, first):
                pe.wait_ge(lo_done, slab + 1)
                pe.wait_ge(prod_l, l * FT + t + 1)
                for c in range(KT):
                    cols = slice(c * P, (c + 1) * P)
                    last = split_mm(bank[4 + c // 2][:, (c % 2) * T:(c % 2 + 1) * T], (hi[:, s, cols], lo[:, s, cols]),
                                    (oh[:, u % 2, :], ol[:, u % 2, :]), first and c % 2 == 0, False)
                last.then_inc(slab_done, 1)

            pe.wait_ge(const_in, 32)
            with pe.Fori(0, DEPTH) as l:
                pe.wait_ge(mix_in_s, 16 * l + 16)
                for s in STEPS:
                    step(l, s)
                at = l * SLABS + FFN0
                ffn_up(l, 0, 0, at, FFN0 % RING, True)
                ffn_up(l, 1, 1, at + 2, (FFN0 + 2) % RING, True)
                ffn_down(l, 0, 0, at + 4, (FFN0 + 4) % RING, True)
                with pe.Fori(0, FTURNS) as i:
                    for u in range(FU):
                        t, o = FU * i + (u + 2), 5 + 3 * u
                        slab = l * SLABS + 3 * FU * i + (FFN0 + o)
                        ffn_up(l, t, u, slab, (FFN0 + o) % RING, False)
                        ffn_down(l, FU * i + (u + 1), u + 1, slab + 2, (FFN0 + o + 2) % RING, False)
                ffn_down(l, FT - 1, FT - 1, l * SLABS + SLABS - 1, (SLABS - 1) % RING, False)
            norm(4 * DEPTH)

        @block.scalar
        def _(act):
            own = Own(act, act_own_s, ACT_OWN)

            def do(out, in_, func, scale=1.0, bias=0.0, **kw):
                return act.activation(out, in_, func, scale=scale, bias=bias, **kw)

            def split(m, s, used, landed):
                act.wait_ge(raw_in[s], landed)
                if used is not None:
                    act.wait_ge(slab_done, used)
                do(hi[:, s, :], raw[:, s, :], ACT.Copy).then_inc(hi_done, 1)

            def ahead(l, n):
                split(n + AHEAD, (n + AHEAD) % RING, l * SLABS + n if n else None,
                      l * (16 * SLABS // RING) + 16 * ((n + AHEAD) // RING + 1))

            def dense(l, n):
                kind = DENSE[n][0]
                ahead(l, n)
                if kind in ("Bv", "Cv") and DENSE[n][1] < 3:
                    return
                if DENSE[n] == ("G", 0):
                    act.wait_ge(dve_["gn2"], n_of("gn2", l, 1))
                if kind in ("A", "Bq", "Bk", "Bv", "Cq", "Ck", "Cv", "G"):
                    act.wait_ge(slab_done, l * SLABS + n + 1)
                if kind == "A":
                    j, m = DENSE[n][1], OUT_OF[n][0]
                    do(a_tile(j), bank[m % 3][:, 0:T], ACT.Identity, scale=omu[:, j:j + 1],
                       bias=cst("zero")).then_inc(mixed_now, 1)
                elif kind in ("Bq", "Bk"):
                    do((qb if kind == "Bq" else kb)[:, DENSE[n][1], :], bank[OUT_OF[n][0] % 3][:, 0:T], ACT.Copy,
                       scale=HD ** -0.5 if kind == "Bq" else 1.0).then_inc(emptied["act"], 1)
                elif kind in ("Bv", "Cv"):
                    for tt, m in enumerate(OUT_OF[n]):
                        do((vb if kind == "Bv" else vc)[:, tt, :], bank[m % 3][:, :], ACT.Copy)\
                            .then_inc(emptied["act"], 1)
                elif kind in ("Cq", "Ck"):
                    do((qc if kind == "Cq" else kc)[:, DENSE[n][1], :], bank[OUT_OF[n][0] % 3][:, 0:T], ACT.Copy)\
                        .then_inc(rope_raw, 1)
                elif kind == "G":
                    b, c = divmod(DENSE[n][1], KT)
                    do(GATE[:, b, c, :], bank[OUT_OF[n][0] % 3][:, 0:T], ACT.Copy).then_inc(emptied["act"], 1)
                elif kind == "BR" and DENSE[n][2] == 2:
                    for u in range(2):
                        c = 2 * DENSE[n][1] + u
                        act.wait_ge(merged, l * KT + c + 1)
                        do(hh[:, c, :], MG[:, c, :], ACT.Copy).then_inc(split_h, 1)

            def norm(half, ready):
                for c in range(KT):
                    ready(c)
                    ins = do(XSQ[:, c, :], x[:, c, :], ACT.Square)
                    if c % (KT // 2) == KT // 2 - 1:
                        ins.then_inc(squared, 1)
                act.wait_ge(pe_["norm"], half // 2 + 1)
                own.mark(do(rs[:, :], bank[3][:, 0:T], ACT.Ln, scale=1.0 / D, bias=cst("eps")))
                own.wait()
                do(rs[:, :], rs[:, :], ACT.Exp, scale=-0.5).then_inc(rms_inv, 1)

            def split_normed(l, before):
                for c in range(KT):
                    act.wait_ge(normed, l * 2 * KT + (before // 2) + c + 1)
                    do(hh[:, c, :], HF[:, c, :], ACT.Copy).then_inc(split_h, 1)

            def step(l, s):
                kind = s[0]
                c = s[1] if len(s) > 1 else 0
                j = c % 2
                if kind == "D":
                    dense(l, s[1])
                elif kind == "norm":
                    k = s[1]

                    def ready(c):
                        if k:
                            act.wait_ge(*n_out(l, OUT_O + c))
                    norm(4 * l + 2 * k, ready)
                    split_normed(l, 2 * KT * k)
                elif kind == "lam":
                    act.wait_ge(pe_["lam"], n_of("lam", l, 1))
                    do(small[:, 2:4], bank[7][:, 0:2], ACT.Exp).then_inc(act_["lam"], 1)
                elif kind == "up":
                    act.wait_ge(*n_out(l, 0))
                    do(DD[0:64, :], DD[0:64, :], ACT.Tanh).then_inc(lora_ready, 1)
                    act.wait_ge(*n_out(l, 1))
                    do(DG[:, :], DG[:, :], ACT.Sigmoid).then_inc(lora_ready, 1)
                    act.wait_ge(pe_["up"], n_of("up", l, 1))
                    for dst, b0, name in ((SG, 3, "w0"), (A_, 5, "a0")):
                        for c in range(BT):
                            ins = do(dst[:, c, :], bank[b0 + c // 2][:, (c % 2) * T:(c % 2 + 1) * T], ACT.Sigmoid,
                                     bias=par(name, c))
                    ins.then_inc(act_["up"], 1)
                elif kind == "upg":
                    act.wait_ge(pe_["upg"], n_of("upg", l, 1))
                    for b in range(2):
                        do(unit(3)[:, b * 512:(b + 1) * 512], bank[3 + b][:, :], ACT.Copy)
                    act.wait_ge(dve_["upg"], n_of("upg", l, 1))
                    own.mark(do(unit(7).rearrange("p (n t) -> p n t", t=C), PP[:, :, 1:C + 1], ACT.Exp,
                                scale=DECAY_SCALE))
                    do(small[:, 16:24], small[:, 8:16], ACT.Exp, scale=-DECAY_SCALE)
                    own.wait()
                    do(PP, PP, ACT.Exp, scale=-DECAY_SCALE).then_inc(act_["upg"], 1)
                elif kind == "kk":
                    act.wait_ge(*n_out(l, 5))
                    for c in range(BT):
                        own.mark(do(KKt[:, c, :], K[:, c, :], ACT.Copy, scale=par("k_k", c)))
                    own.wait()
                    do(unit(8), unit(4), ACT.Square).then_inc(act_mid["kk"], 1)
                    act.wait_ge(dve_mid["kk"], n_of("kk", l, 1))
                    own.mark(do(unit(9), unit(9), ACT.Ln, scale=float(2 ** 20)))
                    own.wait()
                    do(unit(9), unit(9), ACT.Exp, scale=-0.5, bias=cst("kkb")).then_inc(act_["kk"], 1)
                elif kind == "prep":
                    act.wait_ge(dve_["kk"], n_of("kk", l, 1))
                    for c in range(BT):
                        ins = do(SQ[:, c, :], A_[:, c, :], ACT.Identity, scale=par("k_a", c), bias=omu[:, 14 + c:15 + c])
                    ins.then_inc(act_mid["prep"], 1)
                    act.wait_ge(dve_mid["prep"], n_of("prep", l, 1))
                    for c in range(BT):
                        ins = do(SB[:, c, :], SB[:, c, :], ACT.Copy, scale=par("r_k", c))
                    ins.then_inc(act_["prep"], 1)
                elif kind == "nat":
                    act.wait_ge(pe_["nat"], n_of("nat", l, 1))
                    for i, dst in enumerate((Vn[:, 0, :], Vn[:, 1, :], BKn[:, 0, :], BKn[:, 1, :])):
                        ins = do(dst, bank[3 + i][:, :], ACT.Copy)
                    ins.then_inc(act_["nat"], 1)
                elif kind in ("u0", "u1"):
                    act.wait_ge(pe_[kind], n_of(kind, l, c + 1))
                    do(NU[:, j, int(kind[1]), :], bank[5 + j][:, 0:P], ACT.Copy, scale=-1.0).then_inc(act_[kind], 1)
                elif kind == "o":
                    act.wait_ge(pe_["o"], n_of("o", l, c + 1))
                    for hp in range(2):
                        rows = slice(hp * HD, (hp + 1) * HD)
                        ins = do(OT[rows, c, :], bank[3 + hp][rows, 0:T], ACT.Copy)
                    ins.then_inc(act_["o"], 1)
                elif kind == "gn1":
                    act.wait_ge(dve_["gn1"], n_of("gn1", l, 1))
                    do(unit(7), unit(4), ACT.Square).then_inc(act_["gn1"], 1)
                elif kind == "gn2":
                    act.wait_ge(pe_["gn2"], n_of("gn2", l, 1))
                    for b in range(2):
                        own.mark(do(unit(6)[:, b * 512:(b + 1) * 512], bank[5 + b][:, :], ACT.Ln, scale=1.0 / HD,
                                    bias=cst("gneps")))
                    own.wait()
                    do(unit(6), unit(6), ACT.Exp, scale=-0.5).then_inc(act_mid["gn2"], 1)
                    act.wait_ge(dve_mid["gn2"], 2 * l + 1)
                    for c in range(BT):
                        ins = do(OT[:, c, :], OT[:, c, :], ACT.Identity, scale=par("ln_w", c), bias=par("ln_b", c))
                    ins.then_inc(act_mid["gn2"], 1)
                    act.wait_ge(dve_mid["gn2"], 2 * l + 2)
                    do(oh[:, 0:BT, :], OT, ACT.Copy).then_inc(act_["gn2"], 1)
                elif kind == "bz":
                    act.wait_ge(pe_["bz"], n_of("bz", l, c + 1))
                    own.mark(do(W1[:, j, :], bank[3 + j][:, 0:T + P], ACT.Abs))
                    own.wait()
                    own.mark(do(W1[:, j, :], W1[:, j, :], ACT.Exp, scale=-1.0))
                    own.wait()
                    do(W1[:, j, :], W1[:, j, :], ACT.Ln, bias=cst("one")).then_inc(act_["bz"], 1)
                elif kind == "btri":
                    act.wait_ge(pe_["btri"], n_of("btri", l, c + 1))
                    do(AB[:, j, :], bank[3 + j][:, 0:T + P], ACT.Exp).then_inc(act_["btri"], 1)
                elif kind == "bav":
                    if c % 2:
                        act.wait_ge(pe_["bav"], n_of("bav", l, c + 1))
                        do(oh[:, BT + c // 2, :], bank[5 + (c // 2) % 2][:, 0:T], ACT.Copy).then_inc(act_["bav"], 1)
                elif kind == "cs":
                    n, keys = ORD[s], P * (s[2] + 1)
                    f = 28 + 12 * (n % 2)
                    act.wait_ge(dve_mid["cs"], n_of("cs", l, n + 1))
                    for m in range(2):
                        ins = do(PC[:, n % 2, m, 0:keys], bank[3 + 2 * (n % 2) + m][:, 0:keys], ACT.Exp,
                                 scale=HD ** -0.5, bias=small[:, f + 2 + m:f + 3 + m],
                                 accum_out=small[:, f + 4 + m:f + 5 + m])
                    ins.then_inc(act_["cs"], 1)
                elif kind == "ct":
                    n, tt = ORD[s], s[2]
                    act.wait_ge(pe_["ct"], n_of("ct", l, n + 1))
                    do(ATC[:, c % 2, 0:tt + 1, tt * P:(tt + 1) * P],
                       bank[7][:, 0:(tt + 1) * P].rearrange("p (k t) -> p k t", t=P), ACT.Copy)\
                        .then_inc(act_["ct"], 1)
                elif kind == "cav":
                    act.wait_ge(pe_["cav"], n_of("cav", l, c + 1))
                    do(OC[:, c, :], bank[7][:, 0:T], ACT.Copy)
                    do(OSQ[:, c, :], bank[7][:, 0:T], ACT.Square).then_inc(act_["cav"], 1)
                elif kind == "crms":
                    act.wait_ge(pe_["crms"], n_of("crms", l, 1))
                    for b in range(2):
                        own.mark(do(OSQ[:, 2 * b:2 * b + 2, :].rearrange("p c t -> p (c t)"), bank[3 + b][:, :], ACT.Ln,
                                    scale=1.0 / (2 * HD), bias=cst("eps")))
                    own.wait()
                    do(OSQ[:, :, :], OSQ[:, :, :], ACT.Exp, scale=-0.5).then_inc(act_mid["crms"], 1)
                    act.wait_ge(dve_mid["crms"], n_of("crms", l, 1))
                    do(oh[:, 2 * BT:3 * BT, :], OC[:, :, :], ACT.Copy).then_inc(act_["crms"], 1)
                elif kind == "gsig":
                    act.wait_ge(emptied["act"], l * OUTS.count("act") + OUTS.count("act"))
                    for b in range(3):
                        do(unit(2 * b, 2), unit(2 * b, 2), ACT.Sigmoid).then_inc(gates_ready, 1)

            def conv(l, t, u, which, slab, col, reuse):
                act.wait_ge(slab_done, slab + 1)
                if reuse:
                    act.wait_ge(prod_l, l * FT + t + (-1))
                do(CV[:, 2 * (u % 2) + which, :], bank[2 * (u % 2) + which][:, 0:T], ACT.Identity,
                   scale=tap(col, 2), bias=tap(col, 3)).then_inc(tap2, 1)

            def silu(l, t, u):
                act.wait_ge(conv_done, l * 2 * FT + 2 * t + 1)
                g = CV[:, 2 * (u % 2), :]
                do(g, g, ACT.Silu).then_inc(silu_done, 1)

            def product(l, t, u):
                act.wait_ge(prod_done, l * FT + t + 1)
                do(oh[:, u % 2, :], CV[:, 2 * (u % 2), :], ACT.Copy).then_inc(prod_h, 1)

            for m in range(AHEAD):
                split(m, m, None, 16)
            act.wait_ge(const_in, 32)
            act.wait_ge(x_loaded, 32)
            with act.Fori(0, DEPTH) as l:
                own.base, own.n = l * ACT_OWN["layer"], 0
                act.wait_ge(mix_in_s, 16 * l + 16)
                for s in STEPS:
                    step(l, s)
                act.wait_ge(ffn_in_s, 16 * l + 16)
                at = l * SLABS + FFN0
                for t in range(2):
                    for which in range(2):
                        n = FFN0 + 2 * t + which
                        ahead(l, n)
                        conv(l, t, t, which, at + 2 * t + which, 8 + 4 * (2 * t + which), False)
                    silu(l, t, t)
                    if t:
                        ahead(l, FFN0 + 4)
                    product(l, t, t)
                with act.Fori(0, FTURNS) as i:
                    for u in range(FU):
                        t = FU * i + (u + 2)
                        o = FFN0 + 5 + 3 * u
                        for which in range(2):
                            ahead_in(split, l, i, o + which)
                            conv(l, t, u, which, l * SLABS + 3 * FU * i + (o + which),
                                 8 * FU * i + (8 + 8 * (u + 2) + 4 * which), True)
                        silu(l, t, u)
                        ahead_in(split, l, i, o + 2)
                        product(l, t, u)
                ahead(l, SLABS - 1)
                act.wait_ge(x_added, 4 * l + 4)
                assert own.n == ACT_OWN["layer"], ("act", own.n)
            own.base, own.n = DEPTH * ACT_OWN["layer"], 0
            norm(4 * DEPTH, lambda c: None)

        @block.vector
        def _(dve):
            own = Own(dve, dve_own_s, DVE_OWN)
            tt = dve.tensor_tensor
            stt = dve.scalar_tensor_tensor

            def bc(ap, n, w):
                return ap.unsqueeze(2).broadcast_to([P, n, w])

            def rep(ap, n):
                return ap.unsqueeze(1).broadcast_to([P, n, ap.shape[1]])

            def split(m, s, used, landed):
                if used is not None:
                    dve.wait_ge(slab_done, used)
                dve.wait_ge(hi_done, m + 1)
                tt(lo[:, s, :], raw[:, s, :], hi[:, s, :].bitcast(F32), ALU.subtract).then_inc(lo_done, 1)

            def ahead(l, n):
                split(l * SLABS + (n + AHEAD), (n + AHEAD) % RING, l * SLABS + n if n else None, None)

            def lo_tile(l, c, src, count):
                dve.wait_ge(split_h, count)
                tt(hl[:, c, :], src[:, c, :], hh[:, c, :].bitcast(F32), ALU.subtract).then_inc(split_l, 1)

            def lo_merged(l, cp):
                for c in (2 * cp, 2 * cp + 1):
                    lo_tile(l, c, MG, l * 3 * KT + KT + c + 1)

            def rotate(l, n):
                kind, c = DENSE[n]
                dst, i = (qc if kind == "Cq" else kc)[:, c, :], n - DENSE.index(("Cq", 0))
                dve.wait_ge(rope_mm, l * 2 * BT + i + 1)
                own.mark(tt(dst, dst, cst("cos"), ALU.mult))
                own.mark(tt(rs[:, :], bank[OUT_OF[n][0] % 3][:, T:2 * T], cst("sin"), ALU.mult))
                own.wait()
                tt(dst, dst, rs[:, :], ALU.add).then_inc(emptied["dve"], 1)

            def dense(l, n):
                kind = DENSE[n][0]
                ahead(l, n)
                if n and DENSE[n - 1][0] in ("Cq", "Ck"):
                    rotate(l, n - 1)
                if kind == "BR" and DENSE[n][2] == 0 and DENSE[n][1]:
                    lo_merged(l, DENSE[n][1] - 1)
                if DENSE[n] == ("O", 0):
                    lo_merged(l, KT // 2 - 1)
                if kind == "A":
                    j, b = DENSE[n][1], bank[OUT_OF[n][0] % 3]
                    dve.wait_ge(mixed_now, l * A_SLABS + j + 1)
                    dst = a_tile(j)
                    stt(dst[:, 1:T], b[:, 0:T - 1], par("mu", j), dst[:, 1:T], ALU.mult, ALU.add)\
                        .then_inc(emptied["dve"], 1)
                elif kind == "BR":
                    cp, b = DENSE[n][1:]
                    dve.wait_ge(slab_done, l * SLABS + n + 1)
                    if cp == 0:
                        dve.wait_ge(gates_ready, 3 * l + b + 1)
                    for u, m in enumerate(OUT_OF[n]):
                        c = 2 * cp + u
                        tt((BTMP[:, 2 * (b % 2) + u, :] if b else MG[:, c, :]), GATE[:, b, c, :], bank[m % 3][:, 0:T],
                           ALU.mult).then_inc(emptied["dve"], 1)
                    if b:
                        dve.wait_ge(*n_out(l, OUT_OF[n][1]))
                        if b == 2:
                            own.wait()
                        for u in range(2):
                            c = 2 * cp + u
                            ins = tt(MG[:, c, :], MG[:, c, :], BTMP[:, 2 * (b % 2) + u, :], ALU.add)
                            if b == 1:
                                own.mark(ins)
                            else:
                                ins.then_inc(merged, 1)
                elif kind == "O":
                    c = DENSE[n][1]
                    dve.wait_ge(slab_done, l * SLABS + n + 1)
                    tt(x[:, c, :], x[:, c, :], bank[OUT_OF[n][0] % 3][:, 0:T], ALU.add).then_inc(emptied["dve"], 1)

            def norm(half, g, out_sem):
                dve.wait_ge(rms_inv, half // 2 + 1)
                for c in range(KT):
                    stt(HF[:, c, :], x[:, c, :], g(c), rs[:, :], ALU.mult, ALU.mult).then_inc(out_sem, 1)

            def step(l, s):
                kind = s[0]
                c = s[1] if len(s) > 1 else 0
                j = c % 2
                if kind == "D":
                    dense(l, s[1])
                elif kind == "norm":
                    k = s[1]
                    if k:
                        dve.wait_ge(ffn_in_s, 16 * l + 16)
                    norm(4 * l + 2 * k, (lambda c: pf[:, c:c + 1]) if k else (lambda c: par("g", c)), normed)
                    for c in range(KT):
                        lo_tile(l, c, HF, l * 3 * KT + 2 * KT * k + c + 1)
                elif kind == "lam":
                    dve.tensor_scalar(omu[:, 0:14], par("mu", 0, 14), -1.0, 1.0, ALU.mult, ALU.add)
                    dve.tensor_scalar(omu[:, 14:18], par("k_a", 0, 4), -1.0, 1.0, ALU.mult, ALU.add)
                    tt(omu[:, 18:19], par("subln"), par("omli"), ALU.mult)
                    lv = par("lam", 0, 4).rearrange("p (a b) -> p a b", b=2)
                    tt(small[:, 0:2], lv[:, :, 0], lv[:, :, 1], ALU.mult).then_inc(dve_mid["lam"], 1)
                    dve.wait_ge(act_["lam"], n_of("lam", l, 1))
                    stt(small[:, 4:5], small[:, 3:4], small[:, 2:3], par("li"), ALU.subtract, ALU.subtract)\
                        .then_inc(dve_["lam"], 1)
                elif kind == "upg":
                    dve.wait_ge(pe_["upg"], n_of("upg", l, 1))
                    dve.wait_ge(act_["up"], n_of("up", l, 1))
                    own.mark(dve.memset(PP[:, :, 0:1], 0.0))
                    e = unit(6).rearrange("p (n t) -> p n t", t=C)
                    for n in range(8):
                        ins = dve.tensor_tensor_scan(PP[:, n, 1:C + 1], e[:, n, :], e[:, n, :], 0.0, ALU.add,
                                                     ALU.bypass)
                    own.mark(ins)
                    own.wait()
                    own.mark(dve.tensor_copy(small[:, 8:16], PP[:, :, C // 2]))
                    own.wait()
                    tt(PP, PP, bc(small[:, 8:16], 8, C + 1), ALU.subtract).then_inc(dve_["upg"], 1)
                elif kind == "kk":
                    dve.wait_ge(pe_["kk"], n_of("kk", l, 1))
                    for b in range(2):
                        ins = dve.tensor_scalar(unit(9)[:, b * 512:(b + 1) * 512], bank[5 + b][:, :], 1e-24, None, ALU.max)
                    ins.then_inc(dve_mid["kk"], 1)
                    dve.wait_ge(act_["kk"], n_of("kk", l, 1))
                    tt(unit(4), unit(4), unit(9), ALU.mult).then_inc(dve_["kk"], 1)
                elif kind == "prep":
                    dve.wait_ge(act_mid["prep"], n_of("prep", l, 1))
                    dve.wait_ge(*n_out(l, A_SLABS - 1))
                    own.mark(tt(unit(1), unit(1), unit(8), ALU.mult))
                    dve.wait_ge(dve_["kk"], n_of("kk", l, 1))
                    own.mark(tt(unit(5), unit(4), unit(5), ALU.mult))
                    own.wait(own.n - 1)
                    tt(unit(9), unit(0), unit(1), ALU.mult).then_inc(dve_mid["prep"], 1)
                    pend = PP.rearrange("p (c h) t -> p c h t", h=2)[:, :, 0, C]
                    own.mark(tt(small[:, 24:28], pend, small[:, 16:24].rearrange("p (c h) -> p c h", h=2)[:, :, 1],
                                ALU.mult))
                    own.wait()
                    tt(unit(5), unit(5), unit(7), ALU.mult)
                    tt(unit(1), unit(1), unit(7), ALU.mult).then_inc(dve_["prep"], 1)
                elif kind == "bon":
                    dve.wait_ge(pe_["bon"], n_of("bon", l, 1))
                    ar = unit(8, 2).rearrange("p (n a t) -> p n a t", a=2, t=C)
                    own.mark(tt(ar[:, :, 1, :], unit(0).rearrange("p (n t) -> p n t", t=C), PP[:, :, 1:C + 1],
                                ALU.mult))
                    tt(ar[:, :, 0, :], unit(4).rearrange("p (n t) -> p n t", t=C), PP[:, :, 0:C], ALU.mult)
                    own.wait()
                    for b in range(2):
                        cols = slice(b * 512, (b + 1) * 512)
                        ins = tt(unit(0)[:, cols], bank[3 + b][:, :], unit(2)[:, cols], ALU.mult)
                    ins.then_inc(dve_["bon"], 1)
                elif kind == "mat":
                    dve.wait_ge(pe_["mat"], n_of("mat", l, ORD[s] + 1))
                    a, _ = CB["maskS"]
                    both = cb[:, a:a + 2 * P]
                    for dst, b0 in ((ABT, 3), (KBT, 5)):
                        for b in range(2):
                            ins = tt(dst[:, j, 2 * b:2 * b + 2, :], bank[b0 + b][:, :].rearrange("p (i n) -> p i n", i=2),
                                     rep(both, 2), ALU.mult)
                    ins.then_inc(dve_["mat"], 1)
                elif kind == "m1":
                    z = s[2]
                    dve.wait_ge(pe_["m1"], n_of("m1", l, ORD[s] + 1))
                    ins = tt(M1[:, j], bank[3][:, :].rearrange("p (i n) -> p i n", i=4), rep(mask(f"level{z}"), 4),
                             ALU.mult)
                    if z > 1:
                        ins.then_inc(dve_["m1"], 1)
                    else:
                        own.mark(ins)
                        dve.wait_ge(dve_["mat"], n_of("mat", l, ORD[("mat", c)] + 1))
                        own.mark(tt(Y[:, j], ABT[:, j, :, 0:C], rep(mask("levelT"), 4), ALU.mult))
                        own.wait(own.n - 1)
                        tt(X[:, j], rep(cst("ident"), 4), M1[:, j], ALU.subtract)
                        own.wait()
                        tt(Y[:, j], rep(cst("ident"), 4), Y[:, j], ALU.subtract).then_inc(dve_["m1"], 1)
                elif kind == "dxy":
                    dve.wait_ge(pe_["dxy"], n_of("dxy", l, ORD[s] + 1))
                    for dst, b in ((X, 4), (Y, 5)):
                        if s[2] < LEVELS[-1] or dst is Y:
                            ins = tt(dst[:, j], dst[:, j], bank[b + 2 * j][:, :].rearrange("p (i n) -> p i n", i=4),
                                     ALU.subtract)
                    ins.then_inc(dve_["dxy"], 1)
                elif kind in ("rhs0", "rhs1"):
                    dve.wait_ge(pe_[kind], n_of(kind, l, c + 1))
                    dve.tensor_copy(RHS[:, j, :].rearrange("p (h n) -> p h n", h=2), banks(3)[:, :, 0:HD]).then_inc(dve_[kind], 1)
                elif kind == "s1":
                    dve.wait_ge(pe_["s1"], n_of("s1", l, c + 1))
                    for hp in range(2):
                        rows, cols = slice(hp * HD, (hp + 1) * HD), slice(hp * HD, (hp + 1) * HD)
                        ins = dve.tensor_scalar(s0[rows, c, :], bank[7][rows, cols], small[rows, 24 + c:25 + c], None,
                                                ALU.mult)
                    ins.then_inc(dve_["s1"], 1)
                elif kind == "gn1":
                    dve.wait_ge(pe_["gn1"], n_of("gn1", l, 1))
                    for b in range(2):
                        cols = slice(b * 512, (b + 1) * 512)
                        ins = stt(unit(4)[:, cols], bank[3 + b][:, :], -1.0 / HD, unit(4)[:, cols], ALU.mult, ALU.add)
                    ins.then_inc(dve_["gn1"], 1)
                elif kind == "gn2":
                    dve.wait_ge(act_mid["gn2"], 2 * l + 1)
                    tt(unit(4), unit(4), unit(6), ALU.mult).then_inc(dve_mid["gn2"], 1)
                    dve.wait_ge(act_mid["gn2"], 2 * l + 2)
                    own.mark(tt(unit(4), unit(4), unit(0), ALU.add))
                    own.wait()
                    tt(unit(4), unit(4), unit(3), ALU.mult).then_inc(dve_mid["gn2"], 1)
                    dve.wait_ge(act_["gn2"], n_of("gn2", l, 1))
                    tt(ol[:, 0:BT, :], OT, oh[:, 0:BT, :].bitcast(F32), ALU.subtract).then_inc(dve_["gn2"], 1)
                elif kind == "bz":
                    z = bank[3 + j][:, 0:T + P]
                    diag = SP[:, j, :].rearrange("p (k n) -> p k n", n=P)[:, 0:3:2, :]
                    dve.wait_ge(act_["bz"], n_of("bz", l, c + 1))
                    own.mark(stt(SP[:, j, :], z, 0.0, W1[:, j, :], ALU.max, ALU.add))
                    own.wait()
                    tt(diag, diag, rep(mask("maskS"), 2), ALU.mult).then_inc(dve_["bz"], 1)
                elif kind == "btri":
                    diag = AB[:, j, :].rearrange("p (k n) -> p k n", n=P)[:, 0:3:2, :]
                    dve.wait_ge(act_["btri"], n_of("btri", l, c + 1))
                    stt(diag, diag, 3e38, rep(mask("maskS"), 2), ALU.min, ALU.mult).then_inc(dve_["btri"], 1)
                elif kind == "bav":
                    if c % 2:
                        dve.wait_ge(act_["bav"], l * BT + c // 2 + 1)
                        tt(ol[:, BT + c // 2, :], bank[5 + (c // 2) % 2][:, 0:T], oh[:, BT + c // 2, :].bitcast(F32),
                           ALU.subtract).then_inc(dve_["bav"], 1)
                elif kind == "cs":
                    n, keys = ORD[s], P * (s[2] + 1)
                    f = 28 + 12 * (n % 2)
                    dve.wait_ge(pe_["cs"], n_of("cs", l, n + 1))
                    own.mark(dve.tensor_reduce(small[:, f:f + 2],
                                               banks(3 + 2 * (n % 2))[:, :, 0:keys],
                                               AX.X, ALU.max))
                    own.wait()
                    dve.tensor_scalar(small[:, f + 2:f + 4], small[:, f:f + 2], -HD ** -0.5, None, ALU.mult)\
                        .then_inc(dve_mid["cs"], 1)
                    dve.wait_ge(act_["cs"], n_of("cs", l, n + 1))
                    own.mark(dve.reciprocal(small[:, f + 6:f + 8], small[:, f + 4:f + 6]))
                    own.wait()
                    dve.wait_ge(dve_["lam"], n_of("lam", l, 1))
                    own.mark(tt(small[:, f + 8:f + 9], small[:, f + 7:f + 8], small[:, 4:5], ALU.mult))
                    a, b = PC[:, n % 2, 0, 0:keys], PC[:, n % 2, 1, 0:keys]
                    own.mark(dve.tensor_scalar(a, a, small[:, f + 6:f + 7], None, ALU.mult))
                    own.wait()
                    stt(a, b, small[:, f + 8:f + 9], a, ALU.mult, ALU.add).then_inc(dve_["cs"], 1)
                elif kind == "crms":
                    dve.wait_ge(act_mid["crms"], n_of("crms", l, 1))
                    dve.wait_ge(dve_mid["lam"], n_of("lam", l, 1))
                    stt(OC[:, :, :], OC[:, :, :], omu[:, 18:19], OSQ[:, :, :], ALU.mult, ALU.mult)\
                        .then_inc(dve_mid["crms"], 1)
                    dve.wait_ge(act_["crms"], n_of("crms", l, 1))
                    tt(ol[:, 2 * BT:3 * BT, :], OC[:, :, :], oh[:, 2 * BT:3 * BT, :].bitcast(F32), ALU.subtract)\
                        .then_inc(dve_["crms"], 1)

            def conv(l, t, u, which, col):
                k = 2 * (u % 2) + which
                dve.wait_ge(tap2, l * 2 * FT + 2 * t + (which + 1))
                own.mark(stt(CV[:, k, 1:T], bank[k][:, 0:T - 1], tap(col, 1), CV[:, k, 1:T], ALU.mult, ALU.add))
                own.wait()
                stt(CV[:, k, 2:T], bank[k][:, 0:T - 2], tap(col, 0), CV[:, k, 2:T], ALU.mult, ALU.add)\
                    .then_inc(conv_done, 1)

            def product(l, t, u):
                g, v = CV[:, 2 * (u % 2), :], CV[:, 2 * (u % 2) + 1, :]
                dve.wait_ge(silu_done, l * FT + t + 1)
                dve.wait_ge(conv_done, l * 2 * FT + 2 * t + 2)
                tt(g, g, v, ALU.mult).then_inc(prod_done, 1)

            def product_lo(l, t, u):
                dve.wait_ge(prod_h, l * FT + t + 1)
                tt(ol[:, u % 2, :], CV[:, 2 * (u % 2), :], oh[:, u % 2, :].bitcast(F32), ALU.subtract)\
                    .then_inc(prod_l, 1)

            for m in range(AHEAD):
                split(m, m, None, None)
            dve.wait_ge(const_in, 32)
            with dve.Fori(0, DEPTH) as l:
                own.base, own.n = l * DVE_OWN["layer"], 0
                dve.wait_ge(mix_in_s, 16 * l + 16)
                for s in STEPS:
                    step(l, s)
                for t in range(2):
                    for which in range(2):
                        ahead(l, FFN0 + 2 * t + which)
                        conv(l, t, t, which, 8 + 4 * (2 * t + which))
                    product(l, t, t)
                    if t:
                        ahead(l, FFN0 + 4)
                    product_lo(l, t, t)
                before = own.n
                with dve.Fori(0, FTURNS) as i:
                    own.base = l * DVE_OWN["layer"] + i * DVE_OWN["turn"]
                    for u in range(FU):
                        t = FU * i + (u + 2)
                        o = FFN0 + 5 + 3 * u
                        for which in range(2):
                            ahead_in(lambda m, s, used, landed: split(used + AHEAD, s, used, None), l, i, o + which)
                            conv(l, t, u, which, 8 * FU * i + (8 + 8 * (u + 2) + 4 * which))
                        product(l, t, u)
                        ahead_in(lambda m, s, used, landed: split(used + AHEAD, s, used, None), l, i, o + 2)
                        product_lo(l, t, u)
                assert own.n - before == DVE_OWN["turn"], ("dve turn", own.n - before)
                own.base, own.n = l * DVE_OWN["layer"], before + FTURNS * DVE_OWN["turn"]
                ahead(l, SLABS - 1)
                dve.wait_ge(slab_done, l * SLABS + SLABS)
                for b in range(4):
                    pair = x[:, 2 * b:2 * b + 2, :].rearrange("p c t -> p (c t)")
                    tt(pair, pair, bank[4 + b][:, :], ALU.add).then_inc(x_added, 1)
                assert own.n == DVE_OWN["layer"], ("dve", own.n)
            norm(4 * DEPTH, lambda c: fin[:, c:c + 1], y_ready)
        return nc


def constants():
    import numpy as np

    cf, cb = np.zeros((P, NCF), np.float32), np.zeros((P, NCB), np.float32)

    def put(dst, where, name, a):
        dst[:a.shape[0], where[name][0]:where[name][0] + where[name][1]] = a
    i = np.arange(P)
    row, col = i[:, None], i[None, :]
    put(cf, CF, "ident", np.eye(P))
    put(cf, CF, "ones", np.ones((P, P)))
    put(cf, CF, "bones", row // HD == col // HD)
    rope = np.zeros((P, P))
    half = HD // 8
    for m in range(2):
        for d in range(half):
            rope[m * HD + d + half, m * HD + d] = -1.0
            rope[m * HD + d, m * HD + d + half] = 1.0
    put(cf, CF, "rope", rope)
    put(cf, CF, "triN", -(row >= col).astype(np.float32))
    put(cf, CF, "onesN", -np.ones((P, P)))
    inv_freq = np.float32(500000.0) ** (-np.arange(0, 2 * half, 2, dtype=np.float32) / np.float32(2 * half))
    ang = inv_freq[:, None].astype(np.float32) * np.arange(T, dtype=np.float32)[None, :]
    cos, sin = np.ones((P, T)), np.zeros((P, T))
    for m in range(2):
        for o in (0, half):
            cos[m * HD + o:m * HD + o + half] = np.cos(ang)
            sin[m * HD + o:m * HD + o + half] = np.sin(ang)
    put(cf, CF, "cos", cos)
    put(cf, CF, "sin", sin)
    put(cf, CF, "rowL", np.broadcast_to((i < 64).astype(np.float32)[None, :], (P, P)))
    put(cf, CF, "rowR", np.full((P, 64), -1e30))
    for name, v in (("eps", 1e-6), ("gneps", 64e-5), ("kkb", 10 * np.log(2.0)), ("one", 1.0)):
        put(cf, CF, name, np.full((P, 1), v))
    put(cb, CB, "maskS", row < col)
    put(cb, CB, "maskI", row <= col)

    def level(t, s, z):
        return (t // (2 * z) == s // (2 * z)) & (t // z % 2 == 1) & (s // z % 2 == 0)
    put(cb, CB, "levelT", level(col, row, 1))
    for z in LEVELS:
        put(cb, CB, f"level{z}", level(row, col, z))
    return cf, cb.astype(np.float16)


def lay_out(a):
    import numpy as np

    L = a["w_in"].shape[0]
    f = {k: np.asarray(v) for k, v in a.items()}

    def cols_major(w, cols):
        n, k, m = w.shape
        return w.reshape(n, k // P, P, m // cols, cols).transpose(0, 3, 2, 1, 4)

    w = f["w_in"]
    a0, b0, c0, g0 = 0, 1792, 1792 + 1536, 1792 + 3072
    lora = w[:, :, 1536:1792]

    def square(x):
        return cols_major(x, P).reshape(L, -1, P, SLAB)

    def values(x):
        return x.reshape(L, 4, 2, P, BW).transpose(0, 1, 3, 2, 4).reshape(L, 4, P, SLAB)
    parts = [square(lora), square(w[:, :, 512:1024]), square(w[:, :, 0:512]), square(w[:, :, 1024:1536]),
             square(w[:, :, b0:b0 + 1024]), values(w[:, :, b0 + 1024:b0 + 1536]),
             square(w[:, :, c0:c0 + 1024]), values(w[:, :, c0 + 1024:c0 + 1536]), square(w[:, :, g0:])]
    br = np.stack([cols_major(f[n], 2 * P).reshape(L, KT // 2, P, SLAB)
                   for n in ("w_branch_a", "w_branch_b", "w_branch_c")], axis=2)
    parts += [br.reshape(L, -1, P, SLAB), square(f["w_out"])]
    up = square(f["ffn_w_up"]).reshape(L, 2, FT, P, SLAB)
    down = f["ffn_w_down"].reshape(L, FT, P, SLAB)
    ffn = [up[:, 0, 0], up[:, 1, 0]]
    for t in range(1, FT):
        ffn += [up[:, 0, t], up[:, 1, t], down[:, t - 1]]
    ffn.append(down[:, FT - 1])
    parts.append(np.stack(ffn, axis=1))
    stream = np.concatenate(parts, axis=1).reshape(L * SLABS, P, SLAB)
    stream = np.concatenate([stream, np.zeros((RING, P, SLAB), np.float32)])

    def vec(x):
        return x.reshape(L, -1, P).transpose(0, 2, 1)
    mu = f["rwkv_mu"]
    mu = np.concatenate([mu[:, 1536:1792], mu[:, 512:1024], mu[:, 0:512], mu[:, 1024:1536]], axis=1)
    lam = np.zeros((L, P, 4), np.float32)
    lam[:, 0:64] = f["diff_lambda"].transpose(0, 2, 1)
    li = np.array([0.8 - 0.6 * float(np.exp(-0.3 * i)) for i in range(L)])
    li2 = np.stack([np.broadcast_to(v[:, None], (L, P)) for v in (li, 1.0 - li)], axis=2).astype(np.float32)
    mix = np.concatenate([vec(f["norm_mix_g"]), vec(mu), vec(f["rwkv_w0"]), vec(f["rwkv_a0"]), vec(f["rwkv_k_k"]),
                          vec(f["rwkv_k_a"]), vec(f["rwkv_r_k"].reshape(L, -1)), vec(f["rwkv_ln_w"]),
                          vec(f["rwkv_ln_b"]), vec(f["diff_subln_g"]), lam, li2,
                          np.concatenate([f["rwkv_w_up"], f["rwkv_a_up"]], axis=1), f["rwkv_g_up"],
                          np.zeros((L, P, NPM - _o), np.float32)], axis=2)
    cw = np.concatenate([f["ffn_conv_w"], f["ffn_conv_b"][:, None]], axis=1)
    cw = cw.reshape(L, 4, 2, FT, P).transpose(0, 4, 3, 2, 1).reshape(L, P, 8 * FT)
    ffn_par = np.concatenate([vec(f["norm_ffn_g"]), cw], axis=2)
    cf, cb = constants()
    c = np.ascontiguousarray
    return {"x_t": c(f["x"][0].T.reshape(KT, P, T).transpose(1, 0, 2)), "w_stream": c(stream), "mix_par": c(mix),
            "ffn_par": c(ffn_par), "final_g": c(f["norm_final_g"].reshape(KT, P).T), "const_f": c(cf),
            "const_b": c(cb)}


_INS = ["x_t", "w_stream", "mix_par", "ffn_par", "final_g", "const_f", "const_b"]


def kernel(**inputs):
    import numpy as np
    import concourse.bacc as bacc
    from concourse.bass_utils import run_bass_kernel_spmd

    nc = bacc.Bacc("TRN2", target_bir_lowering=False, num_devices=1)
    arrays = lay_out(inputs)
    args = [nc.dram_tensor(n, arrays[n].shape, mybir.dt.from_np(arrays[n].dtype), kind="ExternalInput").ap()
            for n in _INS]
    y = nc.dram_tensor("y_t", (P, KT, T), F32, kind="ExternalOutput").ap()
    hybrid_blocks(nc, *args, y)
    r = run_bass_kernel_spmd(nc, [arrays], core_ids=[0])
    out = r.results[0]["y_t"]
    return np.ascontiguousarray(out.transpose(2, 1, 0).reshape(1, T, D))
```

```python
from contextlib import ExitStack

import concourse.bass as bass
from concourse import mybir

F32 = mybir.dt.float32
F32R = mybir.dt.float32r
F16 = mybir.dt.float16
ALU = mybir.AluOpType
ACT = mybir.ActivationFunctionType
AX = mybir.AxisListType

P = 128
T = 256
D = 1024
KT = D // P
C = 128
HD = 64
AH = 8
CH = 4
BW = 512
BT = BW // P
FT = 2816 // P
SLAB = 1024
RING = 4
AHEAD = 3
DECAY_SCALE = 0.6065306597126334

A_SLABS = 14
DENSE = ([("A", j) for j in range(A_SLABS)]
         + [("Bq", c) for c in range(BT)] + [("Bk", c) for c in range(BT)] + [("Bv", i) for i in range(4)]
         + [("Cq", c) for c in range(BT)] + [("Ck", c) for c in range(BT)] + [("Cv", i) for i in range(4)]
         + [("G", g) for g in range(2 * KT)]
         + [s for i in range(4) for s in (("G", 2 * KT + 2 * i), ("BR", 0, i), ("G", 2 * KT + 2 * i + 1))]
         + [("BR", *bc) for bc in ((1, 0), (1, 1), (2, 0), (1, 2), (2, 1), (1, 3), (2, 2), (2, 3))]
         + [("O", c) for c in range(KT)])
FFN0 = len(DENSE)
SLABS = FFN0 + 3 * FT
FU = 4
FTURNS = (FT - 2) // FU

OUTS, OUT_OF = [], {}
for _n, _s in enumerate(DENSE):
    if _s[0] in ("Bv", "Cv"):
        if _s[1] == 0:
            OUT_OF[_n] = [len(OUTS), len(OUTS) + 1]
            OUTS += ["act", "act"]
        else:
            OUT_OF[_n] = OUT_OF[_n - 1]
    else:
        OUT_OF[_n] = [len(OUTS)]
        OUTS.append("dve")
EMPTIED = {m: OUTS[:m + 1].count(OUTS[m]) for m in range(len(OUTS))}


def mixing_steps():
    at = {k: n for n, k in reversed(list(enumerate(DENSE)))}
    g0 = at[("G", 0)]

    def woven(steps, slabs):
        out, done = [], 0
        for i, s in enumerate(steps):
            out.append(s)
            while done < len(slabs) and done * len(steps) < (i + 1) * len(slabs):
                out.append(("D", slabs[done]))
                done += 1
        return out + [("D", n) for n in slabs[done:]]

    def dense(a, b):
        return [("D", n) for n in range(a, b)]

    steps = [("xs", 0)] + dense(0, 1) + [("lam",)] + dense(1, 2) + [("norm", 0)] + dense(2, 5) + [("lora",)]
    steps += dense(5, 6) + [("up",)] + dense(6, 7) + [("upg",)] + dense(7, 8) + [("kkq",)] + dense(8, 10)
    steps += [("kk",)] + dense(10, 11) + [("prepa",)] + dense(11, 13) + [("prepb",)] + dense(13, 16) + [("bon",)]
    steps += dense(16, 17) + [("natv",)] + dense(17, 18) + [("natk",)] + dense(18, 19)
    n = 19
    for pair in ((0, 1), (2, 3)):
        for i, s in enumerate([(c, what) for c in pair for what in ("ab", "abt", "akb")]):
            steps += [("mat",) + s] + dense(n, n + i % 2)
            n += i % 2
        for z in (2, 4, 8, 16, 32, 64):
            steps += [("m1", c, z) for c in pair] + [("dxy", c, z) for c in pair]
            if z in (2, 8, 32):
                steps += dense(n, n + 1)
                n += 1
        for s in ("rhs0", "u0", "s1", "rhs1", "u1", "o"):
            fill = min(g0 - n, 1 if s in ("u0", "s1", "rhs1", "o") else 0)
            steps += [(s, c) for c in pair] + dense(n, n + fill)
            n += fill
    steps += dense(n, g0) + [("bz", 0), ("gn1",)] + dense(g0, g0 + 1) + [("bz", 1), ("gn2",)] + dense(g0 + 1, g0 + 3)
    heads = []
    for h in range(AH + 2):
        heads += [("btri", h - 1)] if 1 <= h <= AH else []
        heads += [("bz", h)] if 2 <= h < AH else []
        heads += [("bav", h - 2)] if h >= 2 else []
    steps += woven(heads, list(range(g0 + 3, g0 + 2 * KT)))
    maps = []
    cs = [(h, tt) for h in range(CH) for tt in range(2)]
    for i in range(len(cs) + 1):
        maps += [("cs",) + cs[i]] if i < len(cs) else []
        if i:
            maps += [("ct",) + cs[i - 1]]
            maps += [("cav", cs[i - 1][0])] if cs[i - 1][1] else []
    last = at[("BR", 1, 0)]
    steps += [("gsig", 0)] + woven(maps, list(range(g0 + 2 * KT, last)))
    steps += [("crms",)] + dense(last, last + 1) + [("gsig", 1)] + dense(last + 1, last + 2) + [("gsig", 2)]
    steps += dense(last + 2, FFN0)
    out, late = [], []
    for i, s in enumerate(steps):
        out.append(s)
        ready = [e for e in late if not (e == ("E", 0) and ("norm", 0) not in out)
                 and not (DENSE[e[1]][0] == "G" and ("gn2",) not in out)]
        out += ready
        late = [e for e in late if e not in ready]
        if s[0] == "D" and not (DENSE[s[1]][0] in ("Bv", "Cv") and DENSE[s[1]][1] < 3):
            late.append(("E", s[1]))
    return out + late + [("xs", 1)]


STEPS = mixing_steps()
TIMES = {}
ORD = {}
for _s in STEPS:
    ORD[_s] = TIMES.get(_s[0], 0)
    TIMES[_s[0]] = ORD[_s] + 1

CF = {"ident": (0, 128), "ones": (128, 128), "bones": (256, 128), "rope": (384, 128), "triN": (512, 128),
      "onesN": (640, 128), "cos": (768, 256), "sin": (1024, 256), "rowL": (1280, 128), "rowR": (1408, 64),
      "eps": (1472, 1), "gneps": (1473, 1), "kkb": (1474, 1), "one": (1475, 1), "zero": (1476, 1), "pad": (1477, 1)}
NCF = 1478
LEVELS = (1, 2, 4, 8, 16, 32, 64)
CB = {"maskS": (0, 128), "maskI": (128, 128), "levelT": (256, 128)}
CB.update({f"level{z}": (384 + 128 * i, 128) for i, z in enumerate(LEVELS)})
NCB = 384 + 128 * len(LEVELS)
PM, _o = {}, 0
for _name, _w in (("g", 8), ("mu", 14), ("w0", 4), ("a0", 4), ("k_k", 4), ("k_a", 4), ("r_k", 4), ("ln_w", 4),
                  ("ln_b", 4), ("subln", 1), ("lam", 4), ("li", 1), ("omli", 1), ("wa_up", 512), ("g_up", 512)):
    PM[_name] = (_o, _w)
    _o += _w
NPM = _o + _o % 2
PF = {"g": (0, 8), "conv": (8, 4 * 2 * FT)}
NPF = 8 + 8 * FT
ACT_OWN = {"turn": 0, "layer": 28}
DVE_OWN = {"turn": 8, "layer": 116}


class Own:

    def __init__(self, eng, sem, counts):
        self.eng, self.sem, self.counts = eng, sem, counts
        self.base, self.n = 0, 0

    def mark(self, ins):
        ins.then_inc(self.sem, 1)
        self.n += 1
        return self.n

    def wait(self, n=None):
        self.eng.wait_ge(self.sem, self.base + (self.n if n is None else n))


def hybrid_blocks(nc, x_in, w_in, mix_in, ffn_in, fin_in, cf_in, cb_in, y_out):
    DEPTH = w_in.shape[0] // SLABS
    with ExitStack() as ctx:
        def sb(name, shape, dt=F32):
            return ctx.enter_context(nc.sbuf_tensor("sb_" + name, shape, dt))

        def sem(name):
            return ctx.enter_context(nc.semaphore(name))

        raw = sb("raw", [P, RING, SLAB])
        hi = sb("hi", [P, RING, SLAB], F32R)
        lo = sb("lo", [P, RING, SLAB], F32R)
        x = sb("x", [P, KT, T])
        hh = sb("hh", [P, KT, T], F32R)
        hl = sb("hl", [P, KT, T], F32R)
        oh = sb("oh", [P, 3 * BT, T], F32R)
        ol = sb("ol", [P, 3 * BT, T], F32R)
        rw = sb("rw", [P, 11 * 1024 + 8])
        inv = sb("inv", [P, 7168])
        qb = sb("qb", [P, BT, T])
        kb = sb("kb", [P, BT, T])
        vb = sb("vb", [P, 2, BW])
        qc = sb("qc", [P, BT, T])
        kc = sb("kc", [P, BT, T])
        vc = sb("vc", [P, 2, BW])
        cf = sb("cf", [P, NCF])
        cb = sb("cb", [P, NCB], F16)
        pm = sb("pm", [P, NPM])
        pf = sb("pf", [P, NPF])
        fin = sb("fin", [P, KT])
        omu = sb("omu", [P, 32])
        small = sb("small", [P, 64])
        s0 = sb("s0", [P, BT, HD])
        rs = sb("rs", [P, T + 2])

        def unit(i, n=1):
            return rw[:, i * 1024:(i + n) * 1024]

        def tiles(i, n=1):
            return unit(i, n).rearrange("p (c t) -> p c t", t=T)

        R, K, V, G, KKt, A_, SG, B1 = [tiles(i) for i in range(8)]
        AR = unit(8, 2).rearrange("p (c h a t) -> p c h a t", c=BT, h=2, a=2)
        SQ, SB = tiles(8), tiles(9)
        PP = rw[:, 10240:10240 + 8 * (C + 1)].rearrange("p (n t) -> p n t", t=C + 1)
        DD, DG = rw[:, 10240:10496], rw[:, 10496:10752]
        Vn = unit(10).rearrange("p (h c) -> p h c", h=2)
        BKn = unit(7).rearrange("p (a c) -> p a c", a=2)
        RHS = rw[:, 6144:6144 + 256].rearrange("p (c n) -> p c n", c=2)
        NU = rw[:, 6400:6400 + 512].rearrange("p (c h n) -> p c h n", c=2, h=2)
        OT = KKt
        GATE = unit(0, 6).rearrange("p (b c t) -> p b c t", b=3, t=T)
        HF = unit(0, 2).rearrange("p (c t) -> p c t", t=T)
        XSQ = unit(2, 2).rearrange("p (c t) -> p c t", t=T)
        MG = unit(6, 2).rearrange("p (c t) -> p c t", t=T)
        BTMP = unit(8).rearrange("p (c n) -> p c n", c=2)
        TMP = qb[:, 0:2, :]
        UM = unit(8).rearrange("p (s t) -> p s t", s=4)
        CV = unit(9).rearrange("p (s t) -> p s t", s=4)
        ABT = inv[:, 0:2048].rearrange("p (c i n) -> p c i n", c=2, i=4)
        KBT = inv[:, 2048:4096].rearrange("p (c i n) -> p c i n", c=2, i=4)
        X = inv[:, 4096:5120].rearrange("p (c i n) -> p c i n", c=2, i=4)
        Y = inv[:, 5120:6144].rearrange("p (c i n) -> p c i n", c=2, i=4)
        M1 = inv[:, 6144:7168].rearrange("p (c i n) -> p c i n", c=2, i=4)
        W1 = inv[:, 0:768].rearrange("p (s n) -> p s n", s=2)
        SP = inv[:, 768:1536].rearrange("p (s n) -> p s n", s=2)
        AB = inv[:, 1536:2304].rearrange("p (s n) -> p s n", s=2)
        PC = inv[:, 2304:3328].rearrange("p (s m n) -> p s m n", s=2, m=2)
        ATC = inv[:, 3328:4352].rearrange("p (s k t) -> p s k t", s=2, k=2)
        OC = inv[:, 4352:5376].rearrange("p (c t) -> p c t", c=CH)
        OSQ = inv[:, 5376:6400].rearrange("p (c t) -> p c t", c=CH)

        psum = ctx.enter_context(nc.psum_tensor("psum", [P, 8, 512], F32))
        bank = [psum[:, i, :] for i in range(8)]

        def banks(b, n=2):
            return psum[:, b:b + n, :]

        def cst(name):
            a, n = CF[name]
            return cf[:, a:a + n]

        def mask(name):
            a, n = CB[name]
            return cb[:, a:a + n]

        def par(name, i=0, n=1):
            a = PM[name][0]
            return pm[:, a + i:a + i + n]

        raw_in = [sem(f"raw_in{i}") for i in range(RING)]
        hi_done = sem("hi_done")
        lo_done = sem("lo_done")
        slab_done = sem("slab_done")
        emptied = {"act": sem("emptied_act"), "dve": sem("emptied_dve")}
        const_in, x_loaded = sem("const_in"), sem("x_loaded")
        mix_in_s, ffn_in_s = sem("mix_params_in"), sem("ffn_params_in")
        square_done = sem("square_done")
        squared = sem("squared")
        rms_inv = sem("rms_inv")
        split_h, split_l = sem("split_h"), sem("split_l")
        merged_h, merged_l = sem("merged_h"), sem("merged_l")
        x_ready = sem("x_ready")
        mixed_now = sem("mixed_now")
        mixed = sem("mixed")
        rope_raw, rope_mm = sem("rope_raw"), sem("rope_mm")
        gates_ready, merged = sem("gates_ready"), sem("merged")
        y_ready, y_stored = sem("y_ready"), sem("y_stored")
        up_scaled = sem("up_scaled")
        tap2, conv_done = sem("tap2"), sem("conv_done")
        silu_done, prod_done, prod_h, prod_l = sem("silu_done"), sem("prod_done"), sem("prod_h"), sem("prod_l")
        pe_ = {k: sem("pe_" + k) for k in TIMES if k not in ("D", "E", "xs", "gsig", "prepa", "prepb", "kkq", "lora")}
        act_ = {k: sem("act_" + k) for k in TIMES if k not in ("D", "E", "xs", "norm")}
        dve_ = {k: sem("dve_" + k) for k in TIMES if k not in ("D", "E", "xs", "norm")}
        dve_mid = {k: sem("dve_mid_" + k) for k in ("lam", "kk", "prepb", "bon", "gn2", "cs", "crms")}
        act_mid = {k: sem("act_mid_" + k) for k in ("kk", "gn2", "crms")}
        act_own_s, dve_own_s = sem("act_own"), sem("dve_own")
        block = ctx.enter_context(nc.Block())

        def n_of(kind, l, k):
            return l * TIMES[kind] + k

        def n_out(l, m):
            return emptied[OUTS[m]], l * OUTS.count(OUTS[m]) + EMPTIED[m]

        OUT_BV, OUT_CV = OUT_OF[DENSE.index(("Bv", 3))][1], OUT_OF[DENSE.index(("Cv", 3))][1]
        OUT_BK, OUT_CK, OUT_O = (OUT_OF[DENSE.index(k)][0] for k in (("Bk", 3), ("Ck", 3), ("O", 0)))
        ADDS = [n for n, k in enumerate(DENSE) if k[0] == "BR" and k[1]]

        def ahead_in(split, l, i, n):
            split(None, (n + AHEAD) % RING, l * SLABS + 3 * FU * i + n,
                  l * (16 * SLABS // RING) + (16 * 3 * FU // RING) * i + 16 * ((n + AHEAD) // RING + 1))

        def tap(col, k):
            return pf[:, bass.ds(col + k, 1)]

        def a_tile(j):
            if j < 2:
                return (DD, DG)[j][:, :]
            return (K, R, V)[(j - 2) // BT][:, (j - 2) % BT, :]

        @block.sync
        def _(sp):
            for s in range(RING):
                sp.dma_start(raw[:, s], w_in[s]).then_inc(raw_in[s], 16)
                if s == 0:
                    sp.dma_start(cf[:, :], cf_in).then_inc(const_in, 16)
                    sp.dma_start(cb[:, :], cb_in).then_inc(const_in, 16)
            with sp.Fori(1, DEPTH * SLABS // RING + 1) as i:
                for s in range(RING):
                    sp.wait_ge(hi_done, RING * i + (s - RING + 1))
                    sp.wait_ge(lo_done, RING * i + (s - RING + 1))
                    sp.dma_start(raw[:, s], w_in[RING * i + s]).then_inc(raw_in[s], 16)
            sp.wait_ge(y_ready, KT)
            sp.dma_start(y_out, HF).then_inc(y_stored, 16)
            sp.wait_ge(y_stored, 16)
            sp.wait_ge(mix_in_s, 16 * DEPTH + 16)
            sp.wait_ge(ffn_in_s, 16 * DEPTH + 16)
            for s in range(RING):
                sp.wait_ge(raw_in[s], 16 * (DEPTH * SLABS // RING + 1))

        @block.gpsimd
        def _(pool):
            pool.dma_start(x[:, :, :], x_in).then_inc(x_loaded, 16)
            pool.dma_start(fin[:, :], fin_in).then_inc(x_loaded, 16)
            pool.dma_start(pm[:, :], mix_in[0]).then_inc(mix_in_s, 16)
            pool.dma_start(pf[:, :], ffn_in[0]).then_inc(ffn_in_s, 16)
            with pool.Fori(0, DEPTH) as l:
                pool.wait_ge(dve_["gn2"], n_of("gn2", l, 1))
                pool.dma_start(pm[:, :], mix_in[l + 1]).then_inc(mix_in_s, 16)
                pool.wait_ge(conv_done, l * 2 * FT + 2 * FT)
                pool.dma_start(pf[:, :], ffn_in[l + 1]).then_inc(ffn_in_s, 16)

        @block.tensor
        def _(pe):
            def mm(out, lhsT, rhs, start, stop):
                return pe.matmul(out, lhsT, rhs, start=start, stop=stop, skip_group_check=True)

            def after(sig, kind, l, k):
                if k:
                    pe.wait_ge(sig[kind], n_of(kind, l, k))

            def split_mm(out, w, a, start, stop):
                mm(out, w[0], a[0], start, False)
                mm(out, w[0], a[1], False, False)
                return mm(out, w[1], a[0], False, stop)

            def rope(l, n):
                kind, c = DENSE[n]
                pe.wait_ge(rope_raw, l * 2 * BT + (n - DENSE.index(("Cq", 0)) + 1))
                mm(bank[OUT_OF[n][0] % 3][:, T:2 * T], cst("rope"), (qc if kind == "Cq" else kc)[:, c, :],
                   True, True).then_inc(rope_mm, 1)

            def dense(l, n):
                s, kind = n % RING, DENSE[n][0]
                pe.wait_ge(lo_done, l * SLABS + n + 1)
                for m in OUT_OF[n]:
                    if m >= 3 and (n == 0 or m not in OUT_OF[n - 1]):
                        pe.wait_ge(*n_out(l, m - 3))
                if kind == "BR" and DENSE[n][2] == 0:
                    pe.wait_ge(*((dve_["gn2"], n_of("gn2", l, 1)), (dve_["bav"], l * BT + BT),
                                 (dve_["crms"], n_of("crms", l, 1)))[DENSE[n][1]])
                if kind in ("Bv", "Cv"):
                    i = DENSE[n][1]
                    for tt, m in enumerate(OUT_OF[n]):
                        tok = slice(tt * P, (tt + 1) * P)
                        for k2 in range(2):
                            k, cols = 2 * i + k2, slice(k2 * BW, (k2 + 1) * BW)
                            last = split_mm(bank[m % 3][:, :], (hh[:, k, tok], hl[:, k, tok]),
                                            (hi[:, s, cols], lo[:, s, cols]), k == 0, k == KT - 1)
                elif kind == "BR":
                    b, m = DENSE[n][1], OUT_OF[n][0]
                    for u in range(2):
                        for k in range(BT):
                            cols = slice(k * 2 * P + u * P, k * 2 * P + (u + 1) * P)
                            last = split_mm(bank[m % 3][:, u * T:(u + 1) * T], (hi[:, s, cols], lo[:, s, cols]),
                                            (oh[:, b * BT + k, :], ol[:, b * BT + k, :]), u == 0 and k == 0,
                                            k == BT - 1)
                else:
                    m = OUT_OF[n][0]
                    for k in range(KT):
                        if n == 0:
                            pe.wait_ge(split_l, l * 2 * KT + k + 1)
                        if DENSE[n] == ("O", 0) and k % 2 == 0:
                            pe.wait_ge(merged_l, l * (KT // 2) + k // 2 + 1)
                        cols = slice(k * P, (k + 1) * P)
                        src = (oh, ol) if kind == "O" else (hh, hl)
                        last = split_mm(bank[m % 3][:, 0:T], (hi[:, s, cols], lo[:, s, cols]),
                                        (src[0][:, k, :], src[1][:, k, :]), k == 0, k == KT - 1)
                last.then_inc(slab_done, 1)
                if n and DENSE[n - 1][0] in ("Cq", "Ck"):
                    rope(l, n - 1)

            def norm(n):
                pe.wait_ge(squared, n + 1)
                for c in range(2):
                    mm(bank[4][:, 0:T], cst("ones"), XSQ[:, c, :], c == 0, False)
                for c in range(2):
                    for tok in range(2):
                        last = mm(bank[4][:, T + tok:T + tok + 1], XSQ[:, c, tok * P:(tok + 1) * P],
                                  cst("ones")[:, 0:1], False, c == 1)
                last.then_inc(pe_["norm"], 1)

            def step(l, s):
                kind = s[0]
                c = s[1] if len(s) > 1 else 0
                j = c % 2
                if kind == "D":
                    dense(l, s[1])
                elif kind == "norm":
                    norm(2 * l)
                elif kind == "lam":
                    pe.wait_ge(dve_mid["lam"], n_of("lam", l, 1))
                    mm(bank[7][:, 0:2], cst("ones"), small[:, 0:2], True, True).then_inc(pe_["lam"], 1)
                elif kind == "up":
                    pe.wait_ge(act_["lora"], 2 * l + 1)
                    for half, b0 in ((0, 3), (1, 5)):
                        rows = slice(HD * half, HD * (half + 1))
                        for c in range(BT):
                            last = mm(bank[b0 + c // 2][:, (c % 2) * T:(c % 2 + 1) * T],
                                      par("wa_up", c * P, P)[rows], DD[rows, :], c % 2 == 0, True)
                    last.then_inc(pe_["up"], 1)
                elif kind == "upg":
                    pe.wait_ge(act_["lora"], 2 * l + 2)
                    pe.wait_ge(act_["up"], n_of("up", l, 1))
                    for c in range(BT):
                        last = mm(bank[3 + c // 2][:, (c % 2) * T:(c % 2 + 1) * T], par("g_up", c * P, P),
                                  DG[:, :], c % 2 == 0, True)
                    last.then_inc(pe_["upg"], 1)
                elif kind == "kk":
                    pe.wait_ge(act_["kkq"], n_of("kkq", l, 1))
                    for b in range(2):
                        last = mm(bank[5 + b][:, :], cst("bones"), unit(8)[:, b * 512:(b + 1) * 512], True, True)
                    last.then_inc(pe_["kk"], 1)
                elif kind == "bon":
                    pe.wait_ge(act_["prepb"], n_of("prepb", l, 1))
                    for b in range(2):
                        last = mm(bank[6 + b][:, :], cst("bones"), unit(9)[:, b * 512:(b + 1) * 512], True, True)
                    last.then_inc(pe_["bon"], 1)
                elif kind == "natv":
                    pe.wait_ge(mixed, l * A_SLABS + A_SLABS)
                    for ch in range(2):
                        for c in range(BT):
                            last = pe.transpose(bank[3 + ch][:, c * P:(c + 1) * P], V[:, c, ch * C:(ch + 1) * C],
                                                cst("ident"))
                    last.then_inc(pe_["natv"], 1)
                elif kind == "natk":
                    pe.wait_ge(dve_["prepb"], n_of("prepb", l, 1))
                    pe.wait_ge(act_["natv"], n_of("natv", l, 1))
                    for b, src in ((5, K), (3, A_)):
                        for c in range(BT):
                            last = pe.transpose(bank[b][:, c * P:(c + 1) * P], src[:, c, 0:C], cst("ident"))
                    last.then_inc(pe_["natk"], 1)
                elif kind == "mat":
                    what, i = s[2], ORD[s] % 6
                    if i >= 2:
                        pe.wait_ge(dve_["mat"], n_of("mat", l, ORD[s] - 1))
                    elif ORD[s] == 0:
                        pe.wait_ge(act_["natk"], n_of("natk", l, 1))
                        pe.wait_ge(dve_["bon"], n_of("bon", l, 1))
                    elif i == 0:
                        pe.wait_ge(act_["o"], n_of("o", l, 2))
                    b0 = 3 + 2 * (i % 2)
                    for i in range(4):
                        rows, ch = slice(HD * (i // 2), HD * (i // 2 + 1)), i % 2
                        toks = slice(ch * C, (ch + 1) * C)
                        if what == "abt":
                            last = mm(bank[b0 + i // 2][:, ch * P:(ch + 1) * P], AR[rows, c, ch, 0, :],
                                      A_[rows, c, toks], ch == 0, True)
                        else:
                            last = mm(bank[b0 + i // 2][:, ch * 256:(ch + 1) * 256],
                                      (A_ if what == "ab" else K)[rows, c, toks],
                                      AR[rows, c, ch].rearrange("p a t -> p (a t)"), ch == 0, True)
                    last.then_inc(pe_["mat"], 1)
                elif kind == "m1":
                    if s[2] == 2:
                        pe.wait_ge(dve_["mat"], n_of("mat", l, ORD[("mat", c | 1, "akb")] + 1))
                    else:
                        pe.wait_ge(dve_["dxy"], n_of("dxy", l, ORD[("dxy", c, s[2] // 2)] + 1))
                    after(dve_, "m1", l, ORD[s])
                    for i in range(4):
                        last = mm(bank[3][:, i * P:(i + 1) * P], ABT[:, j, i, 0:C], X[:, j, i, :], i == 0, True)
                    last.then_inc(pe_["m1"], 1)
                elif kind == "dxy":
                    pe.wait_ge(dve_["m1"], n_of("m1", l, ORD[("m1", c, s[2])] + 1))
                    if ORD[s] >= 2:
                        pe.wait_ge(dve_["dxy"], n_of("dxy", l, ORD[s] - 1))
                    if s[2] < LEVELS[-1]:
                        for i in range(4):
                            mm(bank[4 + 2 * j][:, i * P:(i + 1) * P], Y[:, j, i, :], M1[:, j, i, :], i == 0, True)
                    for i in range(4):
                        last = mm(bank[5 + 2 * j][:, i * P:(i + 1) * P], M1[:, j, i, :], Y[:, j, i, :], i == 0, True)
                    last.then_inc(pe_["dxy"], 1)
                elif kind == "rhs0":
                    pe.wait_ge(dve_["dxy"], n_of("dxy", l, ORD[("dxy", c | 1, LEVELS[-1])] + 1))
                    after(dve_, "rhs0", l, c)
                    for hp in range(2):
                        last = mm(bank[3 + hp][:, 0:HD], KBT[:, j, 2 * hp, 0:C],
                                  Vn[:, 0, c * P + hp * HD:c * P + (hp + 1) * HD], True, True)
                    last.then_inc(pe_["rhs0"], 1)
                elif kind in ("u0", "u1"):
                    ch = int(kind[1])
                    pe.wait_ge(dve_[f"rhs{ch}"], n_of(f"rhs{ch}", l, c + 1))
                    for hp in range(2):
                        last = mm(bank[5 + j][:, hp * HD:(hp + 1) * HD], Y[:, j, 2 * hp + ch, :],
                                  RHS[:, j, hp * HD:(hp + 1) * HD], hp == 0, True)
                    last.then_inc(pe_[kind], 1)
                elif kind == "s1":
                    pe.wait_ge(act_["u0"], n_of("u0", l, c + 1))
                    after(dve_, "s1", l, c)
                    mm(bank[7][:, 0:P], BKn[:, 0, c * P:(c + 1) * P], Vn[:, 0, c * P:(c + 1) * P], True, False)
                    mm(bank[7][:, 0:P], BKn[:, 1, c * P:(c + 1) * P], NU[:, j, 0, :], False, True)\
                        .then_inc(pe_["s1"], 1)
                elif kind == "rhs1":
                    pe.wait_ge(dve_["s1"], n_of("s1", l, c + 1))
                    after(dve_, "rhs1", l, c)
                    for hp in range(2):
                        rows, out = slice(hp * HD, (hp + 1) * HD), bank[3 + hp][:, 0:HD]
                        mm(out, KBT[:, j, 2 * hp + 1, 0:C], Vn[:, 1, c * P + hp * HD:c * P + (hp + 1) * HD],
                           True, False)
                        last = mm(out, AR[rows, c, 1, 0, :], s0[rows, c, :], False, True)
                    last.then_inc(pe_["rhs1"], 1)
                elif kind == "o":
                    pe.wait_ge(act_["u1"], n_of("u1", l, c + 1))
                    after(act_, "o", l, c)
                    pe.wait_ge(dve_["rhs1"], n_of("rhs1", l, (c | 1) + 1))
                    for hp in range(2):
                        rows, head = slice(hp * HD, (hp + 1) * HD), slice(c * P + hp * HD, c * P + (hp + 1) * HD)
                        for ch in range(2):
                            out, i = bank[3 + hp][rows, ch * C:(ch + 1) * C], 2 * hp + ch
                            mm(out, Vn[:, ch, head], KBT[:, j, i, C:2 * C], ch == 0, False)
                            if ch == 1:
                                mm(out, s0[rows, c, :], AR[rows, c, 1, 1, :], False, False)
                            last = mm(out, NU[:, j, ch, hp * HD:(hp + 1) * HD], ABT[:, j, i, C:2 * C], False, True)
                    last.then_inc(pe_["o"], 1)
                elif kind in ("gn1", "gn2"):
                    if kind == "gn1":
                        pe.wait_ge(act_["o"], n_of("o", l, BT))
                        pe.wait_ge(act_["u1"], n_of("u1", l, BT))
                    else:
                        pe.wait_ge(act_["gn1"], n_of("gn1", l, 1))
                    for b in range(2):
                        last = mm(bank[5 + b][:, :], cst("bones"),
                                  unit(4 if kind == "gn1" else 7)[:, b * 512:(b + 1) * 512], True, True)
                    last.then_inc(pe_[kind], 1)
                elif kind == "bz":
                    h, rows = c, slice(HD * (c % 2), HD * (c % 2 + 1))
                    if h == 0:
                        pe.wait_ge(*n_out(l, OUT_BK))
                        pe.wait_ge(*n_out(l, OUT_BV))
                        pe.wait_ge(act_["o"], n_of("o", l, BT))
                    if h >= 2:
                        pe.wait_ge(act_["btri"], n_of("btri", l, h - 1))
                    out = bank[3 + h % 2]
                    mm(out[:, 0:T], kb[rows, h // 2, 0:P], qb[rows, h // 2, :], True, False)
                    mm(out[:, T:T + P], kb[rows, h // 2, P:T], qb[rows, h // 2, P:T], False, False)\
                        .then_inc(pe_["bz"], 1)
                elif kind == "btri":
                    h, out = c, bank[3 + c % 2]
                    pe.wait_ge(dve_["bz"], n_of("bz", l, h + 1))
                    mm(out[:, 0:T], cst("triN"), SP[:, j, 0:T], False, False)
                    mm(out[:, P:T], cst("onesN"), SP[:, j, T:T + P], False, False)
                    mm(out[:, T:T + P], cst("triN"), SP[:, j, T:T + P], False, True).then_inc(pe_["btri"], 1)
                elif kind == "bav":
                    h, c, rows = c, c // 2, slice(HD * (c % 2), HD * (c % 2 + 1))
                    out = bank[5 + c % 2]
                    pe.wait_ge(dve_["btri"], n_of("btri", l, h + 1))
                    if h == 0:
                        pe.wait_ge(act_mid["gn2"], 2 * l + 1)
                    if h % 2 == 0 and c >= 2:
                        pe.wait_ge(dve_["bav"], l * BT + c - 1)
                    mm(out[rows, 0:T], vb[:, 0, h * HD:(h + 1) * HD], AB[:, j, 0:T], True, False)
                    mm(out[rows, P:T], vb[:, 1, h * HD:(h + 1) * HD], AB[:, j, T:T + P], False, True)\
                        .then_inc(pe_["bav"], 1)
                elif kind == "cs":
                    h, tt, n, keys = s[1], s[2], ORD[s], P * (s[2] + 1)
                    if n == 0:
                        pe.wait_ge(*n_out(l, OUT_CV))
                        pe.wait_ge(*n_out(l, OUT_CK))
                        pe.wait_ge(act_["btri"], n_of("btri", l, AH))
                    if n == 1:
                        pe.wait_ge(dve_["bav"], l * BT + BT)
                    if n >= 2:
                        pe.wait_ge(act_["cs"], n_of("cs", l, n - 1))
                    for m in range(2):
                        rows, out = slice(HD * m, HD * (m + 1)), bank[3 + 2 * (n % 2) + m]
                        mm(out[:, 0:keys], qc[rows, h, tt * P:(tt + 1) * P], kc[rows, h, 0:keys], True, False)
                        one = slice(HD * m, HD * m + 1)
                        last = mm(out[:, keys - 64:keys], cst("rowL")[one, :], cst("rowR")[one, :], False, True)
                    last.then_inc(pe_["cs"], 1)
                elif kind == "ct":
                    n = ORD[s]
                    pe.wait_ge(dve_["cs"], n_of("cs", l, n + 1))
                    after(act_, "ct", l, n)
                    after(act_, "cav", l, n // 2)
                    for b in range(s[2] + 1):
                        last = pe.transpose(bank[7][:, b * P:(b + 1) * P],
                                            PC[:, n % 2, 0, b * P:(b + 1) * P], cst("ident"))
                    last.then_inc(pe_["ct"], 1)
                elif kind == "cav":
                    h = c
                    pe.wait_ge(act_["ct"], n_of("ct", l, 2 * h + 2))
                    mm(bank[7][:, 0:T], vc[:, 0, h * P:(h + 1) * P], ATC[:, h % 2, 0, :], True, False)
                    mm(bank[7][:, P:T], vc[:, 1, h * P:(h + 1) * P], ATC[:, h % 2, 1, P:T], False, True)\
                        .then_inc(pe_["cav"], 1)
                elif kind == "crms":
                    pe.wait_ge(act_["cav"], n_of("cav", l, CH))
                    pe.wait_ge(act_["cs"], n_of("cs", l, 2 * CH))
                    for b in range(2):
                        last = mm(bank[3 + b][:, :], cst("ones"),
                                  OSQ[:, 2 * b:2 * b + 2, :].rearrange("p c t -> p (c t)"), True, True)
                    last.then_inc(pe_["crms"], 1)

            def ffn_up(l, t, u, slab, s0_, first):
                for which in range(2):
                    s = (s0_ + which) % RING
                    pe.wait_ge(lo_done, slab + (which + 1))
                    if not first:
                        pe.wait_ge(up_scaled, l * 2 * FT + 2 * t + (which - 3))
                    for k in range(KT):
                        if first and u == 0 and which == 0:
                            pe.wait_ge(split_l, l * 2 * KT + KT + k + 1)
                        cols = slice(k * P, (k + 1) * P)
                        last = split_mm(bank[2 * (u % 2) + which][:, 0:T], (hi[:, s, cols], lo[:, s, cols]),
                                        (hh[:, k, :], hl[:, k, :]), k == 0, k == KT - 1)
                    last.then_inc(slab_done, 1)

            def ffn_down(l, t, u, slab, s, first):
                pe.wait_ge(lo_done, slab + 1)
                pe.wait_ge(prod_l, l * FT + t + 1)
                for c in range(KT):
                    cols = slice(c * P, (c + 1) * P)
                    last = split_mm(bank[4 + c // 2][:, (c % 2) * T:(c % 2 + 1) * T], (hi[:, s, cols], lo[:, s, cols]),
                                    (oh[:, u % 2, :], ol[:, u % 2, :]), first and c % 2 == 0, False)
                last.then_inc(slab_done, 1)

            pe.wait_ge(const_in, 32)
            with pe.Fori(0, DEPTH) as l:
                pe.wait_ge(mix_in_s, 16 * l + 16)
                for s in STEPS:
                    step(l, s)
                at = l * SLABS + FFN0
                ffn_up(l, 0, 0, at, FFN0 % RING, True)
                norm(2 * l + 1)
                ffn_up(l, 1, 1, at + 2, (FFN0 + 2) % RING, True)
                ffn_down(l, 0, 0, at + 4, (FFN0 + 4) % RING, True)
                with pe.Fori(0, FTURNS) as i:
                    for u in range(FU):
                        t, o = FU * i + (u + 2), 5 + 3 * u
                        slab = l * SLABS + 3 * FU * i + (FFN0 + o)
                        ffn_up(l, t, u, slab, (FFN0 + o) % RING, False)
                        ffn_down(l, FU * i + (u + 1), u + 1, slab + 2, (FFN0 + o + 2) % RING, False)
                ffn_down(l, FT - 1, FT - 1, l * SLABS + SLABS - 1, (SLABS - 1) % RING, False)
            norm(2 * DEPTH)

        @block.scalar
        def _(act):
            own = Own(act, act_own_s, ACT_OWN)

            def do(out, in_, func, scale=1.0, bias=0.0, **kw):
                return act.activation(out, in_, func, scale=scale, bias=bias, **kw)

            def split(m, s, used, landed):
                act.wait_ge(raw_in[s], landed)
                if used is not None:
                    act.wait_ge(slab_done, used)
                do(hi[:, s, :], raw[:, s, :], ACT.Copy).then_inc(hi_done, 1)

            def ahead(l, n):
                split(n + AHEAD, (n + AHEAD) % RING, l * SLABS + n if n else None,
                      l * (16 * SLABS // RING) + 16 * ((n + AHEAD) // RING + 1))

            def empty(l, n):
                kind = DENSE[n][0]
                if kind == "A":
                    j = DENSE[n][1]
                    act.wait_ge(*n_out(l, OUT_OF[n][0]))
                    do(a_tile(j), TMP[:, j % 2, :], ACT.Identity, scale=omu[:, j:j + 1],
                       bias=cst("zero")).then_inc(mixed_now, 1)
                elif kind in ("Bv", "Cv"):
                    act.wait_ge(slab_done, l * SLABS + n + 1)
                    for tt, m in enumerate(OUT_OF[n]):
                        do((vb if kind == "Bv" else vc)[:, tt, :], bank[m % 3][:, :], ACT.Copy,
                           scale=rs[:, T + tt:T + tt + 1]).then_inc(emptied["act"], 1)
                elif kind == "BR" and DENSE[n][1] == 2:
                    pair = slice(2 * DENSE[n][2], 2 * DENSE[n][2] + 2)
                    act.wait_ge(merged, l * len(ADDS) + ADDS.index(n) + 1)
                    do(oh[:, pair, :], MG[:, pair, :], ACT.Copy).then_inc(merged_h, 1)

            def squares(ready=None):
                for b in range(4):
                    if ready:
                        ready(b)
                    do(XSQ[:, 2 * b:2 * b + 2, :], x[:, 2 * b:2 * b + 2, :], ACT.Square).then_inc(square_done, 1)

            def norm(n):
                act.wait_ge(pe_["norm"], n + 1)
                own.mark(do(rs[:, :], bank[4][:, 0:T + 2], ACT.Ln, scale=1.0 / D, bias=cst("eps")))
                own.wait()
                do(rs[:, :], rs[:, :], ACT.Exp, scale=-0.5).then_inc(rms_inv, 1)

            def step(l, s):
                kind = s[0]
                c = s[1] if len(s) > 1 else 0
                j = c % 2
                if kind == "D":
                    ahead(l, s[1])
                elif kind == "E":
                    empty(l, s[1])
                elif kind == "xs":
                    if c:
                        act.wait_ge(ffn_in_s, 16 * l + 16)
                    for t in range(KT):
                        if c:
                            act.wait_ge(*n_out(l, OUT_O + t))
                        elif t % 2 == 0:
                            act.wait_ge(x_ready, 4 * l + t // 2 + 1)
                        do(hh[:, t, :], x[:, t, :], ACT.Copy, scale=pf[:, t:t + 1] if c else par("g", t))\
                            .then_inc(split_h, 1)
                    squares()
                    act.preload_act_table_set("natural_log_exp_and_others")
                elif kind == "norm":
                    norm(2 * l)
                elif kind == "lam":
                    act.wait_ge(pe_["lam"], n_of("lam", l, 1))
                    do(small[:, 2:4], bank[7][:, 0:2], ACT.Exp).then_inc(act_["lam"], 1)
                elif kind == "lora":
                    act.wait_ge(mixed, l * A_SLABS + 1)
                    do(DD[0:64, :], DD[0:64, :], ACT.Tanh).then_inc(act_["lora"], 1)
                    act.wait_ge(mixed, l * A_SLABS + 2)
                    do(DG[:, :], DG[:, :], ACT.Sigmoid).then_inc(act_["lora"], 1)
                elif kind == "up":
                    act.wait_ge(pe_["up"], n_of("up", l, 1))
                    for dst, b0, name in ((SG, 3, "w0"), (A_, 5, "a0")):
                        for c in range(BT):
                            ins = do(dst[:, c, :], bank[b0 + c // 2][:, (c % 2) * T:(c % 2 + 1) * T], ACT.Sigmoid,
                                     bias=par(name, c))
                    ins.then_inc(act_["up"], 1)
                elif kind == "upg":
                    act.preload_act_table_set("natural_log_exp_and_others")
                    act.wait_ge(pe_["upg"], n_of("upg", l, 1))
                    for b in range(2):
                        do(unit(3)[:, b * 512:(b + 1) * 512], bank[3 + b][:, :], ACT.Copy)
                    act.wait_ge(dve_["upg"], n_of("upg", l, 1))
                    own.mark(do(unit(7).rearrange("p (n t) -> p n t", t=C), PP[:, :, 1:C + 1], ACT.Exp,
                                scale=DECAY_SCALE))
                    do(small[:, 16:24], small[:, 8:16], ACT.Exp, scale=-DECAY_SCALE)
                    own.wait()
                    do(PP, PP, ACT.Exp, scale=-DECAY_SCALE).then_inc(act_["upg"], 1)
                elif kind == "kkq":
                    act.wait_ge(mixed, l * A_SLABS + 6)
                    for c in range(BT):
                        own.mark(do(KKt[:, c, :], K[:, c, :], ACT.Copy, scale=par("k_k", c)))
                    own.wait()
                    do(unit(8), unit(4), ACT.Square).then_inc(act_["kkq"], 1)
                elif kind == "kk":
                    act.wait_ge(dve_mid["kk"], n_of("kk", l, 1))
                    own.mark(do(unit(9), unit(9), ACT.Ln, scale=float(2 ** 20)))
                    own.wait()
                    do(unit(9), unit(9), ACT.Exp, scale=-0.5, bias=cst("kkb")).then_inc(act_["kk"], 1)
                    for c in range(BT):
                        ins = do(SQ[:, c, :], A_[:, c, :], ACT.Identity, scale=par("k_a", c), bias=omu[:, 14 + c:15 + c])
                    ins.then_inc(act_mid["kk"], 1)
                elif kind == "prepb":
                    act.wait_ge(dve_mid["prepb"], n_of("prepb", l, 1))
                    for c in range(BT):
                        ins = do(SB[:, c, :], SB[:, c, :], ACT.Copy, scale=par("r_k", c))
                    ins.then_inc(act_["prepb"], 1)
                elif kind == "natv":
                    act.wait_ge(dve_mid["bon"], n_of("bon", l, 1))
                    act.wait_ge(pe_["natv"], n_of("natv", l, 1))
                    do(Vn[:, 0, :], bank[3][:, :], ACT.Copy)
                    do(Vn[:, 1, :], bank[4][:, :], ACT.Copy).then_inc(act_["natv"], 1)
                elif kind == "natk":
                    act.wait_ge(pe_["natk"], n_of("natk", l, 1))
                    do(BKn[:, 0, :], bank[5][:, :], ACT.Copy)
                    do(BKn[:, 1, :], bank[3][:, :], ACT.Copy).then_inc(act_["natk"], 1)
                elif kind in ("u0", "u1"):
                    act.wait_ge(pe_[kind], n_of(kind, l, c + 1))
                    do(NU[:, j, int(kind[1]), :], bank[5 + j][:, 0:P], ACT.Copy, scale=-1.0).then_inc(act_[kind], 1)
                elif kind == "o":
                    act.wait_ge(pe_["o"], n_of("o", l, c + 1))
                    for hp in range(2):
                        rows = slice(hp * HD, (hp + 1) * HD)
                        ins = do(OT[rows, c, :], bank[3 + hp][rows, 0:T], ACT.Copy)
                    ins.then_inc(act_["o"], 1)
                elif kind == "gn1":
                    act.wait_ge(dve_["gn1"], n_of("gn1", l, 1))
                    do(unit(7), unit(4), ACT.Square).then_inc(act_["gn1"], 1)
                elif kind == "gn2":
                    act.wait_ge(pe_["gn2"], n_of("gn2", l, 1))
                    for b in range(2):
                        own.mark(do(unit(6)[:, b * 512:(b + 1) * 512], bank[5 + b][:, :], ACT.Ln, scale=1.0 / HD,
                                    bias=cst("gneps")))
                    own.wait()
                    do(unit(6), unit(6), ACT.Exp, scale=-0.5).then_inc(act_mid["gn2"], 1)
                    act.wait_ge(dve_mid["gn2"], 2 * l + 1)
                    for c in range(BT):
                        ins = do(OT[:, c, :], OT[:, c, :], ACT.Identity, scale=par("ln_w", c), bias=par("ln_b", c))
                    ins.then_inc(act_mid["gn2"], 1)
                    act.wait_ge(dve_mid["gn2"], 2 * l + 2)
                    do(oh[:, 0:BT, :], OT, ACT.Copy).then_inc(act_["gn2"], 1)
                elif kind == "bz":
                    act.wait_ge(pe_["bz"], n_of("bz", l, c + 1))
                    own.mark(do(W1[:, j, :], bank[3 + j][:, 0:T + P], ACT.Abs))
                    own.wait()
                    own.mark(do(W1[:, j, :], W1[:, j, :], ACT.Exp, scale=-1.0))
                    own.wait()
                    do(W1[:, j, :], W1[:, j, :], ACT.Ln, bias=cst("one")).then_inc(act_["bz"], 1)
                elif kind == "btri":
                    act.wait_ge(pe_["btri"], n_of("btri", l, c + 1))
                    do(AB[:, j, :], bank[3 + j][:, 0:T + P], ACT.Exp).then_inc(act_["btri"], 1)
                elif kind == "bav":
                    if c % 2:
                        act.wait_ge(pe_["bav"], n_of("bav", l, c + 1))
                        do(oh[:, BT + c // 2, :], bank[5 + (c // 2) % 2][:, 0:T], ACT.Copy).then_inc(act_["bav"], 1)
                elif kind == "cs":
                    n, keys = ORD[s], P * (s[2] + 1)
                    f = 28 + 12 * (n % 2)
                    act.wait_ge(dve_mid["cs"], n_of("cs", l, n + 1))
                    for m in range(2):
                        ins = do(PC[:, n % 2, m, 0:keys], bank[3 + 2 * (n % 2) + m][:, 0:keys], ACT.Exp,
                                 scale=HD ** -0.5, bias=small[:, f + 2 + m:f + 3 + m],
                                 accum_out=small[:, f + 4 + m:f + 5 + m])
                    ins.then_inc(act_["cs"], 1)
                elif kind == "ct":
                    n, tt = ORD[s], s[2]
                    act.wait_ge(pe_["ct"], n_of("ct", l, n + 1))
                    do(ATC[:, c % 2, 0:tt + 1, tt * P:(tt + 1) * P],
                       bank[7][:, 0:(tt + 1) * P].rearrange("p (k t) -> p k t", t=P), ACT.Copy)\
                        .then_inc(act_["ct"], 1)
                elif kind == "cav":
                    act.wait_ge(pe_["cav"], n_of("cav", l, c + 1))
                    do(OC[:, c, :], bank[7][:, 0:T], ACT.Copy)
                    do(OSQ[:, c, :], bank[7][:, 0:T], ACT.Square).then_inc(act_["cav"], 1)
                elif kind == "crms":
                    act.wait_ge(pe_["crms"], n_of("crms", l, 1))
                    for b in range(2):
                        own.mark(do(OSQ[:, 2 * b:2 * b + 2, :].rearrange("p c t -> p (c t)"), bank[3 + b][:, :], ACT.Ln,
                                    scale=1.0 / (2 * HD), bias=cst("eps")))
                    own.wait()
                    do(OSQ[:, :, :], OSQ[:, :, :], ACT.Exp, scale=-0.5).then_inc(act_mid["crms"], 1)
                    act.wait_ge(dve_mid["crms"], n_of("crms", l, 1))
                    do(oh[:, 2 * BT:3 * BT, :], OC[:, :, :], ACT.Copy).then_inc(act_["crms"], 1)
                elif kind == "gsig":
                    act.wait_ge(*n_out(l, OUT_OF[DENSE.index(("G", KT * c + KT - 1))][0]))
                    do(unit(2 * c, 2), unit(2 * c, 2), ACT.Sigmoid).then_inc(gates_ready, 1)
                    if c in (0, 2):
                        act.preload_act_table_set("natural_log_exp_and_others")

            def conv(l, t, u, which, col, reuse):
                act.wait_ge(up_scaled, l * 2 * FT + 2 * t + (which + 1))
                if reuse:
                    act.wait_ge(prod_l, l * FT + t + (-1))
                k = 2 * (u % 2) + which
                do(CV[:, k, :], UM[:, k, :], ACT.Identity, scale=tap(col, 2), bias=tap(col, 3)).then_inc(tap2, 1)

            def silu(l, t, u):
                act.wait_ge(conv_done, l * 2 * FT + 2 * t + 1)
                g = CV[:, 2 * (u % 2), :]
                do(g, g, ACT.Silu).then_inc(silu_done, 1)

            def product(l, t, u):
                act.wait_ge(prod_done, l * FT + t + 1)
                do(oh[:, u % 2, :], CV[:, 2 * (u % 2), :], ACT.Copy).then_inc(prod_h, 1)

            for m in range(AHEAD):
                split(m, m, None, 16)
            act.wait_ge(const_in, 32)
            with act.Fori(0, DEPTH) as l:
                own.base, own.n = l * ACT_OWN["layer"], 0
                act.wait_ge(mix_in_s, 16 * l + 16)
                for s in STEPS:
                    step(l, s)
                act.wait_ge(ffn_in_s, 16 * l + 16)
                for t in range(2):
                    for which in range(2):
                        ahead(l, FFN0 + 2 * t + which)
                        if t == which == 0:
                            norm(2 * l + 1)
                            act.preload_act_table(ACT.Silu)
                    for which in range(2):
                        conv(l, t, t, which, 8 + 4 * (2 * t + which), False)
                    silu(l, t, t)
                    if t:
                        ahead(l, FFN0 + 4)
                    product(l, t, t)
                with act.Fori(0, FTURNS) as i:
                    for u in range(FU):
                        t = FU * i + (u + 2)
                        o = FFN0 + 5 + 3 * u
                        for which in range(2):
                            ahead_in(split, l, i, o + which)
                        for which in range(2):
                            conv(l, t, u, which, 8 * FU * i + (8 + 8 * (u + 2) + 4 * which), True)
                        silu(l, t, u)
                        ahead_in(split, l, i, o + 2)
                        product(l, t, u)
                ahead(l, SLABS - 1)
                assert own.n == ACT_OWN["layer"], ("act", own.n)
            own.base, own.n = DEPTH * ACT_OWN["layer"], 0
            squares(lambda b: act.wait_ge(x_ready, 4 * DEPTH + b + 1))
            act.preload_act_table_set("natural_log_exp_and_others")
            norm(2 * DEPTH)

        @block.vector
        def _(dve):
            own = Own(dve, dve_own_s, DVE_OWN)
            tt = dve.tensor_tensor
            stt = dve.scalar_tensor_tensor

            def bc(ap, n, w):
                return ap.unsqueeze(2).broadcast_to([P, n, w])

            def rep(ap, n):
                return ap.unsqueeze(1).broadcast_to([P, n, ap.shape[1]])

            def split(m, s, used, landed):
                if used is not None:
                    dve.wait_ge(slab_done, used)
                dve.wait_ge(hi_done, m + 1)
                tt(lo[:, s, :], raw[:, s, :], hi[:, s, :].bitcast(F32), ALU.subtract).then_inc(lo_done, 1)

            def ahead(l, n):
                split(l * SLABS + (n + AHEAD), (n + AHEAD) % RING, l * SLABS + n if n else None, None)

            def add_squares(n):
                dve.wait_ge(square_done, 4 * n + 4)
                own.mark(tt(XSQ[:, 0:4, :], XSQ[:, 0:4, :], XSQ[:, 4:8, :], ALU.add))
                own.wait()
                tt(XSQ[:, 0:2, :], XSQ[:, 0:2, :], XSQ[:, 2:4, :], ALU.add).then_inc(squared, 1)

            def lo_merged(l, cp):
                pair = slice(2 * cp, 2 * cp + 2)
                dve.wait_ge(merged_h, l * (KT // 2) + cp + 1)
                tt(ol[:, pair, :], MG[:, pair, :], oh[:, pair, :].bitcast(F32), ALU.subtract).then_inc(merged_l, 1)

            def mix_before(l, j):
                dst = a_tile(j)
                dve.wait_ge(mixed_now, l * A_SLABS + j + 1)
                stt(dst[:, 1:T], TMP[:, j % 2, 0:T - 1], par("mu", j), dst[:, 1:T], ALU.mult, ALU.add)\
                    .then_inc(mixed, 1)

            def rotate(l, n):
                kind, c = DENSE[n]
                dst, i = (qc if kind == "Cq" else kc)[:, c, :], n - DENSE.index(("Cq", 0))
                partner = bank[OUT_OF[n][0] % 3][:, T:2 * T]
                dve.wait_ge(rope_mm, l * 2 * BT + i + 1)
                own.mark(tt(dst, dst, cst("cos"), ALU.mult))
                own.mark(tt(partner, partner, cst("sin"), ALU.mult))
                own.wait()
                tt(dst, dst, partner, ALU.add).then_inc(emptied["dve"], 1)

            def empty(l, n):
                kind, b = DENSE[n][0], bank[OUT_OF[n][0] % 3]
                if n == A_SLABS:
                    mix_before(l, A_SLABS - 1)
                if DENSE[n] == ("Cv", 3):
                    rotate(l, DENSE.index(("Ck", 3)))
                elif DENSE[n - 1][0] in ("Cq", "Ck"):
                    rotate(l, n - 1)
                if kind not in ("Bv", "Cv"):
                    dve.wait_ge(slab_done, l * SLABS + n + 1)
                if kind == "A":
                    j = DENSE[n][1]
                    if j == 0:
                        dve.wait_ge(rms_inv, 2 * l + 1)
                    if j >= 2:
                        dve.wait_ge(mixed, l * A_SLABS + j - 1)
                    tt(TMP[:, j % 2, :], b[:, 0:T], rs[:, 0:T], ALU.mult).then_inc(emptied["dve"], 1)
                    if j:
                        mix_before(l, j - 1)
                elif kind in ("Bq", "Bk"):
                    if n == A_SLABS:
                        dve.wait_ge(mixed, l * A_SLABS + A_SLABS)
                    stt((qb if kind == "Bq" else kb)[:, DENSE[n][1], :], b[:, 0:T],
                        HD ** -0.5 if kind == "Bq" else 1.0, rs[:, 0:T], ALU.mult, ALU.mult).then_inc(emptied["dve"], 1)
                elif kind in ("Cq", "Ck"):
                    tt((qc if kind == "Cq" else kc)[:, DENSE[n][1], :], b[:, 0:T], rs[:, 0:T], ALU.mult)\
                        .then_inc(rope_raw, 1)
                elif kind == "G":
                    g, c = divmod(DENSE[n][1], KT)
                    tt(GATE[:, g, c, :], b[:, 0:T], rs[:, 0:T], ALU.mult).then_inc(emptied["dve"], 1)
                elif kind == "BR":
                    g, cp = DENSE[n][1:]
                    pair = slice(2 * cp, 2 * cp + 2)
                    out = b[:, :].rearrange("p (c t) -> p c t", t=T)
                    if cp == 0:
                        dve.wait_ge(gates_ready, 3 * l + g + 1)
                    if g == 0:
                        tt(MG[:, pair, :], GATE[:, g, pair, :], out, ALU.mult).then_inc(emptied["dve"], 1)
                    else:
                        i = ADDS.index(n)
                        tmp = BTMP[:, i % 2, :].rearrange("p (c t) -> p c t", t=T)
                        if i >= 2:
                            dve.wait_ge(merged, l * len(ADDS) + i - 1)
                        tt(tmp, GATE[:, g, pair, :], out, ALU.mult).then_inc(emptied["dve"], 1)
                        dve.wait_ge(*n_out(l, OUT_OF[n][0]))
                        tt(MG[:, pair, :], MG[:, pair, :], tmp, ALU.add).then_inc(merged, 1)
                        if g == 2 and cp:
                            lo_merged(l, cp - 1)
                        if g == 2 and cp == KT // 2 - 1:
                            lo_merged(l, cp)
                elif kind == "O":
                    c = DENSE[n][1]
                    tt(x[:, c, :], x[:, c, :], b[:, 0:T], ALU.add).then_inc(emptied["dve"], 1)

            def step(l, s):
                kind = s[0]
                c = s[1] if len(s) > 1 else 0
                j = c % 2
                if kind == "D":
                    ahead(l, s[1])
                elif kind == "E":
                    empty(l, s[1])
                elif kind == "xs":
                    for t in range(KT):
                        dve.wait_ge(split_h, l * 2 * KT + KT * c + t + 1)
                        stt(hl[:, t, :], x[:, t, :], pf[:, t:t + 1] if c else par("g", t),
                            hh[:, t, :].bitcast(F32), ALU.mult, ALU.subtract).then_inc(split_l, 1)
                    add_squares(2 * l + c)
                elif kind == "lam":
                    dve.tensor_scalar(omu[:, 0:14], par("mu", 0, 14), -1.0, 1.0, ALU.mult, ALU.add)
                    dve.tensor_scalar(omu[:, 14:18], par("k_a", 0, 4), -1.0, 1.0, ALU.mult, ALU.add)
                    tt(omu[:, 18:19], par("subln"), par("omli"), ALU.mult)
                    lv = par("lam", 0, 4).rearrange("p (a b) -> p a b", b=2)
                    tt(small[:, 0:2], lv[:, :, 0], lv[:, :, 1], ALU.mult).then_inc(dve_mid["lam"], 1)
                    dve.wait_ge(act_["lam"], n_of("lam", l, 1))
                    stt(small[:, 4:5], small[:, 3:4], small[:, 2:3], par("li"), ALU.subtract, ALU.subtract)\
                        .then_inc(dve_["lam"], 1)
                elif kind == "upg":
                    dve.wait_ge(pe_["upg"], n_of("upg", l, 1))
                    dve.wait_ge(act_["up"], n_of("up", l, 1))
                    own.mark(dve.memset(PP[:, :, 0:1], 0.0))
                    e = unit(6).rearrange("p (n t) -> p n t", t=C)
                    for n in range(8):
                        ins = dve.tensor_tensor_scan(PP[:, n, 1:C + 1], e[:, n, :], e[:, n, :], 0.0, ALU.add,
                                                     ALU.bypass)
                    own.mark(ins)
                    own.wait()
                    own.mark(dve.tensor_copy(small[:, 8:16], PP[:, :, C // 2]))
                    own.wait()
                    tt(PP, PP, bc(small[:, 8:16], 8, C + 1), ALU.subtract).then_inc(dve_["upg"], 1)
                elif kind == "kk":
                    dve.wait_ge(pe_["kk"], n_of("kk", l, 1))
                    for b in range(2):
                        ins = dve.tensor_scalar(unit(9)[:, b * 512:(b + 1) * 512], bank[5 + b][:, :], 1e-24, None, ALU.max)
                    ins.then_inc(dve_mid["kk"], 1)
                    dve.wait_ge(act_["kk"], n_of("kk", l, 1))
                    tt(unit(4), unit(4), unit(9), ALU.mult).then_inc(dve_["kk"], 1)
                elif kind == "prepa":
                    dve.wait_ge(act_mid["kk"], n_of("kk", l, 1))
                    own.mark(tt(unit(1), unit(1), unit(8), ALU.mult))
                    dve.wait_ge(dve_["kk"], n_of("kk", l, 1))
                    own.mark(tt(unit(5), unit(4), unit(5), ALU.mult))
                    pend = PP.rearrange("p (c h) t -> p c h t", h=2)[:, :, 0, C]
                    tt(small[:, 24:28], pend, small[:, 16:24].rearrange("p (c h) -> p c h", h=2)[:, :, 1], ALU.mult)
                    own.wait()
                    tt(unit(5), unit(5), unit(7), ALU.mult).then_inc(dve_["prepa"], 1)
                elif kind == "prepb":
                    tt(unit(9), unit(0), unit(1), ALU.mult).then_inc(dve_mid["prepb"], 1)
                    dve.wait_ge(dve_mid["prepb"], n_of("prepb", l, 1))
                    dve.wait_ge(dve_["prepa"], n_of("prepa", l, 1))
                    tt(unit(1), unit(1), unit(7), ALU.mult).then_inc(dve_["prepb"], 1)
                elif kind == "bon":
                    dve.wait_ge(pe_["bon"], n_of("bon", l, 1))
                    ar = unit(8, 2).rearrange("p (n a t) -> p n a t", a=2, t=C)
                    tt(ar[:, :, 1, :], unit(0).rearrange("p (n t) -> p n t", t=C), PP[:, :, 1:C + 1],
                       ALU.mult)
                    tt(ar[:, :, 0, :], unit(4).rearrange("p (n t) -> p n t", t=C), PP[:, :, 0:C], ALU.mult)\
                        .then_inc(dve_mid["bon"], 1)
                    dve.wait_ge(dve_mid["bon"], n_of("bon", l, 1))
                    dve.wait_ge(mixed, l * A_SLABS + A_SLABS)
                    for b in range(2):
                        cols = slice(b * 512, (b + 1) * 512)
                        ins = tt(unit(0)[:, cols], bank[6 + b][:, :], unit(2)[:, cols], ALU.mult)
                    ins.then_inc(dve_["bon"], 1)
                elif kind == "mat":
                    what, b0 = s[2], 3 + 2 * (ORD[s] % 2)
                    dve.wait_ge(pe_["mat"], n_of("mat", l, ORD[s] + 1))
                    if what == "abt":
                        for b in range(2):
                            ins = tt(M1[:, j, 2 * b:2 * b + 2, :],
                                     bank[b0 + b][:, 0:2 * P].rearrange("p (i n) -> p i n", i=2),
                                     rep(mask("level1"), 2), ALU.mult)
                        own.mark(ins)
                        dve.wait_ge(dve_["mat"], n_of("mat", l, ORD[s]))
                        own.mark(tt(Y[:, j], ABT[:, j, :, 0:C], rep(mask("levelT"), 4), ALU.mult))
                        own.wait(own.n - 1)
                        tt(X[:, j], rep(cst("ident"), 4), M1[:, j], ALU.subtract)
                        own.wait()
                        tt(Y[:, j], rep(cst("ident"), 4), Y[:, j], ALU.subtract).then_inc(dve_["mat"], 1)
                    else:
                        a, _ = CB["maskS"]
                        both = cb[:, a:a + 2 * P]
                        for b in range(2):
                            ins = tt((ABT if what == "ab" else KBT)[:, j, 2 * b:2 * b + 2, :],
                                     bank[b0 + b][:, :].rearrange("p (i n) -> p i n", i=2), rep(both, 2), ALU.mult)
                        ins.then_inc(dve_["mat"], 1)
                elif kind == "m1":
                    dve.wait_ge(pe_["m1"], n_of("m1", l, ORD[s] + 1))
                    tt(M1[:, j], bank[3][:, :].rearrange("p (i n) -> p i n", i=4), rep(mask(f"level{s[2]}"), 4),
                       ALU.mult).then_inc(dve_["m1"], 1)
                elif kind == "dxy":
                    dve.wait_ge(pe_["dxy"], n_of("dxy", l, ORD[s] + 1))
                    for dst, b in ((X, 4), (Y, 5)):
                        if s[2] < LEVELS[-1] or dst is Y:
                            ins = tt(dst[:, j], dst[:, j], bank[b + 2 * j][:, :].rearrange("p (i n) -> p i n", i=4),
                                     ALU.subtract)
                    ins.then_inc(dve_["dxy"], 1)
                elif kind in ("rhs0", "rhs1"):
                    dve.wait_ge(pe_[kind], n_of(kind, l, c + 1))
                    dve.tensor_copy(RHS[:, j, :].rearrange("p (h n) -> p h n", h=2), banks(3)[:, :, 0:HD]).then_inc(dve_[kind], 1)
                elif kind == "s1":
                    dve.wait_ge(pe_["s1"], n_of("s1", l, c + 1))
                    for hp in range(2):
                        rows, cols = slice(hp * HD, (hp + 1) * HD), slice(hp * HD, (hp + 1) * HD)
                        ins = dve.tensor_scalar(s0[rows, c, :], bank[7][rows, cols], small[rows, 24 + c:25 + c], None,
                                                ALU.mult)
                    ins.then_inc(dve_["s1"], 1)
                elif kind == "gn1":
                    dve.wait_ge(pe_["gn1"], n_of("gn1", l, 1))
                    for b in range(2):
                        cols = slice(b * 512, (b + 1) * 512)
                        ins = stt(unit(4)[:, cols], bank[5 + b][:, :], -1.0 / HD, unit(4)[:, cols], ALU.mult, ALU.add)
                    ins.then_inc(dve_["gn1"], 1)
                elif kind == "gn2":
                    dve.wait_ge(act_mid["gn2"], 2 * l + 1)
                    tt(unit(4), unit(4), unit(6), ALU.mult).then_inc(dve_mid["gn2"], 1)
                    dve.wait_ge(act_mid["gn2"], 2 * l + 2)
                    own.mark(tt(unit(4), unit(4), unit(0), ALU.add))
                    own.wait()
                    tt(unit(4), unit(4), unit(3), ALU.mult).then_inc(dve_mid["gn2"], 1)
                    dve.wait_ge(act_["gn2"], n_of("gn2", l, 1))
                    tt(ol[:, 0:BT, :], OT, oh[:, 0:BT, :].bitcast(F32), ALU.subtract).then_inc(dve_["gn2"], 1)
                elif kind == "bz":
                    z = bank[3 + j][:, 0:T + P]
                    diag = SP[:, j, :].rearrange("p (k n) -> p k n", n=P)[:, 0:3:2, :]
                    dve.wait_ge(act_["bz"], n_of("bz", l, c + 1))
                    own.mark(stt(SP[:, j, :], z, 0.0, W1[:, j, :], ALU.max, ALU.add))
                    own.wait()
                    tt(diag, diag, rep(mask("maskS"), 2), ALU.mult).then_inc(dve_["bz"], 1)
                elif kind == "btri":
                    diag = AB[:, j, :].rearrange("p (k n) -> p k n", n=P)[:, 0:3:2, :]
                    dve.wait_ge(act_["btri"], n_of("btri", l, c + 1))
                    stt(diag, diag, 3e38, rep(mask("maskS"), 2), ALU.min, ALU.mult).then_inc(dve_["btri"], 1)
                elif kind == "bav":
                    if c % 2:
                        dve.wait_ge(act_["bav"], l * BT + c // 2 + 1)
                        tt(ol[:, BT + c // 2, :], bank[5 + (c // 2) % 2][:, 0:T], oh[:, BT + c // 2, :].bitcast(F32),
                           ALU.subtract).then_inc(dve_["bav"], 1)
                elif kind == "cs":
                    n, keys = ORD[s], P * (s[2] + 1)
                    f = 28 + 12 * (n % 2)
                    dve.wait_ge(pe_["cs"], n_of("cs", l, n + 1))
                    own.mark(dve.tensor_reduce(small[:, f:f + 2],
                                               banks(3 + 2 * (n % 2))[:, :, 0:keys],
                                               AX.X, ALU.max))
                    own.wait()
                    dve.tensor_scalar(small[:, f + 2:f + 4], small[:, f:f + 2], -HD ** -0.5, None, ALU.mult)\
                        .then_inc(dve_mid["cs"], 1)
                    dve.wait_ge(act_["cs"], n_of("cs", l, n + 1))
                    own.mark(dve.reciprocal(small[:, f + 6:f + 8], small[:, f + 4:f + 6]))
                    own.wait()
                    dve.wait_ge(dve_["lam"], n_of("lam", l, 1))
                    own.mark(tt(small[:, f + 8:f + 9], small[:, f + 7:f + 8], small[:, 4:5], ALU.mult))
                    a, b = PC[:, n % 2, 0, 0:keys], PC[:, n % 2, 1, 0:keys]
                    own.mark(dve.tensor_scalar(a, a, small[:, f + 6:f + 7], None, ALU.mult))
                    own.wait()
                    stt(a, b, small[:, f + 8:f + 9], a, ALU.mult, ALU.add).then_inc(dve_["cs"], 1)
                elif kind == "crms":
                    dve.wait_ge(act_mid["crms"], n_of("crms", l, 1))
                    dve.wait_ge(dve_mid["lam"], n_of("lam", l, 1))
                    stt(OC[:, :, :], OC[:, :, :], omu[:, 18:19], OSQ[:, :, :], ALU.mult, ALU.mult)\
                        .then_inc(dve_mid["crms"], 1)
                    dve.wait_ge(act_["crms"], n_of("crms", l, 1))
                    tt(ol[:, 2 * BT:3 * BT, :], OC[:, :, :], oh[:, 2 * BT:3 * BT, :].bitcast(F32), ALU.subtract)\
                        .then_inc(dve_["crms"], 1)

            def scale_up(l, t, u, which, slab):
                k = 2 * (u % 2) + which
                dve.wait_ge(slab_done, slab + 1)
                tt(UM[:, k, :], bank[k][:, 0:T], rs[:, 0:T], ALU.mult).then_inc(up_scaled, 1)

            def conv(l, t, u, which, col):
                k = 2 * (u % 2) + which
                dve.wait_ge(tap2, l * 2 * FT + 2 * t + (which + 1))
                own.mark(stt(CV[:, k, 1:T], UM[:, k, 0:T - 1], tap(col, 1), CV[:, k, 1:T], ALU.mult, ALU.add))
                own.wait()
                stt(CV[:, k, 2:T], UM[:, k, 0:T - 2], tap(col, 0), CV[:, k, 2:T], ALU.mult, ALU.add)\
                    .then_inc(conv_done, 1)

            def product(l, t, u):
                g, v = CV[:, 2 * (u % 2), :], CV[:, 2 * (u % 2) + 1, :]
                dve.wait_ge(silu_done, l * FT + t + 1)
                dve.wait_ge(conv_done, l * 2 * FT + 2 * t + 2)
                tt(g, g, v, ALU.mult).then_inc(prod_done, 1)

            def product_lo(l, t, u):
                dve.wait_ge(prod_h, l * FT + t + 1)
                tt(ol[:, u % 2, :], CV[:, 2 * (u % 2), :], oh[:, u % 2, :].bitcast(F32), ALU.subtract)\
                    .then_inc(prod_l, 1)

            for m in range(AHEAD):
                split(m, m, None, None)
            dve.wait_ge(const_in, 32)
            dve.wait_ge(x_loaded, 32)
            dve.memset(small[:, 63:64], 0.0).then_inc(x_ready, 4)
            with dve.Fori(0, DEPTH) as l:
                own.base, own.n = l * DVE_OWN["layer"], 0
                dve.wait_ge(mix_in_s, 16 * l + 16)
                for s in STEPS:
                    step(l, s)
                for t in range(2):
                    for which in range(2):
                        n = FFN0 + 2 * t + which
                        ahead(l, n)
                        if n == FFN0:
                            dve.wait_ge(rms_inv, 2 * l + 2)
                        scale_up(l, t, t, which, l * SLABS + n)
                    for which in range(2):
                        conv(l, t, t, which, 8 + 4 * (2 * t + which))
                    product(l, t, t)
                    if t:
                        ahead(l, FFN0 + 4)
                    product_lo(l, t, t)
                before = own.n
                with dve.Fori(0, FTURNS) as i:
                    own.base = l * DVE_OWN["layer"] + i * DVE_OWN["turn"]
                    for u in range(FU):
                        t = FU * i + (u + 2)
                        o = FFN0 + 5 + 3 * u
                        for which in range(2):
                            ahead_in(lambda m, s, used, landed: split(used + AHEAD, s, used, None), l, i, o + which)
                            scale_up(l, t, u, which, l * SLABS + 3 * FU * i + (o + which))
                        for which in range(2):
                            conv(l, t, u, which, 8 * FU * i + (8 + 8 * (u + 2) + 4 * which))
                        product(l, t, u)
                        ahead_in(lambda m, s, used, landed: split(used + AHEAD, s, used, None), l, i, o + 2)
                        product_lo(l, t, u)
                assert own.n - before == DVE_OWN["turn"], ("dve turn", own.n - before)
                own.base, own.n = l * DVE_OWN["layer"], before + FTURNS * DVE_OWN["turn"]
                ahead(l, SLABS - 1)
                dve.wait_ge(slab_done, l * SLABS + SLABS)
                for b in range(4):
                    pair = x[:, 2 * b:2 * b + 2, :].rearrange("p c t -> p (c t)")
                    tt(pair, pair, bank[4 + b][:, :], ALU.add).then_inc(x_ready, 1)
                assert own.n == DVE_OWN["layer"], ("dve", own.n)
            own.base, own.n = DEPTH * DVE_OWN["layer"], 0
            add_squares(2 * DEPTH)
            dve.wait_ge(rms_inv, 2 * DEPTH + 1)
            for c in range(KT):
                stt(HF[:, c, :], x[:, c, :], fin[:, c:c + 1], rs[:, 0:T], ALU.mult, ALU.mult).then_inc(y_ready, 1)
        return nc


def constants():
    import numpy as np

    cf, cb = np.zeros((P, NCF), np.float32), np.zeros((P, NCB), np.float32)

    def put(dst, where, name, a):
        dst[:a.shape[0], where[name][0]:where[name][0] + where[name][1]] = a
    i = np.arange(P)
    row, col = i[:, None], i[None, :]
    put(cf, CF, "ident", np.eye(P))
    put(cf, CF, "ones", np.ones((P, P)))
    put(cf, CF, "bones", row // HD == col // HD)
    rope = np.zeros((P, P))
    half = HD // 8
    for m in range(2):
        for d in range(half):
            rope[m * HD + d + half, m * HD + d] = -1.0
            rope[m * HD + d, m * HD + d + half] = 1.0
    put(cf, CF, "rope", rope)
    put(cf, CF, "triN", -(row >= col).astype(np.float32))
    put(cf, CF, "onesN", -np.ones((P, P)))
    inv_freq = np.float32(500000.0) ** (-np.arange(0, 2 * half, 2, dtype=np.float32) / np.float32(2 * half))
    ang = inv_freq[:, None].astype(np.float32) * np.arange(T, dtype=np.float32)[None, :]
    cos, sin = np.ones((P, T)), np.zeros((P, T))
    for m in range(2):
        for o in (0, half):
            cos[m * HD + o:m * HD + o + half] = np.cos(ang)
            sin[m * HD + o:m * HD + o + half] = np.sin(ang)
    put(cf, CF, "cos", cos)
    put(cf, CF, "sin", sin)
    put(cf, CF, "rowL", np.broadcast_to((i < 64).astype(np.float32)[None, :], (P, P)))
    put(cf, CF, "rowR", np.full((P, 64), -1e30))
    for name, v in (("eps", 1e-6), ("gneps", 64e-5), ("kkb", 10 * np.log(2.0)), ("one", 1.0)):
        put(cf, CF, name, np.full((P, 1), v))
    put(cb, CB, "maskS", row < col)
    put(cb, CB, "maskI", row <= col)

    def level(t, s, z):
        return (t // (2 * z) == s // (2 * z)) & (t // z % 2 == 1) & (s // z % 2 == 0)
    put(cb, CB, "levelT", level(col, row, 1))
    for z in LEVELS:
        put(cb, CB, f"level{z}", level(row, col, z))
    return cf, cb.astype(np.float16)


def lay_out(a):
    import numpy as np

    L = a["w_in"].shape[0]
    f = {k: np.asarray(v) for k, v in a.items()}

    def cols_major(w, cols):
        n, k, m = w.shape
        return w.reshape(n, k // P, P, m // cols, cols).transpose(0, 3, 2, 1, 4)

    w = f["w_in"]
    a0, b0, c0, g0 = 0, 1792, 1792 + 1536, 1792 + 3072
    lora = w[:, :, 1536:1792]

    def square(x):
        return cols_major(x, P).reshape(L, -1, P, SLAB)

    def values(x):
        return x.reshape(L, 4, 2, P, BW).transpose(0, 1, 3, 2, 4).reshape(L, 4, P, SLAB)
    parts = [square(lora), square(w[:, :, 512:1024]), square(w[:, :, 0:512]), square(w[:, :, 1024:1536]),
             square(w[:, :, b0:b0 + 1024]), values(w[:, :, b0 + 1024:b0 + 1536]),
             square(w[:, :, c0:c0 + 1024]), values(w[:, :, c0 + 1024:c0 + 1536]), None]
    gates = square(w[:, :, g0:])
    br = [cols_major(f[n], 2 * P).reshape(L, KT // 2, P, SLAB) for n in ("w_branch_a", "w_branch_b", "w_branch_c")]
    parts[-1] = np.stack([gates[:, k[1]] if k[0] == "G" else br[k[1]][:, k[2]] for k in DENSE if k[0] in ("G", "BR")],
                         axis=1)
    parts += [square(f["w_out"])]
    up = square(f["ffn_w_up"]).reshape(L, 2, FT, P, SLAB)
    down = f["ffn_w_down"].reshape(L, FT, P, SLAB)
    ffn = [up[:, 0, 0], up[:, 1, 0]]
    for t in range(1, FT):
        ffn += [up[:, 0, t], up[:, 1, t], down[:, t - 1]]
    ffn.append(down[:, FT - 1])
    parts.append(np.stack(ffn, axis=1))
    stream = np.concatenate(parts, axis=1).reshape(L * SLABS, P, SLAB)
    stream = np.concatenate([stream, np.zeros((RING, P, SLAB), np.float32)])

    def vec(x):
        return x.reshape(L, -1, P).transpose(0, 2, 1)
    mu = f["rwkv_mu"]
    mu = np.concatenate([mu[:, 1536:1792], mu[:, 512:1024], mu[:, 0:512], mu[:, 1024:1536]], axis=1)
    lam = np.zeros((L, P, 4), np.float32)
    lam[:, 0:64] = f["diff_lambda"].transpose(0, 2, 1)
    li = np.array([0.8 - 0.6 * float(np.exp(-0.3 * i)) for i in range(L)])
    li2 = np.stack([np.broadcast_to(v[:, None], (L, P)) for v in (li, 1.0 - li)], axis=2).astype(np.float32)
    mix = np.concatenate([vec(f["norm_mix_g"]), vec(mu), vec(f["rwkv_w0"]), vec(f["rwkv_a0"]), vec(f["rwkv_k_k"]),
                          vec(f["rwkv_k_a"]), vec(f["rwkv_r_k"].reshape(L, -1)), vec(f["rwkv_ln_w"]),
                          vec(f["rwkv_ln_b"]), vec(f["diff_subln_g"]), lam, li2,
                          np.concatenate([f["rwkv_w_up"], f["rwkv_a_up"]], axis=1), f["rwkv_g_up"],
                          np.zeros((L, P, NPM - _o), np.float32)], axis=2)
    cw = np.concatenate([f["ffn_conv_w"], f["ffn_conv_b"][:, None]], axis=1)
    cw = cw.reshape(L, 4, 2, FT, P).transpose(0, 4, 3, 2, 1).reshape(L, P, 8 * FT)
    ffn_par = np.concatenate([vec(f["norm_ffn_g"]), cw], axis=2)
    mix, ffn_par = (np.concatenate([v, np.zeros_like(v[:1])]) for v in (mix, ffn_par))
    cf, cb = constants()
    c = np.ascontiguousarray
    return {"x_t": c(f["x"][0].T.reshape(KT, P, T).transpose(1, 0, 2)), "w_stream": c(stream), "mix_par": c(mix),
            "ffn_par": c(ffn_par), "final_g": c(f["norm_final_g"].reshape(KT, P).T), "const_f": c(cf),
            "const_b": c(cb)}


_INS = ["x_t", "w_stream", "mix_par", "ffn_par", "final_g", "const_f", "const_b"]


def kernel(**inputs):
    import numpy as np
    import concourse.bacc as bacc
    from concourse.bass_utils import run_bass_kernel_spmd

    nc = bacc.Bacc("TRN2", target_bir_lowering=False, num_devices=1)
    arrays = lay_out(inputs)
    args = [nc.dram_tensor(n, arrays[n].shape, mybir.dt.from_np(arrays[n].dtype), kind="ExternalInput").ap()
            for n in _INS]
    y = nc.dram_tensor("y_t", (P, KT, T), F32, kind="ExternalOutput").ap()
    hybrid_blocks(nc, *args, y)
    r = run_bass_kernel_spmd(nc, [arrays], core_ids=[0])
    out = r.results[0]["y_t"]
    return np.ascontiguousarray(out.transpose(2, 1, 0).reshape(1, T, D))
```

```python
from contextlib import ExitStack

import concourse.bass as bass
from concourse import mybir

F32 = mybir.dt.float32
F32R = mybir.dt.float32r
F16 = mybir.dt.float16
ALU = mybir.AluOpType
ACT = mybir.ActivationFunctionType
AX = mybir.AxisListType

P = 128
T = 256
D = 1024
KT = D // P
C = 128
HD = 64
AH = 8
CH = 4
BW = 512
BT = BW // P
FT = 2816 // P
SLAB = 1024
RING = 4
AHEAD = 3
DECAY_SCALE = 0.6065306597126334

A_SLABS = 14
DENSE = ([("A", j) for j in range(A_SLABS)]
         + [("Bq", c) for c in range(BT)] + [("Bk", c) for c in range(BT)] + [("Bv", i) for i in range(4)]
         + [("Cq", c) for c in range(BT)] + [("Ck", c) for c in range(BT)] + [("Cv", i) for i in range(4)]
         + [("G", g) for g in range(2 * KT)]
         + [s for i in range(4) for s in (("G", 2 * KT + 2 * i), ("BR", 0, i), ("G", 2 * KT + 2 * i + 1))]
         + [("BR", *bc) for bc in ((1, 0), (1, 1), (2, 0), (1, 2), (2, 1), (1, 3), (2, 2), (2, 3))]
         + [("O", c) for c in range(KT)])
FFN0 = len(DENSE)
SLABS = FFN0 + 3 * FT
FU = 4
FTURNS = (FT - 2) // FU

OUTS, OUT_OF = [], {}
for _n, _s in enumerate(DENSE):
    if _s[0] in ("Bv", "Cv"):
        if _s[1] == 0:
            OUT_OF[_n] = [len(OUTS), len(OUTS) + 1]
            OUTS += ["act", "act"]
        else:
            OUT_OF[_n] = OUT_OF[_n - 1]
    else:
        OUT_OF[_n] = [len(OUTS)]
        OUTS.append("dve")
EMPTIED = {m: OUTS[:m + 1].count(OUTS[m]) for m in range(len(OUTS))}


def mixing_steps():
    at = {k: n for n, k in reversed(list(enumerate(DENSE)))}
    g0 = at[("G", 0)]

    def woven(steps, slabs):
        out, done = [], 0
        for i, s in enumerate(steps):
            out.append(s)
            while done < len(slabs) and done * len(steps) < (i + 1) * len(slabs):
                out.append(("D", slabs[done]))
                done += 1
        return out + [("D", n) for n in slabs[done:]]

    def dense(a, b):
        return [("D", n) for n in range(a, b)]

    steps = [("xs", 0)] + dense(0, 2) + [("norm", 0), ("lam",)] + dense(2, 5) + [("lora",)]
    steps += dense(5, 6) + [("up",)] + dense(6, 7) + [("upg",)] + dense(7, 8) + [("kkq",)] + dense(8, 11)
    steps += [("kk",)] + dense(11, 12) + [("kkn",)] + dense(12, 13) + [("prepa",)] + dense(13, 14) + [("prepb",)]
    steps += dense(14, 15) + [("rk",)] + dense(15, 17) + [("bon",)] + dense(17, 18) + [("natv",)] + dense(18, 19)
    steps += [("natk",)]
    n = 19
    for pair in ((0, 1), (2, 3)):
        for i, s in enumerate([(c, what) for c in pair for what in ("ab", "abt", "akb")]):
            fill = 1 if i in (0, 3) else 0
            steps += dense(n, n + fill) + [("mat",) + s]
            n += fill
        steps += dense(n, n + 1)
        n += 1
        for z in (2, 4, 8, 16, 32, 64):
            steps += [("m1", c, z) for c in pair] + [("dxy", c, z) for c in pair]
            if z == 8:
                steps += dense(n, n + 1)
                n += 1
        for s in ("rhs0", "u0", "s1", "rhs1", "u1", "o"):
            fill = min(g0 - n, 1)
            steps += dense(n, n + fill) + [(s, c) for c in pair]
            n += fill
    steps += dense(n, g0) + [("bz", 0), ("gn1",)] + dense(g0, g0 + 1) + [("bz", 1), ("gn2",)] + dense(g0 + 1, g0 + 2)
    steps += [("btri", 0), ("gn3",)] + dense(g0 + 2, g0 + 3) + [("gn4",)]
    heads = [("bz", 2)]
    for h in range(2, AH + 2):
        heads += [("btri", h - 1)] if h <= AH else []
        heads += [("bz", h)] if 3 <= h < AH else []
        heads += [("bav", h - 2)]
    steps += woven(heads, list(range(g0 + 3, g0 + 2 * KT)))
    maps = []
    cs = [(h, tt) for h in range(CH) for tt in range(2)]
    for i in range(len(cs) + 1):
        maps += [("cs",) + cs[i]] if i < len(cs) else []
        maps += [("cav", cs[i - 2][0])] if i >= 2 and cs[i - 2][1] else []
        maps += [("ct",) + cs[i - 1]] if i else []
    maps += [("cav", CH - 1)]
    last = at[("BR", 1, 0)]
    m = g0 + 2 * KT
    steps += maps[:1] + [("gsig", 0)] + dense(m, m + 2) + [("gsig", 1)]
    steps += woven(maps[1:], list(range(m + 2, last)))
    steps += [("crms",)] + dense(last, last + 2) + [("gsig", 2)]
    steps += dense(last + 2, last + 3) + [("gsig", 3)] + dense(last + 3, FFN0)
    out, late = [], []
    for i, s in enumerate(steps):
        out.append(s)
        ready = [e for e in late if not (e == ("E", 0) and ("norm", 0) not in out)
                 and not (DENSE[e[1]][0] == "G" and ("gn3",) not in out)]
        out += ready
        late = [e for e in late if e not in ready]
        if s[0] == "D" and not (DENSE[s[1]][0] in ("Bv", "Cv") and DENSE[s[1]][1] < 3):
            late.append(("E", s[1]))
    return out + late + [("xs", 1)]


STEPS = mixing_steps()
DVE_STEPS = list(STEPS)
for _i in range(len(STEPS) - 1):
    if STEPS[_i][0] == "D" and STEPS[_i + 1][0] == "E":
        DVE_STEPS[_i], DVE_STEPS[_i + 1] = STEPS[_i + 1], STEPS[_i]
TIMES = {}
ORD = {}
for _s in STEPS:
    ORD[_s] = TIMES.get(_s[0], 0)
    TIMES[_s[0]] = ORD[_s] + 1

_i = DVE_STEPS.index(("E", DENSE.index(("BR", 2, 3))))
_k = DVE_STEPS.index(("D", DENSE.index(("BR", 2, 3))))
DVE_STEPS[_k:_i + 1] = [DVE_STEPS[_i]] + DVE_STEPS[_k:_i]

ACT_STEPS = list(STEPS)
for _i in range(len(STEPS) - 1):
    if (STEPS[_i][0], STEPS[_i + 1][0]) == ("E", "D") and STEPS[_i + 1][1] == STEPS[_i][1] + 1:
        ACT_STEPS[_i], ACT_STEPS[_i + 1] = STEPS[_i + 1], STEPS[_i]

X_STEP = {s: i for i, s in enumerate(s for s in STEPS if s[0] == "dxy" and s[2] < 64)}
X_STEPS = len(X_STEP)

CF = {"ident": (0, 128), "ones": (128, 128), "bones": (256, 128), "rope": (384, 128), "triN": (512, 128),
      "onesN": (640, 128), "cos": (768, 256), "sin": (1024, 256), "rowL": (1280, 128), "rowR": (1408, 64),
      "eps": (1472, 1), "gneps": (1473, 1), "kkb": (1474, 1), "one": (1475, 1), "zero": (1476, 1), "pad": (1477, 1)}
NCF = 1478
LEVELS = (1, 2, 4, 8, 16, 32, 64)
CB = {"maskS": (0, 128), "maskI": (128, 128), "levelT": (256, 128)}
CB.update({f"level{z}": (384 + 128 * i, 128) for i, z in enumerate(LEVELS)})
NCB = 384 + 128 * len(LEVELS)
PM, _o = {}, 0
for _name, _w in (("g", 8), ("mu", 14), ("w0", 4), ("a0", 4), ("k_k", 4), ("k_a", 4), ("r_k", 4), ("ln_w", 4),
                  ("ln_b", 4), ("subln", 1), ("lam", 4), ("li", 1), ("omli", 1), ("wa_up", 512), ("g_up", 512)):
    PM[_name] = (_o, _w)
    _o += _w
NPM = _o + _o % 2
NPF = 8 + 8 * FT
ACT_OWN = {"turn": 0, "layer": 28}
DVE_OWN = {"turn": 8, "layer": 114}


class Own:

    def __init__(self, eng, sem, counts):
        self.eng, self.sem, self.counts = eng, sem, counts
        self.base, self.n = 0, 0

    def mark(self, ins):
        ins.then_inc(self.sem, 1)
        self.n += 1
        return self.n

    def wait(self, n=None):
        self.eng.wait_ge(self.sem, self.base + (self.n if n is None else n))


def hybrid_blocks(nc, x_in, w_in, mix_in, ffn_in, fin_in, cf_in, cb_in, y_out):
    DEPTH = w_in.shape[0] // SLABS
    with ExitStack() as ctx:
        def sb(name, shape, dt=F32):
            return ctx.enter_context(nc.sbuf_tensor("sb_" + name, shape, dt))

        def sem(name):
            return ctx.enter_context(nc.semaphore(name))

        raw = sb("raw", [P, RING, SLAB])
        hi = sb("hi", [P, RING, SLAB], F32R)
        lo = sb("lo", [P, RING, SLAB], F32R)
        x = sb("x", [P, KT, T])
        hh = sb("hh", [P, KT, T], F32R)
        hl = sb("hl", [P, KT, T], F32R)
        oh = sb("oh", [P, 3 * BT, T], F32R)
        ol = sb("ol", [P, 3 * BT, T], F32R)
        rw = sb("rw", [P, 11 * 1024 + 8])
        inv = sb("inv", [P, 7168])
        qb = sb("qb", [P, BT, T])
        kb = sb("kb", [P, BT, T])
        vb = sb("vb", [P, 2, BW])
        qc = sb("qc", [P, BT, T])
        kc = sb("kc", [P, BT, T])
        vc = sb("vc", [P, 2, BW])
        cf = sb("cf", [P, NCF])
        cb = sb("cb", [P, NCB], F16)
        pm = sb("pm", [P, NPM])
        pf = sb("pf", [P, NPF])
        fin = sb("fin", [P, KT])
        omu = sb("omu", [P, 32])
        small = sb("small", [P, 64])
        s0 = sb("s0", [P, BT, HD])
        rs = sb("rs", [P, T + 2])

        def unit(i, n=1):
            return rw[:, i * 1024:(i + n) * 1024]

        def tiles(i, n=1):
            return unit(i, n).rearrange("p (c t) -> p c t", t=T)

        R, K, V, KKt, A_, SG = [tiles(i) for i in (0, 1, 2, 4, 5, 6)]
        AR = unit(8, 2).rearrange("p (c h a t) -> p c h a t", c=BT, h=2, a=2)
        SQ, SB = tiles(8), tiles(9)
        PP = rw[:, 10240:10240 + 8 * (C + 1)].rearrange("p (n t) -> p n t", t=C + 1)
        DD, DG = rw[:, 10240:10496], rw[:, 10496:10752]
        Vn = unit(10).rearrange("p (h c) -> p h c", h=2)
        BKn = unit(7).rearrange("p (a c) -> p a c", a=2)
        RHS = rw[:, 6144:6144 + 256].rearrange("p (c n) -> p c n", c=2)
        NU = rw[:, 6400:6400 + 512].rearrange("p (c h n) -> p c h n", c=2, h=2)
        OT = KKt
        GATE = unit(0, 6).rearrange("p (b c t) -> p b c t", b=3, t=T)
        HF = unit(0, 2).rearrange("p (c t) -> p c t", t=T)
        XSQ = unit(2, 2).rearrange("p (c t) -> p c t", t=T)
        MG = unit(6, 2).rearrange("p (c t) -> p c t", t=T)
        BTMP = unit(8, 2).rearrange("p (b s c t) -> p b s c t", b=2, s=2, t=T)
        TMP = qb[:, 0:2, :]
        UM = unit(8).rearrange("p (s t) -> p s t", s=4)
        CV = unit(9).rearrange("p (s t) -> p s t", s=4)
        ABT = inv[:, 0:2048].rearrange("p (c i n) -> p c i n", c=2, i=4)
        KBT = inv[:, 2048:4096].rearrange("p (c i n) -> p c i n", c=2, i=4)
        X = inv[:, 4096:5120].rearrange("p (c i n) -> p c i n", c=2, i=4)
        Y = inv[:, 5120:6144].rearrange("p (c i n) -> p c i n", c=2, i=4)
        M1 = inv[:, 6144:7168].rearrange("p (c i n) -> p c i n", c=2, i=4)
        W1 = inv[:, 0:768].rearrange("p (s n) -> p s n", s=2)
        SP = inv[:, 768:1536].rearrange("p (s n) -> p s n", s=2)
        AB = inv[:, 1536:2304].rearrange("p (s n) -> p s n", s=2)
        PC = inv[:, 2304:3328].rearrange("p (s m n) -> p s m n", s=2, m=2)
        ATC = inv[:, 3328:4352].rearrange("p (s k t) -> p s k t", s=2, k=2)
        OC = inv[:, 4352:5376].rearrange("p (c t) -> p c t", c=CH)
        OSQ = inv[:, 5376:6400].rearrange("p (c t) -> p c t", c=CH)

        psum = ctx.enter_context(nc.psum_tensor("psum", [P, 8, 512], F32))
        bank = [psum[:, i, :] for i in range(8)]

        def banks(b, n=2):
            return psum[:, b:b + n, :]

        def cst(name):
            a, n = CF[name]
            return cf[:, a:a + n]

        def mask(name):
            a, n = CB[name]
            return cb[:, a:a + n]

        def par(name, i=0, n=1):
            a = PM[name][0]
            return pm[:, a + i:a + i + n]

        raw_in = [sem(f"raw_in{i}") for i in range(RING)]
        hi_done = sem("hi_done")
        lo_done = sem("lo_done")
        slab_done = sem("slab_done")
        emptied = {"act": sem("emptied_act"), "dve": sem("emptied_dve")}
        const_in, x_loaded, fin_loaded = sem("const_in"), sem("x_loaded"), sem("fin_loaded")
        ups_in_s = sem("low_rank_in")
        mix_in_s, ffn_in_s = sem("mix_params_in"), sem("ffn_params_in")
        square_done = sem("square_done")
        squared = sem("squared")
        rms_inv = sem("rms_inv")
        split_h, split_l = sem("split_h"), sem("split_l")
        merged_h, merged_l = sem("merged_h"), sem("merged_l")
        x_ready = sem("x_ready")
        mixed_now = sem("mixed_now")
        mixed = sem("mixed")
        rope_raw, rope_mm = sem("rope_raw"), sem("rope_mm")
        gates_ready = sem("gates_ready")
        merged_b, merged = sem("merged_b"), sem("merged")
        y_ready, y_stored = sem("y_ready"), sem("y_stored")
        up_scaled = sem("up_scaled")
        tap2, conv_done = sem("tap2"), sem("conv_done")
        silu_done, prod_done, prod_h, prod_l = sem("silu_done"), sem("prod_done"), sem("prod_h"), sem("prod_l")
        pe_ = {k: sem("pe_" + k) for k in TIMES
               if k not in ("D", "E", "xs", "gsig", "prepa", "prepb", "rk", "kkn", "kkq", "lora", "gn3", "gn4")}
        act_ = {k: sem("act_" + k) for k in TIMES if k not in ("D", "E", "xs", "norm")}
        dve_ = {k: sem("dve_" + k) for k in TIMES if k not in ("D", "E", "xs", "norm")}
        dve_mid = {k: sem("dve_mid_" + k) for k in ("lam", "prepb", "bon", "cs", "crms")}
        act_mid = {k: sem("act_mid_" + k) for k in ("crms",)}
        x_mm, x_done = sem("x_mm"), sem("x_done")
        pool_own, beta_ready = sem("pool_own"), sem("beta_ready")
        act_own_s, dve_own_s = sem("act_own"), sem("dve_own")
        block = ctx.enter_context(nc.Block())

        def n_of(kind, l, k):
            return l * TIMES[kind] + k

        def n_out(l, m):
            return emptied[OUTS[m]], l * OUTS.count(OUTS[m]) + EMPTIED[m]

        OUT_BV, OUT_CV = OUT_OF[DENSE.index(("Bv", 3))][1], OUT_OF[DENSE.index(("Cv", 3))][1]
        OUT_BK, OUT_CK, OUT_O = (OUT_OF[DENSE.index(k)][0] for k in (("Bk", 3), ("Ck", 3), ("O", 0)))

        def ahead_in(split, l, i, n):
            split(None, (n + AHEAD) % RING, l * SLABS + 3 * FU * i + n,
                  l * (16 * SLABS // RING) + (16 * 3 * FU // RING) * i + 16 * ((n + AHEAD) // RING + 1))

        def tap(col, k):
            return pf[:, bass.ds(col + k, 1)]

        def a_tile(j):
            if j < 2:
                return (DD, DG)[j][:, :]
            return (K, R, V)[(j - 2) // BT][:, (j - 2) % BT, :]

        @block.sync
        def _(sp):
            for b in range(4):
                sp.dma_start(x[:, 2 * b:2 * b + 2, :], x_in[:, 2 * b:2 * b + 2, :]).then_inc(x_loaded, 16)
            for s in range(RING):
                sp.dma_start(raw[:, s], w_in[s]).then_inc(raw_in[s], 16)
                if s == 2:
                    sp.dma_start(cf[:, :], cf_in).then_inc(const_in, 16)
                    sp.dma_start(cb[:, :], cb_in).then_inc(const_in, 16)
            with sp.Fori(1, DEPTH * SLABS // RING + 1) as i:
                for s in range(RING):
                    sp.wait_ge(hi_done, RING * i + (s - RING + 1))
                    sp.wait_ge(lo_done, RING * i + (s - RING + 1))
                    sp.dma_start(raw[:, s], w_in[RING * i + s]).then_inc(raw_in[s], 16)
            for b in range(4):
                sp.wait_ge(y_ready, 2 * b + 2)
                sp.dma_start(y_out[:, 2 * b:2 * b + 2, :], HF[:, 2 * b:2 * b + 2, :]).then_inc(y_stored, 16)
            sp.wait_ge(y_stored, 64)
            sp.wait_ge(ups_in_s, 16 * DEPTH + 16)
            sp.wait_ge(mix_in_s, 16 * DEPTH + 16)
            sp.wait_ge(ffn_in_s, 16 * DEPTH + 16)
            for s in range(RING):
                sp.wait_ge(raw_in[s], 16 * (DEPTH * SLABS // RING + 1))

        @block.gpsimd
        def _(pool):
            pool.dma_start(fin[:, :], fin_in).then_inc(fin_loaded, 16)
            pool.dma_start(pf[:, :], ffn_in[0]).then_inc(ffn_in_s, 16)
            with pool.Fori(0, DEPTH) as l:
                pool.wait_ge(dve_["prepa"], n_of("prepa", l, 1))
                pool.tensor_tensor(unit(5), unit(4), unit(5), ALU.mult).then_inc(pool_own, 1)
                pool.wait_ge(pool_own, l + 1)
                pool.tensor_tensor(unit(5), unit(5), unit(7), ALU.mult).then_inc(beta_ready, 1)
                for cp in range(KT // 2):
                    pair = slice(2 * cp, 2 * cp + 2)
                    pool.wait_ge(*n_out(l, OUT_OF[DENSE.index(("BR", 1, cp))][0]))
                    pool.tensor_tensor(MG[:, pair, :], MG[:, pair, :], BTMP[:, 0, cp % 2], ALU.add)\
                        .then_inc(merged_b, 1)
                pool.wait_ge(conv_done, l * 2 * FT + 2 * FT)
                pool.dma_start(pf[:, :], ffn_in[l + 1]).then_inc(ffn_in_s, 16)

        @block.tensor
        def _(pe):
            def mm(out, lhsT, rhs, start, stop):
                return pe.matmul(out, lhsT, rhs, start=start, stop=stop, skip_group_check=True)

            def after(sig, kind, l, k):
                if k:
                    pe.wait_ge(sig[kind], n_of(kind, l, k))

            def split_mm(out, w, a, start, stop):
                mm(out, w[0], a[0], start, False)
                mm(out, w[0], a[1], False, False)
                return mm(out, w[1], a[0], False, stop)

            def rope(l, n):
                kind, c = DENSE[n]
                pe.wait_ge(rope_raw, l * 2 * BT + (n - DENSE.index(("Cq", 0)) + 1))
                mm(bank[OUT_OF[n][0] % 3][:, T:2 * T], cst("rope"), (qc if kind == "Cq" else kc)[:, c, :],
                   True, True).then_inc(rope_mm, 1)

            def dense(l, n):
                s, kind = n % RING, DENSE[n][0]
                pe.wait_ge(lo_done, l * SLABS + n + 1)
                for m in OUT_OF[n]:
                    if m >= 3 and (n == 0 or m not in OUT_OF[n - 1]):
                        pe.wait_ge(*n_out(l, m - 3))
                if kind == "BR" and DENSE[n][2] == 0:
                    pe.wait_ge(*((dve_["gn4"], n_of("gn4", l, 1)), (dve_["bav"], l * BT + BT),
                                 (dve_["crms"], n_of("crms", l, 1)))[DENSE[n][1]])
                if kind in ("Bv", "Cv"):
                    i = DENSE[n][1]
                    for tt, m in enumerate(OUT_OF[n]):
                        tok = slice(tt * P, (tt + 1) * P)
                        for k2 in range(2):
                            k, cols = 2 * i + k2, slice(k2 * BW, (k2 + 1) * BW)
                            last = split_mm(bank[m % 3][:, :], (hh[:, k, tok], hl[:, k, tok]),
                                            (hi[:, s, cols], lo[:, s, cols]), k == 0, k == KT - 1)
                elif kind == "BR":
                    b, m = DENSE[n][1], OUT_OF[n][0]
                    for u in range(2):
                        for k in range(BT):
                            cols = slice(k * 2 * P + u * P, k * 2 * P + (u + 1) * P)
                            last = split_mm(bank[m % 3][:, u * T:(u + 1) * T], (hi[:, s, cols], lo[:, s, cols]),
                                            (oh[:, b * BT + k, :], ol[:, b * BT + k, :]), u == 0 and k == 0,
                                            k == BT - 1)
                else:
                    m = OUT_OF[n][0]
                    src = (oh, ol) if kind == "O" else (hh, hl)
                    for k in range(KT):
                        if DENSE[n] == ("O", 0) and k % 2 == 0:
                            pe.wait_ge(merged_l, l * (KT // 2) + k // 2 + 1)
                        cols = slice(k * P, (k + 1) * P)
                        last = split_mm(bank[m % 3][:, 0:T], (hi[:, s, cols], lo[:, s, cols]),
                                        (src[0][:, k, :], src[1][:, k, :]), k == 0, k == KT - 1)
                last.then_inc(slab_done, 1)
                if n and DENSE[n - 1][0] in ("Cq", "Ck"):
                    rope(l, n - 1)

            def two_slabs(slab, s0_, tiles):
                pe.wait_ge(lo_done, slab + 2)
                for k in range(KT):
                    pe.wait_ge(split_l, tiles + k + 1)
                    for i in range(2):
                        s, cols = (s0_ + i) % RING, slice(k * P, (k + 1) * P)
                        last = split_mm(bank[i][:, 0:T], (hi[:, s, cols], lo[:, s, cols]),
                                        (hh[:, k, :], hl[:, k, :]), k == 0, k == KT - 1)
                        if k == KT - 1:
                            last.then_inc(slab_done, 1)

            def norm(n):
                pe.wait_ge(squared, n + 1)
                for c in range(2):
                    mm(bank[4][:, 0:T], cst("ones"), XSQ[:, c, :], c == 0, False)
                for c in range(2):
                    for tok in range(2):
                        last = mm(bank[4][:, T + tok:T + tok + 1], XSQ[:, c, tok * P:(tok + 1) * P],
                                  cst("ones")[:, 0:1], False, c == 1)
                last.then_inc(pe_["norm"], 1)

            def step(l, s):
                kind = s[0]
                c = s[1] if len(s) > 1 else 0
                j = c % 2
                if kind == "D" and s[1] == 0:
                    two_slabs(l * SLABS, 0, l * 2 * KT)
                elif kind == "D" and s[1] > 1:
                    dense(l, s[1])
                elif kind == "norm":
                    pe.wait_ge(const_in, 32)
                    norm(2 * l)
                elif kind == "lam":
                    pe.wait_ge(dve_mid["lam"], n_of("lam", l, 1))
                    mm(bank[7][:, 0:2], cst("ones"), small[:, 0:2], True, True).then_inc(pe_["lam"], 1)
                elif kind == "up":
                    pe.wait_ge(ups_in_s, 16 * l + 16)
                    pe.wait_ge(act_["lora"], 2 * l + 1)
                    for half, b0 in ((0, 3), (1, 5)):
                        rows = slice(HD * half, HD * (half + 1))
                        for c in range(BT):
                            last = mm(bank[b0 + c // 2][:, (c % 2) * T:(c % 2 + 1) * T],
                                      par("wa_up", c * P, P)[rows], DD[rows, :], c % 2 == 0, True)
                    last.then_inc(pe_["up"], 1)
                elif kind == "upg":
                    pe.wait_ge(act_["lora"], 2 * l + 2)
                    pe.wait_ge(act_["up"], n_of("up", l, 1))
                    for c in range(BT):
                        last = mm(bank[3 + c // 2][:, (c % 2) * T:(c % 2 + 1) * T], par("g_up", c * P, P),
                                  DG[:, :], c % 2 == 0, True)
                    last.then_inc(pe_["upg"], 1)
                elif kind == "kk":
                    pe.wait_ge(act_["kkq"], n_of("kkq", l, 1))
                    for b in range(2):
                        last = mm(bank[5 + b][:, :], cst("bones"), unit(8)[:, b * 512:(b + 1) * 512], True, True)
                    last.then_inc(pe_["kk"], 1)
                elif kind == "bon":
                    pe.wait_ge(act_["rk"], n_of("rk", l, 1))
                    for b in range(2):
                        last = mm(bank[6 + b][:, :], cst("bones"), unit(9)[:, b * 512:(b + 1) * 512], True, True)
                    last.then_inc(pe_["bon"], 1)
                elif kind == "natv":
                    pe.wait_ge(mixed, l * A_SLABS + A_SLABS)
                    for ch in range(2):
                        for c in range(BT):
                            last = pe.transpose(bank[3 + ch][:, c * P:(c + 1) * P], V[:, c, ch * C:(ch + 1) * C],
                                                cst("ident"))
                    last.then_inc(pe_["natv"], 1)
                elif kind == "natk":
                    pe.wait_ge(dve_["prepb"], n_of("prepb", l, 1))
                    pe.wait_ge(beta_ready, l + 1)
                    pe.wait_ge(act_["natv"], n_of("natv", l, 1))
                    for b, src in ((5, K), (3, A_)):
                        for c in range(BT):
                            last = pe.transpose(bank[b][:, c * P:(c + 1) * P], src[:, c, 0:C], cst("ident"))
                    last.then_inc(pe_["natk"], 1)
                elif kind == "mat":
                    what, i = s[2], ORD[s] % 6
                    if i >= 2:
                        pe.wait_ge(dve_["mat"], n_of("mat", l, ORD[s] - 1))
                    elif ORD[s] == 0:
                        pe.wait_ge(act_["natk"], n_of("natk", l, 1))
                        pe.wait_ge(dve_["bon"], n_of("bon", l, 1))
                    elif i == 0:
                        pe.wait_ge(act_["o"], n_of("o", l, 2))
                    b0 = 3 + 2 * (i % 2)
                    for i in range(4):
                        rows, ch = slice(HD * (i // 2), HD * (i // 2 + 1)), i % 2
                        toks = slice(ch * C, (ch + 1) * C)
                        if what == "abt":
                            last = mm(bank[b0 + i // 2][:, ch * P:(ch + 1) * P], AR[rows, c, ch, 0, :],
                                      A_[rows, c, toks], ch == 0, True)
                        else:
                            last = mm(bank[b0 + i // 2][:, ch * 256:(ch + 1) * 256],
                                      (A_ if what == "ab" else K)[rows, c, toks],
                                      AR[rows, c, ch].rearrange("p a t -> p (a t)"), ch == 0, True)
                    last.then_inc(pe_["mat"], 1)
                elif kind == "m1":
                    if s[2] == 2:
                        pe.wait_ge(dve_["mat"], n_of("mat", l, ORD[("mat", c | 1, "akb")] + 1))
                    else:
                        pe.wait_ge(x_done, l * X_STEPS + X_STEP[("dxy", c, s[2] // 2)] + 1)
                    for i in range(4):
                        last = mm(bank[4 + 2 * j][:, i * P:(i + 1) * P], ABT[:, j, i, 0:C], X[:, j, i, :], i == 0, True)
                    last.then_inc(pe_["m1"], 1)
                elif kind == "dxy":
                    pe.wait_ge(dve_["m1"], n_of("m1", l, ORD[("m1", c, s[2])] + 1))
                    if ORD[s] >= 2:
                        pe.wait_ge(dve_["dxy"], n_of("dxy", l, ORD[s] - 1))
                    if s[2] < LEVELS[-1]:
                        for i in range(4):
                            last = mm(bank[4 + 2 * j][:, i * P:(i + 1) * P], Y[:, j, i, :], M1[:, j, i, :], i == 0,
                                      True)
                        last.then_inc(x_mm, 1)
                    for i in range(4):
                        last = mm(bank[5 + 2 * j][:, i * P:(i + 1) * P], M1[:, j, i, :], Y[:, j, i, :], i == 0, True)
                    last.then_inc(pe_["dxy"], 1)
                elif kind == "rhs0":
                    pe.wait_ge(dve_["dxy"], n_of("dxy", l, ORD[("dxy", c | 1, LEVELS[-1])] + 1))
                    for hp in range(2):
                        last = mm(bank[3 + j][:, hp * HD:(hp + 1) * HD], KBT[:, j, 2 * hp, 0:C],
                                  Vn[:, 0, c * P + hp * HD:c * P + (hp + 1) * HD], hp == 0, True)
                    last.then_inc(pe_["rhs0"], 1)
                elif kind in ("u0", "u1"):
                    ch = int(kind[1])
                    pe.wait_ge(dve_[f"rhs{ch}"], n_of(f"rhs{ch}", l, c + 1))
                    for hp in range(2):
                        last = mm(bank[(3 if ch else 5) + j][:, hp * HD:(hp + 1) * HD], Y[:, j, 2 * hp + ch, :],
                                  RHS[:, j, hp * HD:(hp + 1) * HD], hp == 0, True)
                    last.then_inc(pe_[kind], 1)
                elif kind == "s1":
                    pe.wait_ge(act_["u0"], n_of("u0", l, c + 1))
                    mm(bank[3 if j else 7][:, 0:P], BKn[:, 0, c * P:(c + 1) * P], Vn[:, 0, c * P:(c + 1) * P], True, False)
                    mm(bank[3 if j else 7][:, 0:P], BKn[:, 1, c * P:(c + 1) * P], NU[:, j, 0, :], False, True)\
                        .then_inc(pe_["s1"], 1)
                elif kind == "rhs1":
                    pe.wait_ge(dve_["s1"], n_of("s1", l, c + 1))
                    for hp in range(2):
                        rows, out = slice(hp * HD, (hp + 1) * HD), bank[4 + 2 * j + hp][:, 0:HD]
                        mm(out, KBT[:, j, 2 * hp + 1, 0:C], Vn[:, 1, c * P + hp * HD:c * P + (hp + 1) * HD],
                           True, False)
                        last = mm(out, AR[rows, c, 1, 0, :], s0[rows, c, :], False, True)
                    last.then_inc(pe_["rhs1"], 1)
                elif kind == "o":
                    pe.wait_ge(act_["u1"], n_of("u1", l, c + 1))
                    for hp in range(2):
                        rows, head = slice(hp * HD, (hp + 1) * HD), slice(c * P + hp * HD, c * P + (hp + 1) * HD)
                        for ch in range(2):
                            out, i = bank[(3 if j else 5) + hp][rows, ch * C:(ch + 1) * C], 2 * hp + ch
                            mm(out, Vn[:, ch, head], KBT[:, j, i, C:2 * C], ch == 0, False)
                            if ch == 1:
                                mm(out, s0[rows, c, :], AR[rows, c, 1, 1, :], False, False)
                            last = mm(out, NU[:, j, ch, hp * HD:(hp + 1) * HD], ABT[:, j, i, C:2 * C], False, True)
                    last.then_inc(pe_["o"], 1)
                elif kind in ("gn1", "gn2"):
                    if kind == "gn1":
                        pe.wait_ge(act_["o"], n_of("o", l, BT))
                        pe.wait_ge(act_["u1"], n_of("u1", l, BT))
                    else:
                        pe.wait_ge(act_["gn1"], n_of("gn1", l, 1))
                    for b in range(2):
                        last = mm(bank[5 + b][:, :], cst("bones"),
                                  unit(4 if kind == "gn1" else 7)[:, b * 512:(b + 1) * 512], True, True)
                    last.then_inc(pe_[kind], 1)
                elif kind == "bz":
                    h, rows = c, slice(HD * (c % 2), HD * (c % 2 + 1))
                    if h == 0:
                        pe.wait_ge(*n_out(l, OUT_BK))
                        pe.wait_ge(*n_out(l, OUT_BV))
                        pe.wait_ge(act_["o"], n_of("o", l, BT))
                    if h >= 2:
                        pe.wait_ge(act_["btri"], n_of("btri", l, h - 1))
                    out = bank[3 + h % 2]
                    mm(out[:, 0:T], kb[rows, h // 2, 0:P], qb[rows, h // 2, :], True, False)
                    mm(out[:, T:T + P], kb[rows, h // 2, P:T], qb[rows, h // 2, P:T], False, False)\
                        .then_inc(pe_["bz"], 1)
                elif kind == "btri":
                    h, out = c, bank[3 + c % 2]
                    pe.wait_ge(dve_["bz"], n_of("bz", l, h + 1))
                    mm(out[:, 0:T], cst("triN"), SP[:, j, 0:T], False, False)
                    mm(out[:, P:T], cst("onesN"), SP[:, j, T:T + P], False, False)
                    mm(out[:, T:T + P], cst("triN"), SP[:, j, T:T + P], False, True).then_inc(pe_["btri"], 1)
                elif kind == "bav":
                    h, c, rows = c, c // 2, slice(HD * (c % 2), HD * (c % 2 + 1))
                    out = bank[5 + c % 2]
                    pe.wait_ge(dve_["btri"], n_of("btri", l, h + 1))
                    if h == 0:
                        pe.wait_ge(act_["gn2"], n_of("gn2", l, 1))
                    if h % 2 == 0 and c >= 2:
                        pe.wait_ge(dve_["bav"], l * BT + c - 1)
                    mm(out[rows, 0:T], vb[:, 0, h * HD:(h + 1) * HD], AB[:, j, 0:T], True, False)
                    mm(out[rows, P:T], vb[:, 1, h * HD:(h + 1) * HD], AB[:, j, T:T + P], False, True)\
                        .then_inc(pe_["bav"], 1)
                elif kind == "cs":
                    h, tt, n, keys = s[1], s[2], ORD[s], P * (s[2] + 1)
                    if n == 0:
                        pe.wait_ge(*n_out(l, OUT_CV))
                        pe.wait_ge(*n_out(l, OUT_CK))
                        pe.wait_ge(act_["btri"], n_of("btri", l, AH))
                    if n == 1:
                        pe.wait_ge(dve_["bav"], l * BT + BT)
                    if n >= 2:
                        pe.wait_ge(act_["cs"], n_of("cs", l, n - 1))
                    for m in range(2):
                        rows, out = slice(HD * m, HD * (m + 1)), bank[3 + 2 * (n % 2) + m]
                        mm(out[:, 0:keys], qc[rows, h, tt * P:(tt + 1) * P], kc[rows, h, 0:keys], True, False)
                        one = slice(HD * m, HD * m + 1)
                        last = mm(out[:, keys - 64:keys], cst("rowL")[one, :], cst("rowR")[one, :], False, True)
                    last.then_inc(pe_["cs"], 1)
                elif kind == "ct":
                    n = ORD[s]
                    pe.wait_ge(dve_["cs"], n_of("cs", l, n + 1))
                    after(act_, "ct", l, n)
                    after(act_, "cav", l, n // 2)
                    for b in range(s[2] + 1):
                        last = pe.transpose(bank[7][:, b * P:(b + 1) * P],
                                            PC[:, n % 2, 0, b * P:(b + 1) * P], cst("ident"))
                    last.then_inc(pe_["ct"], 1)
                elif kind == "cav":
                    h = c
                    pe.wait_ge(act_["ct"], n_of("ct", l, 2 * h + 2))
                    mm(bank[7][:, 0:T], vc[:, 0, h * P:(h + 1) * P], ATC[:, h % 2, 0, :], True, False)
                    mm(bank[7][:, P:T], vc[:, 1, h * P:(h + 1) * P], ATC[:, h % 2, 1, P:T], False, True)\
                        .then_inc(pe_["cav"], 1)
                elif kind == "crms":
                    pe.wait_ge(act_["cav"], n_of("cav", l, CH))
                    pe.wait_ge(act_["cs"], n_of("cs", l, 2 * CH))
                    for b in range(2):
                        last = mm(bank[3 + b][:, :], cst("ones"),
                                  OSQ[:, 2 * b:2 * b + 2, :].rearrange("p c t -> p (c t)"), True, True)
                    last.then_inc(pe_["crms"], 1)

            def ffn_up(l, t, u, slab, s0_, first):
                for which in range(2):
                    s = (s0_ + which) % RING
                    pe.wait_ge(lo_done, slab + (which + 1))
                    if not first:
                        pe.wait_ge(up_scaled, l * 2 * FT + 2 * t + (which - 3))
                    for k in range(KT):
                        cols = slice(k * P, (k + 1) * P)
                        last = split_mm(bank[2 * (u % 2) + which][:, 0:T], (hi[:, s, cols], lo[:, s, cols]),
                                        (hh[:, k, :], hl[:, k, :]), k == 0, k == KT - 1)
                    last.then_inc(slab_done, 1)

            def ffn_down(l, t, u, slab, s, first):
                pe.wait_ge(lo_done, slab + 1)
                pe.wait_ge(prod_l, l * FT + t + 1)
                for c in range(KT):
                    cols = slice(c * P, (c + 1) * P)
                    last = split_mm(bank[4 + c // 2][:, (c % 2) * T:(c % 2 + 1) * T], (hi[:, s, cols], lo[:, s, cols]),
                                    (oh[:, u % 2, :], ol[:, u % 2, :]), first and c % 2 == 0, False)
                last.then_inc(slab_done, 1)

            with pe.Fori(0, DEPTH) as l:
                pe.wait_ge(mix_in_s, 16 * l + 16)
                for s in STEPS:
                    step(l, s)
                at = l * SLABS + FFN0
                pe.wait_ge(*n_out(l, len(OUTS) - 1))
                two_slabs(at, FFN0 % RING, l * 2 * KT + KT)
                norm(2 * l + 1)
                ffn_up(l, 1, 1, at + 2, (FFN0 + 2) % RING, True)
                ffn_down(l, 0, 0, at + 4, (FFN0 + 4) % RING, True)
                with pe.Fori(0, FTURNS) as i:
                    for u in range(FU):
                        t, o = FU * i + (u + 2), 5 + 3 * u
                        slab = l * SLABS + 3 * FU * i + (FFN0 + o)
                        ffn_up(l, t, u, slab, (FFN0 + o) % RING, False)
                        ffn_down(l, FU * i + (u + 1), u + 1, slab + 2, (FFN0 + o + 2) % RING, False)
                ffn_down(l, FT - 1, FT - 1, l * SLABS + SLABS - 1, (SLABS - 1) % RING, False)
            norm(2 * DEPTH)

        @block.scalar
        def _(act):
            own = Own(act, act_own_s, ACT_OWN)

            def load_parameters(l):
                act.dma_start(pm[:, 0:PM["wa_up"][0]], mix_in[l, :, 0:PM["wa_up"][0]]).then_inc(mix_in_s, 16)
                act.dma_start(pm[:, PM["wa_up"][0]:], mix_in[l, :, PM["wa_up"][0]:]).then_inc(ups_in_s, 16)

            def do(out, in_, func, scale=1.0, bias=0.0, **kw):
                return act.activation(out, in_, func, scale=scale, bias=bias, **kw)

            def split(m, s, used, landed):
                act.wait_ge(raw_in[s], landed)
                if used is not None:
                    act.wait_ge(slab_done, used)
                do(hi[:, s, :], raw[:, s, :], ACT.Copy).then_inc(hi_done, 1)

            def ahead(l, n):
                split(n + AHEAD, (n + AHEAD) % RING, l * SLABS + n if n else None,
                      l * (16 * SLABS // RING) + 16 * ((n + AHEAD) // RING + 1))

            def hi_merged(l, cp):
                pair = slice(2 * cp, 2 * cp + 2)
                act.wait_ge(merged, l * (KT // 2) + cp + 1)
                do(oh[:, pair, :], MG[:, pair, :], ACT.Copy).then_inc(merged_h, 1)

            def empty(l, n):
                kind = DENSE[n][0]
                if kind == "A":
                    j = DENSE[n][1]
                    if j == 0:
                        act.wait_ge(dve_mid["lam"], n_of("lam", l, 1))
                    act.wait_ge(*n_out(l, OUT_OF[n][0]))
                    do(a_tile(j), TMP[:, j % 2, :], ACT.Identity, scale=omu[:, j:j + 1],
                       bias=cst("zero")).then_inc(mixed_now, 1)
                elif kind in ("Bv", "Cv"):
                    act.wait_ge(slab_done, l * SLABS + n + 1)
                    for tt, m in enumerate(OUT_OF[n]):
                        do((vb if kind == "Bv" else vc)[:, tt, :], bank[m % 3][:, :], ACT.Copy,
                           scale=rs[:, T + tt:T + tt + 1]).then_inc(emptied["act"], 1)
                elif kind == "BR" and DENSE[n][1] == 2:
                    cp = DENSE[n][2]
                    if cp:
                        hi_merged(l, cp - 1)
                    if cp == KT // 2 - 1:
                        hi_merged(l, cp)
                elif kind == "O":
                    c = DENSE[n][1]
                    if c == 0:
                        act.wait_ge(ffn_in_s, 16 * l + 16)
                    act.wait_ge(*n_out(l, OUT_O + c))
                    do(hh[:, c, :], x[:, c, :], ACT.Copy, scale=pf[:, c:c + 1]).then_inc(split_h, 1)
                    if c % 2:
                        do(XSQ[:, c - 1:c + 1, :], x[:, c - 1:c + 1, :], ACT.Square).then_inc(square_done, 1)

            def squares(ready=None):
                for b in range(4):
                    if ready:
                        ready(b)
                    do(XSQ[:, 2 * b:2 * b + 2, :], x[:, 2 * b:2 * b + 2, :], ACT.Square).then_inc(square_done, 1)

            def norm(n):
                act.wait_ge(pe_["norm"], n + 1)
                own.mark(do(rs[:, :], bank[4][:, 0:T + 2], ACT.Ln, scale=1.0 / D, bias=cst("eps")))
                own.wait()
                do(rs[:, :], rs[:, :], ACT.Exp, scale=-0.5).then_inc(rms_inv, 1)

            def step(l, s):
                kind = s[0]
                c = s[1] if len(s) > 1 else 0
                j = c % 2
                if kind == "D":
                    ahead(l, s[1])
                elif kind == "E":
                    empty(l, s[1])
                elif kind == "xs":
                    if c == 0:
                        for t in range(KT):
                            if t % 2 == 0:
                                act.wait_ge(x_ready, 4 * l + t // 2 + 1)
                            do(hh[:, t, :], x[:, t, :], ACT.Copy, scale=par("g", t)).then_inc(split_h, 1)
                        squares()
                    else:
                        act.preload_act_table_set("natural_log_exp_and_others")
                elif kind == "norm":
                    norm(2 * l)
                elif kind == "lam":
                    act.wait_ge(pe_["lam"], n_of("lam", l, 1))
                    do(small[:, 2:4], bank[7][:, 0:2], ACT.Exp).then_inc(act_["lam"], 1)
                elif kind == "lora":
                    act.wait_ge(mixed, l * A_SLABS + 1)
                    do(DD[0:64, :], DD[0:64, :], ACT.Tanh).then_inc(act_["lora"], 1)
                    act.wait_ge(mixed, l * A_SLABS + 2)
                    do(DG[:, :], DG[:, :], ACT.Sigmoid).then_inc(act_["lora"], 1)
                elif kind == "up":
                    act.wait_ge(pe_["up"], n_of("up", l, 1))
                    for dst, b0, name in ((SG, 3, "w0"), (A_, 5, "a0")):
                        for c in range(BT):
                            ins = do(dst[:, c, :], bank[b0 + c // 2][:, (c % 2) * T:(c % 2 + 1) * T], ACT.Sigmoid,
                                     bias=par(name, c))
                    ins.then_inc(act_["up"], 1)
                elif kind == "upg":
                    act.preload_act_table_set("natural_log_exp_and_others")
                    act.wait_ge(pe_["upg"], n_of("upg", l, 1))
                    for b in range(2):
                        do(unit(3)[:, b * 512:(b + 1) * 512], bank[3 + b][:, :], ACT.Copy)
                    act.wait_ge(dve_["upg"], n_of("upg", l, 1))
                    own.mark(do(unit(7).rearrange("p (n t) -> p n t", t=C), PP[:, :, 1:C + 1], ACT.Exp,
                                scale=DECAY_SCALE))
                    do(small[:, 16:24], small[:, 8:16], ACT.Exp, scale=-DECAY_SCALE)
                    own.wait()
                    do(PP, PP, ACT.Exp, scale=-DECAY_SCALE).then_inc(act_["upg"], 1)
                elif kind == "kkq":
                    act.wait_ge(mixed, l * A_SLABS + 6)
                    for c in range(BT):
                        own.mark(do(KKt[:, c, :], K[:, c, :], ACT.Copy, scale=par("k_k", c)))
                    own.wait()
                    do(unit(8), unit(4), ACT.Square).then_inc(act_["kkq"], 1)
                elif kind == "kk":
                    act.wait_ge(pe_["kk"], n_of("kk", l, 1))
                    for c in range(BT):
                        ins = do(SQ[:, c, :], A_[:, c, :], ACT.Identity, scale=par("k_a", c), bias=omu[:, 14 + c:15 + c])
                    ins.then_inc(act_["kk"], 1)
                elif kind == "kkn":
                    act.wait_ge(dve_["kk"], n_of("kk", l, 1))
                    own.mark(do(unit(9), unit(9), ACT.Ln, scale=float(2 ** 20)))
                    own.wait()
                    do(unit(9), unit(9), ACT.Exp, scale=-0.5, bias=cst("kkb")).then_inc(act_["kkn"], 1)
                elif kind == "rk":
                    act.wait_ge(dve_mid["prepb"], n_of("prepb", l, 1))
                    for c in range(BT):
                        ins = do(SB[:, c, :], SB[:, c, :], ACT.Copy, scale=par("r_k", c))
                    ins.then_inc(act_["rk"], 1)
                elif kind == "natv":
                    act.wait_ge(dve_mid["bon"], n_of("bon", l, 1))
                    act.wait_ge(pe_["natv"], n_of("natv", l, 1))
                    do(Vn[:, 0, :], bank[3][:, :], ACT.Copy)
                    do(Vn[:, 1, :], bank[4][:, :], ACT.Copy).then_inc(act_["natv"], 1)
                elif kind == "natk":
                    act.wait_ge(pe_["natk"], n_of("natk", l, 1))
                    do(BKn[:, 0, :], bank[5][:, :], ACT.Copy)
                    do(BKn[:, 1, :], bank[3][:, :], ACT.Copy).then_inc(act_["natk"], 1)
                elif kind in ("u0", "u1"):
                    act.wait_ge(pe_[kind], n_of(kind, l, c + 1))
                    do(NU[:, j, int(kind[1]), :], bank[(3 if kind == "u1" else 5) + j][:, 0:P], ACT.Copy, scale=-1.0).then_inc(act_[kind], 1)
                elif kind == "o":
                    act.wait_ge(pe_["o"], n_of("o", l, c + 1))
                    for hp in range(2):
                        rows = slice(hp * HD, (hp + 1) * HD)
                        ins = do(OT[rows, c, :], bank[(3 if j else 5) + hp][rows, 0:T], ACT.Copy)
                    ins.then_inc(act_["o"], 1)
                elif kind == "gn1":
                    act.wait_ge(dve_["gn1"], n_of("gn1", l, 1))
                    do(unit(7), unit(4), ACT.Square).then_inc(act_["gn1"], 1)
                elif kind == "gn2":
                    act.wait_ge(pe_["gn2"], n_of("gn2", l, 1))
                    for b in range(2):
                        own.mark(do(unit(6)[:, b * 512:(b + 1) * 512], bank[5 + b][:, :], ACT.Ln, scale=1.0 / HD,
                                    bias=cst("gneps")))
                    own.wait()
                    do(unit(6), unit(6), ACT.Exp, scale=-0.5).then_inc(act_["gn2"], 1)
                elif kind == "gn3":
                    act.wait_ge(dve_["gn2"], n_of("gn2", l, 1))
                    for c in range(BT):
                        ins = do(OT[:, c, :], OT[:, c, :], ACT.Identity, scale=par("ln_w", c), bias=par("ln_b", c))
                    ins.then_inc(act_["gn3"], 1)
                elif kind == "gn4":
                    act.wait_ge(dve_["gn3"], n_of("gn3", l, 1))
                    do(oh[:, 0:BT, :], OT, ACT.Copy).then_inc(act_["gn4"], 1)
                elif kind == "bz":
                    act.wait_ge(pe_["bz"], n_of("bz", l, c + 1))
                    own.mark(do(W1[:, j, :], bank[3 + j][:, 0:T + P], ACT.Abs))
                    own.wait()
                    own.mark(do(W1[:, j, :], W1[:, j, :], ACT.Exp, scale=-1.0))
                    own.wait()
                    do(W1[:, j, :], W1[:, j, :], ACT.Ln, bias=cst("one")).then_inc(act_["bz"], 1)
                elif kind == "btri":
                    act.wait_ge(pe_["btri"], n_of("btri", l, c + 1))
                    do(AB[:, j, :], bank[3 + j][:, 0:T + P], ACT.Exp).then_inc(act_["btri"], 1)
                elif kind == "bav":
                    if c % 2:
                        act.wait_ge(pe_["bav"], n_of("bav", l, c + 1))
                        do(oh[:, BT + c // 2, :], bank[5 + (c // 2) % 2][:, 0:T], ACT.Copy).then_inc(act_["bav"], 1)
                elif kind == "cs":
                    n, keys = ORD[s], P * (s[2] + 1)
                    f = 28 + 12 * (n % 2)
                    act.wait_ge(dve_mid["cs"], n_of("cs", l, n + 1))
                    for m in range(2):
                        ins = do(PC[:, n % 2, m, 0:keys], bank[3 + 2 * (n % 2) + m][:, 0:keys], ACT.Exp,
                                 scale=HD ** -0.5, bias=small[:, f + 2 + m:f + 3 + m],
                                 accum_out=small[:, f + 4 + m:f + 5 + m])
                    ins.then_inc(act_["cs"], 1)
                elif kind == "ct":
                    n, tt = ORD[s], s[2]
                    act.wait_ge(pe_["ct"], n_of("ct", l, n + 1))
                    do(ATC[:, c % 2, 0:tt + 1, tt * P:(tt + 1) * P],
                       bank[7][:, 0:(tt + 1) * P].rearrange("p (k t) -> p k t", t=P), ACT.Copy)\
                        .then_inc(act_["ct"], 1)
                elif kind == "cav":
                    act.wait_ge(pe_["cav"], n_of("cav", l, c + 1))
                    do(OC[:, c, :], bank[7][:, 0:T], ACT.Copy)
                    do(OSQ[:, c, :], bank[7][:, 0:T], ACT.Square).then_inc(act_["cav"], 1)
                elif kind == "crms":
                    act.wait_ge(pe_["crms"], n_of("crms", l, 1))
                    for b in range(2):
                        own.mark(do(OSQ[:, 2 * b:2 * b + 2, :].rearrange("p c t -> p (c t)"), bank[3 + b][:, :], ACT.Ln,
                                    scale=1.0 / (2 * HD), bias=cst("eps")))
                    own.wait()
                    do(OSQ[:, :, :], OSQ[:, :, :], ACT.Exp, scale=-0.5).then_inc(act_mid["crms"], 1)
                    act.wait_ge(dve_mid["crms"], n_of("crms", l, 1))
                    do(oh[:, 2 * BT:3 * BT, :], OC[:, :, :], ACT.Copy).then_inc(act_["crms"], 1)
                elif kind == "gsig":
                    act.wait_ge(*n_out(l, OUT_OF[DENSE.index(("G", KT * min(c, 2) + KT - 1))][0]))
                    g = unit(2 * c, 2) if c < 2 else unit(2 + c)
                    do(g, g, ACT.Sigmoid).then_inc(gates_ready, 1)
                    if c == 1:
                        act.wait_ge(dve_["gn4"], n_of("gn4", l, 1))
                        act.wait_ge(dve_mid["lam"], n_of("lam", l, 1))
                        load_parameters(l + 1)
                    if c in (1, 3):
                        act.preload_act_table_set("natural_log_exp_and_others")

            def conv(l, t, u, which, col, reuse):
                act.wait_ge(up_scaled, l * 2 * FT + 2 * t + (which + 1))
                if reuse:
                    act.wait_ge(prod_l, l * FT + t + (-1))
                k = 2 * (u % 2) + which
                do(CV[:, k, :], UM[:, k, :], ACT.Identity, scale=tap(col, 2), bias=tap(col, 3)).then_inc(tap2, 1)

            def silu(l, t, u):
                act.wait_ge(conv_done, l * 2 * FT + 2 * t + 1)
                g = CV[:, 2 * (u % 2), :]
                do(g, g, ACT.Silu).then_inc(silu_done, 1)

            def product(l, t, u):
                act.wait_ge(prod_done, l * FT + t + 1)
                do(oh[:, u % 2, :], CV[:, 2 * (u % 2), :], ACT.Copy).then_inc(prod_h, 1)

            load_parameters(0)
            act.preload_act_table_set("natural_log_exp_and_others")
            for m in range(AHEAD):
                split(m, m, None, 16)
            with act.Fori(0, DEPTH) as l:
                own.base, own.n = l * ACT_OWN["layer"], 0
                act.wait_ge(mix_in_s, 16 * l + 16)
                for s in ACT_STEPS:
                    step(l, s)
                act.wait_ge(ffn_in_s, 16 * l + 16)
                for t in range(2):
                    for which in range(2):
                        ahead(l, FFN0 + 2 * t + which)
                    if t == 0:
                        norm(2 * l + 1)
                        act.preload_act_table(ACT.Silu)
                    for which in range(2):
                        conv(l, t, t, which, 8 + 4 * (2 * t + which), False)
                    silu(l, t, t)
                    if t:
                        ahead(l, FFN0 + 4)
                    product(l, t, t)
                with act.Fori(0, FTURNS) as i:
                    for u in range(FU):
                        t = FU * i + (u + 2)
                        o = FFN0 + 5 + 3 * u
                        for which in range(2):
                            ahead_in(split, l, i, o + which)
                        for which in range(2):
                            conv(l, t, u, which, 8 * FU * i + (8 + 8 * (u + 2) + 4 * which), True)
                        silu(l, t, u)
                        ahead_in(split, l, i, o + 2)
                        product(l, t, u)
                ahead(l, SLABS - 1)
                act.preload_act_table_set("natural_log_exp_and_others")
                assert own.n == ACT_OWN["layer"], ("act", own.n)
            own.base, own.n = DEPTH * ACT_OWN["layer"], 0
            squares(lambda b: act.wait_ge(x_ready, 4 * DEPTH + b + 1))
            norm(2 * DEPTH)

        @block.vector
        def _(dve):
            own = Own(dve, dve_own_s, DVE_OWN)
            tt = dve.tensor_tensor
            stt = dve.scalar_tensor_tensor

            def bc(ap, n, w):
                return ap.unsqueeze(2).broadcast_to([P, n, w])

            def rep(ap, n):
                return ap.unsqueeze(1).broadcast_to([P, n, ap.shape[1]])

            def split(m, s, used, landed):
                if used is not None:
                    dve.wait_ge(slab_done, used)
                dve.wait_ge(hi_done, m + 1)
                tt(lo[:, s, :], raw[:, s, :], hi[:, s, :].bitcast(F32), ALU.subtract).then_inc(lo_done, 1)

            def ahead(l, n):
                split(l * SLABS + (n + AHEAD), (n + AHEAD) % RING, l * SLABS + n if n else None, None)

            def lo_x(l, half, t):
                dve.wait_ge(split_h, l * 2 * KT + KT * half + t + 1)
                stt(hl[:, t, :], x[:, t, :], pf[:, t:t + 1] if half else par("g", t),
                    hh[:, t, :].bitcast(F32), ALU.mult, ALU.subtract).then_inc(split_l, 1)

            def add_squares(n):
                dve.wait_ge(square_done, 4 * n + 4)
                own.mark(tt(XSQ[:, 0:4, :], XSQ[:, 0:4, :], XSQ[:, 4:8, :], ALU.add))
                own.wait()
                tt(XSQ[:, 0:2, :], XSQ[:, 0:2, :], XSQ[:, 2:4, :], ALU.add).then_inc(squared, 1)

            def lo_merged(l, cp):
                pair = slice(2 * cp, 2 * cp + 2)
                dve.wait_ge(merged_h, l * (KT // 2) + cp + 1)
                tt(ol[:, pair, :], MG[:, pair, :], oh[:, pair, :].bitcast(F32), ALU.subtract).then_inc(merged_l, 1)

            def mix_before(l, j):
                dst = a_tile(j)
                dve.wait_ge(mixed_now, l * A_SLABS + j + 1)
                stt(dst[:, 1:T], TMP[:, j % 2, 0:T - 1], par("mu", j), dst[:, 1:T], ALU.mult, ALU.add)\
                    .then_inc(mixed, 1)

            def rotate(l, n):
                kind, c = DENSE[n]
                dst, i = (qc if kind == "Cq" else kc)[:, c, :], n - DENSE.index(("Cq", 0))
                partner = bank[OUT_OF[n][0] % 3][:, T:2 * T]
                dve.wait_ge(rope_mm, l * 2 * BT + i + 1)
                own.mark(tt(dst, dst, cst("cos"), ALU.mult))
                own.mark(tt(partner, partner, cst("sin"), ALU.mult))
                own.wait()
                tt(dst, dst, partner, ALU.add).then_inc(emptied["dve"], 1)

            def empty(l, n):
                kind, b = DENSE[n][0], bank[OUT_OF[n][0] % 3]
                if n == A_SLABS:
                    mix_before(l, A_SLABS - 1)
                if DENSE[n] == ("Cv", 3):
                    rotate(l, DENSE.index(("Ck", 3)))
                elif DENSE[n - 1][0] in ("Cq", "Ck"):
                    rotate(l, n - 1)
                if kind not in ("Bv", "Cv"):
                    dve.wait_ge(slab_done, l * SLABS + n + 1)
                if kind == "A":
                    j = DENSE[n][1]
                    if j == 0:
                        dve.wait_ge(rms_inv, 2 * l + 1)
                    if j >= 2:
                        dve.wait_ge(mixed, l * A_SLABS + j - 1)
                    tt(TMP[:, j % 2, :], b[:, 0:T], rs[:, 0:T], ALU.mult).then_inc(emptied["dve"], 1)
                    if j:
                        mix_before(l, j - 1)
                elif kind in ("Bq", "Bk"):
                    if n == A_SLABS:
                        dve.wait_ge(mixed, l * A_SLABS + A_SLABS)
                    stt((qb if kind == "Bq" else kb)[:, DENSE[n][1], :], b[:, 0:T],
                        HD ** -0.5 if kind == "Bq" else 1.0, rs[:, 0:T], ALU.mult, ALU.mult).then_inc(emptied["dve"], 1)
                elif kind in ("Cq", "Ck"):
                    tt((qc if kind == "Cq" else kc)[:, DENSE[n][1], :], b[:, 0:T], rs[:, 0:T], ALU.mult)\
                        .then_inc(rope_raw, 1)
                elif kind == "G":
                    g, c = divmod(DENSE[n][1], KT)
                    tt(GATE[:, g, c, :], b[:, 0:T], rs[:, 0:T], ALU.mult).then_inc(emptied["dve"], 1)
                elif kind == "BR":
                    g, cp = DENSE[n][1:]
                    pair = slice(2 * cp, 2 * cp + 2)
                    out = b[:, :].rearrange("p (c t) -> p c t", t=T)
                    if cp == 0:
                        dve.wait_ge(gates_ready, 4 * l + g + 1)
                    if g == cp == 2:
                        dve.wait_ge(gates_ready, 4 * l + 4)
                    if g == 0:
                        tt(MG[:, pair, :], GATE[:, g, pair, :], out, ALU.mult).then_inc(emptied["dve"], 1)
                    else:
                        tmp = BTMP[:, g - 1, cp % 2]
                        if cp >= 2:
                            dve.wait_ge(merged if g == 2 else merged_b, l * (KT // 2) + cp - 1)
                        tt(tmp, GATE[:, g, pair, :], out, ALU.mult).then_inc(emptied["dve"], 1)
                        if g == 2:
                            dve.wait_ge(*n_out(l, OUT_OF[n][0]))
                            dve.wait_ge(merged_b, l * (KT // 2) + cp + 1)
                            tt(MG[:, pair, :], MG[:, pair, :], tmp, ALU.add).then_inc(merged, 1)
                        if g == 2 and cp:
                            lo_merged(l, cp - 1)
                        if g == 2 and cp == KT // 2 - 1:
                            lo_merged(l, cp)
                elif kind == "O":
                    c = DENSE[n][1]
                    tt(x[:, c, :], x[:, c, :], b[:, 0:T], ALU.add).then_inc(emptied["dve"], 1)
                    if c:
                        lo_x(l, 1, c - 1)

            def step(l, s):
                kind = s[0]
                c = s[1] if len(s) > 1 else 0
                j = c % 2
                if kind == "D":
                    ahead(l, s[1])
                elif kind == "E":
                    empty(l, s[1])
                elif kind == "xs":
                    for t in range(KT) if c == 0 else (KT - 1,):
                        lo_x(l, c, t)
                    if c == 0:
                        dve.tensor_scalar(omu[:, 0:14], par("mu", 0, 14), -1.0, 1.0, ALU.mult, ALU.add)
                        dve.tensor_scalar(omu[:, 14:18], par("k_a", 0, 4), -1.0, 1.0, ALU.mult, ALU.add)
                        tt(omu[:, 18:19], par("subln"), par("omli"), ALU.mult)
                        lv = par("lam", 0, 4).rearrange("p (a b) -> p a b", b=2)
                        tt(small[:, 0:2], lv[:, :, 0], lv[:, :, 1], ALU.mult).then_inc(dve_mid["lam"], 1)
                    add_squares(2 * l + c)
                elif kind == "lam":
                    dve.wait_ge(act_["lam"], n_of("lam", l, 1))
                    stt(small[:, 4:5], small[:, 3:4], small[:, 2:3], par("li"), ALU.subtract, ALU.subtract)\
                        .then_inc(dve_["lam"], 1)
                elif kind == "upg":
                    dve.wait_ge(pe_["upg"], n_of("upg", l, 1))
                    dve.wait_ge(act_["up"], n_of("up", l, 1))
                    own.mark(dve.memset(PP[:, :, 0:1], 0.0))
                    e = unit(6).rearrange("p (n t) -> p n t", t=C)
                    for n in range(8):
                        ins = dve.tensor_tensor_scan(PP[:, n, 1:C + 1], e[:, n, :], e[:, n, :], 0.0, ALU.add,
                                                     ALU.bypass)
                    own.mark(ins)
                    own.wait()
                    own.mark(dve.tensor_copy(small[:, 8:16], PP[:, :, C // 2]))
                    own.wait()
                    tt(PP, PP, bc(small[:, 8:16], 8, C + 1), ALU.subtract).then_inc(dve_["upg"], 1)
                elif kind == "kk":
                    dve.wait_ge(pe_["kk"], n_of("kk", l, 1))
                    for b in range(2):
                        ins = dve.tensor_scalar(unit(9)[:, b * 512:(b + 1) * 512], bank[5 + b][:, :], 1e-24, None, ALU.max)
                    ins.then_inc(dve_["kk"], 1)
                elif kind == "kkn":
                    dve.wait_ge(act_["kk"], n_of("kk", l, 1))
                    tt(unit(1), unit(1), unit(8), ALU.mult).then_inc(dve_["kkn"], 1)
                    pend = PP.rearrange("p (c h) t -> p c h t", h=2)[:, :, 0, C]
                    tt(small[:, 24:28], pend, small[:, 16:24].rearrange("p (c h) -> p c h", h=2)[:, :, 1], ALU.mult)
                elif kind == "prepa":
                    dve.wait_ge(act_["kkn"], n_of("kkn", l, 1))
                    tt(unit(4), unit(4), unit(9), ALU.mult).then_inc(dve_["prepa"], 1)
                elif kind == "prepb":
                    dve.wait_ge(dve_["prepa"], n_of("prepa", l, 1))
                    tt(unit(9), unit(0), unit(1), ALU.mult).then_inc(dve_mid["prepb"], 1)
                    dve.wait_ge(dve_mid["prepb"], n_of("prepb", l, 1))
                    dve.wait_ge(dve_["prepa"], n_of("prepa", l, 1))
                    tt(unit(1), unit(1), unit(7), ALU.mult).then_inc(dve_["prepb"], 1)
                elif kind == "bon":
                    dve.wait_ge(pe_["bon"], n_of("bon", l, 1))
                    ar = unit(8, 2).rearrange("p (n a t) -> p n a t", a=2, t=C)
                    tt(ar[:, :, 1, :], unit(0).rearrange("p (n t) -> p n t", t=C), PP[:, :, 1:C + 1],
                       ALU.mult)
                    tt(ar[:, :, 0, :], unit(4).rearrange("p (n t) -> p n t", t=C), PP[:, :, 0:C], ALU.mult)\
                        .then_inc(dve_mid["bon"], 1)
                    dve.wait_ge(dve_mid["bon"], n_of("bon", l, 1))
                    dve.wait_ge(mixed, l * A_SLABS + A_SLABS)
                    for b in range(2):
                        cols = slice(b * 512, (b + 1) * 512)
                        ins = tt(unit(0)[:, cols], bank[6 + b][:, :], unit(2)[:, cols], ALU.mult)
                    ins.then_inc(dve_["bon"], 1)
                elif kind == "mat":
                    what, b0 = s[2], 3 + 2 * (ORD[s] % 2)
                    dve.wait_ge(pe_["mat"], n_of("mat", l, ORD[s] + 1))
                    if what == "abt":
                        for b in range(2):
                            ins = tt(M1[:, j, 2 * b:2 * b + 2, :],
                                     bank[b0 + b][:, 0:2 * P].rearrange("p (i n) -> p i n", i=2),
                                     rep(mask("level1"), 2), ALU.mult)
                        own.mark(ins)
                        dve.wait_ge(dve_["mat"], n_of("mat", l, ORD[s]))
                        own.mark(tt(Y[:, j], ABT[:, j, :, 0:C], rep(mask("levelT"), 4), ALU.mult))
                        own.wait(own.n - 1)
                        tt(X[:, j], rep(cst("ident"), 4), M1[:, j], ALU.subtract)
                        own.wait()
                        tt(Y[:, j], rep(cst("ident"), 4), Y[:, j], ALU.subtract).then_inc(dve_["mat"], 1)
                    else:
                        a, _ = CB["maskS"]
                        both = cb[:, a:a + 2 * P]
                        for b in range(2):
                            ins = tt((ABT if what == "ab" else KBT)[:, j, 2 * b:2 * b + 2, :],
                                     bank[b0 + b][:, :].rearrange("p (i n) -> p i n", i=2), rep(both, 2), ALU.mult)
                        ins.then_inc(dve_["mat"], 1)
                elif kind == "m1":
                    dve.wait_ge(pe_["m1"], n_of("m1", l, ORD[s] + 1))
                    tt(M1[:, j], bank[4 + 2 * j][:, :].rearrange("p (i n) -> p i n", i=4), rep(mask(f"level{s[2]}"), 4),
                       ALU.mult).then_inc(dve_["m1"], 1)
                elif kind == "dxy":
                    if s in X_STEP:
                        dve.wait_ge(x_mm, l * X_STEPS + X_STEP[s] + 1)
                        tt(X[:, j], X[:, j], bank[4 + 2 * j][:, :].rearrange("p (i n) -> p i n", i=4),
                           ALU.subtract).then_inc(x_done, 1)
                    dve.wait_ge(pe_["dxy"], n_of("dxy", l, ORD[s] + 1))
                    tt(Y[:, j], Y[:, j], bank[5 + 2 * j][:, :].rearrange("p (i n) -> p i n", i=4),
                       ALU.subtract).then_inc(dve_["dxy"], 1)
                elif kind in ("rhs0", "rhs1"):
                    dve.wait_ge(pe_[kind], n_of(kind, l, c + 1))
                    src = bank[3 + j][:, 0:P].rearrange("p (h n) -> p h n", h=2) if kind == "rhs0" \
                        else banks(4 + 2 * j)[:, :, 0:HD]
                    dve.tensor_copy(RHS[:, j, :].rearrange("p (h n) -> p h n", h=2), src).then_inc(dve_[kind], 1)
                elif kind == "s1":
                    dve.wait_ge(pe_["s1"], n_of("s1", l, c + 1))
                    for hp in range(2):
                        rows, cols = slice(hp * HD, (hp + 1) * HD), slice(hp * HD, (hp + 1) * HD)
                        ins = dve.tensor_scalar(s0[rows, c, :], bank[3 if j else 7][rows, cols], small[rows, 24 + c:25 + c], None,
                                                ALU.mult)
                    ins.then_inc(dve_["s1"], 1)
                elif kind == "gn1":
                    dve.wait_ge(pe_["gn1"], n_of("gn1", l, 1))
                    for b in range(2):
                        cols = slice(b * 512, (b + 1) * 512)
                        ins = stt(unit(4)[:, cols], bank[5 + b][:, :], -1.0 / HD, unit(4)[:, cols], ALU.mult, ALU.add)
                    ins.then_inc(dve_["gn1"], 1)
                elif kind == "gn2":
                    dve.wait_ge(act_["gn2"], n_of("gn2", l, 1))
                    tt(unit(4), unit(4), unit(6), ALU.mult).then_inc(dve_["gn2"], 1)
                elif kind == "gn3":
                    dve.wait_ge(act_["gn3"], n_of("gn3", l, 1))
                    own.mark(tt(unit(4), unit(4), unit(0), ALU.add))
                    own.wait()
                    tt(unit(4), unit(4), unit(3), ALU.mult).then_inc(dve_["gn3"], 1)
                elif kind == "gn4":
                    dve.wait_ge(act_["gn4"], n_of("gn4", l, 1))
                    tt(ol[:, 0:BT, :], OT, oh[:, 0:BT, :].bitcast(F32), ALU.subtract).then_inc(dve_["gn4"], 1)
                elif kind == "bz":
                    z = bank[3 + j][:, 0:T + P]
                    diag = SP[:, j, :].rearrange("p (k n) -> p k n", n=P)[:, 0:3:2, :]
                    dve.wait_ge(act_["bz"], n_of("bz", l, c + 1))
                    own.mark(stt(SP[:, j, :], z, 0.0, W1[:, j, :], ALU.max, ALU.add))
                    own.wait()
                    tt(diag, diag, rep(mask("maskS"), 2), ALU.mult).then_inc(dve_["bz"], 1)
                elif kind == "btri":
                    diag = AB[:, j, :].rearrange("p (k n) -> p k n", n=P)[:, 0:3:2, :]
                    dve.wait_ge(act_["btri"], n_of("btri", l, c + 1))
                    stt(diag, diag, 3e38, rep(mask("maskS"), 2), ALU.min, ALU.mult).then_inc(dve_["btri"], 1)
                elif kind == "bav":
                    if c % 2:
                        dve.wait_ge(act_["bav"], l * BT + c // 2 + 1)
                        tt(ol[:, BT + c // 2, :], bank[5 + (c // 2) % 2][:, 0:T], oh[:, BT + c // 2, :].bitcast(F32),
                           ALU.subtract).then_inc(dve_["bav"], 1)
                elif kind == "cs":
                    n, keys = ORD[s], P * (s[2] + 1)
                    f = 28 + 12 * (n % 2)
                    dve.wait_ge(pe_["cs"], n_of("cs", l, n + 1))
                    own.mark(dve.tensor_reduce(small[:, f:f + 2],
                                               banks(3 + 2 * (n % 2))[:, :, 0:keys],
                                               AX.X, ALU.max))
                    own.wait()
                    dve.tensor_scalar(small[:, f + 2:f + 4], small[:, f:f + 2], -HD ** -0.5, None, ALU.mult)\
                        .then_inc(dve_mid["cs"], 1)
                    dve.wait_ge(act_["cs"], n_of("cs", l, n + 1))
                    own.mark(dve.reciprocal(small[:, f + 6:f + 8], small[:, f + 4:f + 6]))
                    own.wait()
                    dve.wait_ge(dve_["lam"], n_of("lam", l, 1))
                    own.mark(tt(small[:, f + 8:f + 9], small[:, f + 7:f + 8], small[:, 4:5], ALU.mult))
                    a, b = PC[:, n % 2, 0, 0:keys], PC[:, n % 2, 1, 0:keys]
                    own.mark(dve.tensor_scalar(a, a, small[:, f + 6:f + 7], None, ALU.mult))
                    own.wait()
                    stt(a, b, small[:, f + 8:f + 9], a, ALU.mult, ALU.add).then_inc(dve_["cs"], 1)
                elif kind == "crms":
                    dve.wait_ge(act_mid["crms"], n_of("crms", l, 1))
                    dve.wait_ge(dve_mid["lam"], n_of("lam", l, 1))
                    stt(OC[:, :, :], OC[:, :, :], omu[:, 18:19], OSQ[:, :, :], ALU.mult, ALU.mult)\
                        .then_inc(dve_mid["crms"], 1)
                    dve.wait_ge(act_["crms"], n_of("crms", l, 1))
                    tt(ol[:, 2 * BT:3 * BT, :], OC[:, :, :], oh[:, 2 * BT:3 * BT, :].bitcast(F32), ALU.subtract)\
                        .then_inc(dve_["crms"], 1)

            def scale_up(l, t, u, which, slab):
                k = 2 * (u % 2) + which
                dve.wait_ge(slab_done, slab + 1)
                tt(UM[:, k, :], bank[k][:, 0:T], rs[:, 0:T], ALU.mult).then_inc(up_scaled, 1)

            def conv(l, t, u, which, col):
                k = 2 * (u % 2) + which
                dve.wait_ge(tap2, l * 2 * FT + 2 * t + (which + 1))
                own.mark(stt(CV[:, k, 1:T], UM[:, k, 0:T - 1], tap(col, 1), CV[:, k, 1:T], ALU.mult, ALU.add))
                own.wait()
                stt(CV[:, k, 2:T], UM[:, k, 0:T - 2], tap(col, 0), CV[:, k, 2:T], ALU.mult, ALU.add)\
                    .then_inc(conv_done, 1)

            def product(l, t, u):
                g, v = CV[:, 2 * (u % 2), :], CV[:, 2 * (u % 2) + 1, :]
                dve.wait_ge(silu_done, l * FT + t + 1)
                dve.wait_ge(conv_done, l * 2 * FT + 2 * t + 2)
                tt(g, g, v, ALU.mult).then_inc(prod_done, 1)

            def product_lo(l, t, u):
                dve.wait_ge(prod_h, l * FT + t + 1)
                tt(ol[:, u % 2, :], CV[:, 2 * (u % 2), :], oh[:, u % 2, :].bitcast(F32), ALU.subtract)\
                    .then_inc(prod_l, 1)

            dve.wait_ge(x_loaded, 64)
            dve.memset(small[:, 63:64], 0.0).then_inc(x_ready, 4)
            for m in range(AHEAD):
                split(m, m, None, None)
            with dve.Fori(0, DEPTH) as l:
                own.base, own.n = l * DVE_OWN["layer"], 0
                dve.wait_ge(mix_in_s, 16 * l + 16)
                for s in DVE_STEPS:
                    step(l, s)
                for t in range(2):
                    for which in range(2):
                        n = FFN0 + 2 * t + which
                        ahead(l, n)
                        if n == FFN0:
                            dve.wait_ge(rms_inv, 2 * l + 2)
                        scale_up(l, t, t, which, l * SLABS + n)
                    for which in range(2):
                        conv(l, t, t, which, 8 + 4 * (2 * t + which))
                    product(l, t, t)
                    if t:
                        ahead(l, FFN0 + 4)
                    product_lo(l, t, t)
                before = own.n
                with dve.Fori(0, FTURNS) as i:
                    own.base = l * DVE_OWN["layer"] + i * DVE_OWN["turn"]
                    for u in range(FU):
                        t = FU * i + (u + 2)
                        o = FFN0 + 5 + 3 * u
                        for which in range(2):
                            ahead_in(lambda m, s, used, landed: split(used + AHEAD, s, used, None), l, i, o + which)
                            scale_up(l, t, u, which, l * SLABS + 3 * FU * i + (o + which))
                        for which in range(2):
                            conv(l, t, u, which, 8 * FU * i + (8 + 8 * (u + 2) + 4 * which))
                        product(l, t, u)
                        ahead_in(lambda m, s, used, landed: split(used + AHEAD, s, used, None), l, i, o + 2)
                        product_lo(l, t, u)
                assert own.n - before == DVE_OWN["turn"], ("dve turn", own.n - before)
                own.base, own.n = l * DVE_OWN["layer"], before + FTURNS * DVE_OWN["turn"]
                ahead(l, SLABS - 1)
                dve.wait_ge(slab_done, l * SLABS + SLABS)
                for b in range(4):
                    pair = x[:, 2 * b:2 * b + 2, :].rearrange("p c t -> p (c t)")
                    tt(pair, pair, bank[4 + b][:, :], ALU.add).then_inc(x_ready, 1)
                assert own.n == DVE_OWN["layer"], ("dve", own.n)
            own.base, own.n = DEPTH * DVE_OWN["layer"], 0
            add_squares(2 * DEPTH)
            dve.wait_ge(fin_loaded, 16)
            dve.wait_ge(rms_inv, 2 * DEPTH + 1)
            for c in range(KT):
                stt(HF[:, c, :], x[:, c, :], fin[:, c:c + 1], rs[:, 0:T], ALU.mult, ALU.mult).then_inc(y_ready, 1)
        return nc


def constants():
    import numpy as np

    cf, cb = np.zeros((P, NCF), np.float32), np.zeros((P, NCB), np.float32)

    def put(dst, where, name, a):
        dst[:a.shape[0], where[name][0]:where[name][0] + where[name][1]] = a
    i = np.arange(P)
    row, col = i[:, None], i[None, :]
    put(cf, CF, "ident", np.eye(P))
    put(cf, CF, "ones", np.ones((P, P)))
    put(cf, CF, "bones", row // HD == col // HD)
    rope = np.zeros((P, P))
    half = HD // 8
    for m in range(2):
        for d in range(half):
            rope[m * HD + d + half, m * HD + d] = -1.0
            rope[m * HD + d, m * HD + d + half] = 1.0
    put(cf, CF, "rope", rope)
    put(cf, CF, "triN", -(row >= col).astype(np.float32))
    put(cf, CF, "onesN", -np.ones((P, P)))
    inv_freq = np.float32(500000.0) ** (-np.arange(0, 2 * half, 2, dtype=np.float32) / np.float32(2 * half))
    ang = inv_freq[:, None].astype(np.float32) * np.arange(T, dtype=np.float32)[None, :]
    cos, sin = np.ones((P, T)), np.zeros((P, T))
    for m in range(2):
        for o in (0, half):
            cos[m * HD + o:m * HD + o + half] = np.cos(ang)
            sin[m * HD + o:m * HD + o + half] = np.sin(ang)
    put(cf, CF, "cos", cos)
    put(cf, CF, "sin", sin)
    put(cf, CF, "rowL", np.broadcast_to((i < 64).astype(np.float32)[None, :], (P, P)))
    put(cf, CF, "rowR", np.full((P, 64), -1e30))
    for name, v in (("eps", 1e-6), ("gneps", 64e-5), ("kkb", 10 * np.log(2.0)), ("one", 1.0)):
        put(cf, CF, name, np.full((P, 1), v))
    put(cb, CB, "maskS", row < col)
    put(cb, CB, "maskI", row <= col)

    def level(t, s, z):
        return (t // (2 * z) == s // (2 * z)) & (t // z % 2 == 1) & (s // z % 2 == 0)
    put(cb, CB, "levelT", level(col, row, 1))
    for z in LEVELS:
        put(cb, CB, f"level{z}", level(row, col, z))
    return cf, cb.astype(np.float16)


def lay_out(a):
    import numpy as np

    L = a["w_in"].shape[0]
    f = {k: np.asarray(v) for k, v in a.items()}

    def cols_major(w, cols):
        n, k, m = w.shape
        return w.reshape(n, k // P, P, m // cols, cols).transpose(0, 3, 2, 1, 4)

    w = f["w_in"]
    b0, c0, g0 = 1792, 1792 + 1536, 1792 + 3072
    lora = w[:, :, 1536:1792]

    def square(x):
        return cols_major(x, P).reshape(L, -1, P, SLAB)

    def values(x):
        return x.reshape(L, 4, 2, P, BW).transpose(0, 1, 3, 2, 4).reshape(L, 4, P, SLAB)
    parts = [square(lora), square(w[:, :, 512:1024]), square(w[:, :, 0:512]), square(w[:, :, 1024:1536]),
             square(w[:, :, b0:b0 + 1024]), values(w[:, :, b0 + 1024:b0 + 1536]),
             square(w[:, :, c0:c0 + 1024]), values(w[:, :, c0 + 1024:c0 + 1536]), None]
    gates = square(w[:, :, g0:])
    br = [cols_major(f[n], 2 * P).reshape(L, KT // 2, P, SLAB) for n in ("w_branch_a", "w_branch_b", "w_branch_c")]
    parts[-1] = np.stack([gates[:, k[1]] if k[0] == "G" else br[k[1]][:, k[2]] for k in DENSE if k[0] in ("G", "BR")],
                         axis=1)
    parts += [square(f["w_out"])]
    up = square(f["ffn_w_up"]).reshape(L, 2, FT, P, SLAB)
    down = f["ffn_w_down"].reshape(L, FT, P, SLAB)
    ffn = [up[:, 0, 0], up[:, 1, 0]]
    for t in range(1, FT):
        ffn += [up[:, 0, t], up[:, 1, t], down[:, t - 1]]
    ffn.append(down[:, FT - 1])
    parts.append(np.stack(ffn, axis=1))
    stream = np.concatenate(parts, axis=1).reshape(L * SLABS, P, SLAB)
    stream = np.concatenate([stream, np.zeros((RING, P, SLAB), np.float32)])

    def vec(x):
        return x.reshape(L, -1, P).transpose(0, 2, 1)
    mu = f["rwkv_mu"]
    mu = np.concatenate([mu[:, 1536:1792], mu[:, 512:1024], mu[:, 0:512], mu[:, 1024:1536]], axis=1)
    lam = np.zeros((L, P, 4), np.float32)
    lam[:, 0:64] = f["diff_lambda"].transpose(0, 2, 1)
    li = np.array([0.8 - 0.6 * float(np.exp(-0.3 * i)) for i in range(L)])
    li2 = np.stack([np.broadcast_to(v[:, None], (L, P)) for v in (li, 1.0 - li)], axis=2).astype(np.float32)
    mix = np.concatenate([vec(f["norm_mix_g"]), vec(mu), vec(f["rwkv_w0"]), vec(f["rwkv_a0"]), vec(f["rwkv_k_k"]),
                          vec(f["rwkv_k_a"]), vec(f["rwkv_r_k"].reshape(L, -1)), vec(f["rwkv_ln_w"]),
                          vec(f["rwkv_ln_b"]), vec(f["diff_subln_g"]), lam, li2,
                          np.concatenate([f["rwkv_w_up"], f["rwkv_a_up"]], axis=1), f["rwkv_g_up"],
                          np.zeros((L, P, NPM - _o), np.float32)], axis=2)
    cw = np.concatenate([f["ffn_conv_w"], f["ffn_conv_b"][:, None]], axis=1)
    cw = cw.reshape(L, 4, 2, FT, P).transpose(0, 4, 3, 2, 1).reshape(L, P, 8 * FT)
    ffn_par = np.concatenate([vec(f["norm_ffn_g"]), cw], axis=2)
    mix, ffn_par = (np.concatenate([v, np.zeros_like(v[:1])]) for v in (mix, ffn_par))
    cf, cb = constants()
    c = np.ascontiguousarray
    return {"x_t": c(f["x"][0].T.reshape(KT, P, T).transpose(1, 0, 2)), "w_stream": c(stream), "mix_par": c(mix),
            "ffn_par": c(ffn_par), "final_g": c(f["norm_final_g"].reshape(KT, P).T), "const_f": c(cf),
            "const_b": c(cb)}


_INS = ["x_t", "w_stream", "mix_par", "ffn_par", "final_g", "const_f", "const_b"]


def kernel(**inputs):
    import numpy as np
    import concourse.bacc as bacc
    from concourse.bass_utils import run_bass_kernel_spmd

    nc = bacc.Bacc("TRN2", target_bir_lowering=False, num_devices=1)
    arrays = lay_out(inputs)
    args = [nc.dram_tensor(n, arrays[n].shape, mybir.dt.from_np(arrays[n].dtype), kind="ExternalInput").ap()
            for n in _INS]
    y = nc.dram_tensor("y_t", (P, KT, T), F32, kind="ExternalOutput").ap()
    hybrid_blocks(nc, *args, y)
    r = run_bass_kernel_spmd(nc, [arrays], core_ids=[0])
    out = r.results[0]["y_t"]
    return np.ascontiguousarray(out.transpose(2, 1, 0).reshape(1, T, D))
```
